# Optimizing a Trainium2 kernel written in Bass

```python
import jax, jax.numpy as jnp
from jax import lax
import numpy as np

D_MODEL = 1024
BATCH = 1
SEQ = 512
DEPTH = 2

WINDOWS = (128, 512, 2048)
DILATIONS = (1, 4, 16)
N_GROUPS = 3
HEADS_PER_GROUP = 8
HEAD_DIM = 128
N_ATTN_HEADS = N_GROUPS * HEADS_PER_GROUP
ATTN_OUT_WIDTH = HEADS_PER_GROUP * HEAD_DIM
QKV_WIDTH = N_GROUPS * 3 * HEADS_PER_GROUP * HEAD_DIM
NUM_BUCKETS = 32
MAX_DISTANCE = 2048
LRU_WIDTH = D_MODEL
LRU_BLOCKS = 4
LRU_BLOCK_WIDTH = LRU_WIDTH // LRU_BLOCKS
LRU_CONV_WIDTH = 4
LRU_C = 8.0
D_FF = 3 * D_MODEL
FFN_CONV_WIDTH = 3

RMS_EPS = 1e-6
NEG_INF = -1e30
N_ATTN_LAYERS = (DEPTH + 1) // 2
N_LRU_LAYERS = DEPTH // 2


def rms_norm(x, g):
    xf = x.astype(jnp.float32)
    y = xf * lax.rsqrt(jnp.mean(xf * xf, axis=-1, keepdims=True) + RMS_EPS)
    return (y * g.astype(jnp.float32)).astype(x.dtype)

def causal_dwconv(x, w, b):
    K = w.shape[0]
    S = x.shape[1]
    xp = jnp.pad(x, ((0, 0), (K - 1, 0), (0, 0)))
    out = b
    for k in range(K):
        out = out + xp[:, k:k + S] * w[k]
    return out

def t5_bucket(dist):
    max_exact = NUM_BUCKETS // 2
    d = np.maximum(dist, 1).astype(np.float64)
    large = max_exact + (np.log(d / max_exact) / np.log(MAX_DISTANCE / max_exact)
                         * (NUM_BUCKETS - max_exact)).astype(np.int32)
    large = np.minimum(large, NUM_BUCKETS - 1)
    return np.where(dist < max_exact, dist, large).astype(np.int32)

def band_geometry(band):
    i = np.arange(band)[:, None]
    k = np.arange(2 * band)[None, :]
    m = i + band - k
    valid = (m >= 0) & (m <= band)
    return m, valid, k

def dilated_group_attention(q, k, v, bias_table, window, dilation):
    B, S, H, Dh = q.shape
    band = window // dilation
    span = dilation * band
    S_pad = -(-S // span) * span
    U = S_pad // dilation
    nb = U // band

    def to_strided(t):
        t = jnp.pad(t, ((0, 0), (0, S_pad - S), (0, 0), (0, 0)))
        t = t.reshape(B, U, dilation, H, Dh).transpose(0, 2, 3, 1, 4)
        return t.reshape(B, dilation, H, nb, band, Dh)

    qs, ks, vs = to_strided(q), to_strided(k), to_strided(v)
    pad_blk = ((0, 0), (0, 0), (0, 0), (1, 0), (0, 0), (0, 0))
    kk = jnp.concatenate([jnp.pad(ks, pad_blk)[:, :, :, :-1], ks], axis=-2)
    vv = jnp.concatenate([jnp.pad(vs, pad_blk)[:, :, :, :-1], vs], axis=-2)

    m, valid, kidx = band_geometry(band)
    bucket = t5_bucket(np.clip(m, 0, band) * dilation)
    bias = jnp.transpose(bias_table.astype(jnp.float32)[bucket], (2, 0, 1))
    blk = np.arange(nb)[:, None, None]
    mask = valid[None] & ((blk > 0) | (kidx[None] >= band))

    scale = HEAD_DIM ** -0.5
    logits = jnp.einsum('bxhnqd,bxhnkd->bxhnqk', qs, kk,
                        preferred_element_type=jnp.float32) * scale
    logits = logits + bias[None, None, :, None]
    logits = jnp.where(mask[None, None, None], logits, NEG_INF)
    mx = jnp.max(logits, axis=-1, keepdims=True)
    p = jnp.exp(logits - mx)
    s = jnp.sum(p, axis=-1, keepdims=True)
    o = jnp.einsum('bxhnqk,bxhnkd->bxhnqd', p, vv.astype(jnp.float32)) / s
    lse = (mx + jnp.log(s))[..., 0]

    o = o.reshape(B, dilation, H, U, Dh).transpose(0, 3, 1, 2, 4).reshape(B, S_pad, H, Dh)[:, :S]
    lse = lse.reshape(B, dilation, H, U).transpose(0, 3, 1, 2).reshape(B, S_pad, H)[:, :S]
    return o, lse

def dilated_attention_mixer(x, w_qkv, w_o, rel_bias):
    B, S, _ = x.shape
    qkv = (x @ w_qkv).reshape(B, S, N_GROUPS, 3, HEADS_PER_GROUP, HEAD_DIM)
    outs, lses = [], []
    for g in range(N_GROUPS):
        tbl = rel_bias[:, g * HEADS_PER_GROUP:(g + 1) * HEADS_PER_GROUP]
        o, lse = dilated_group_attention(qkv[:, :, g, 0], qkv[:, :, g, 1], qkv[:, :, g, 2],
                                         tbl, WINDOWS[g], DILATIONS[g])
        outs.append(o)
        lses.append(lse)
    alpha = jax.nn.softmax(jnp.stack(lses), axis=0)
    o = jnp.sum(alpha[..., None] * jnp.stack(outs), axis=0)
    return o.reshape(B, S, ATTN_OUT_WIDTH).astype(x.dtype) @ w_o

def _lru_combine(c1, c2):
    a1, b1 = c1
    a2, b2 = c2
    return a1 * a2, a2 * b1 + b2

def rglru_mixer(x, w_in, conv_w, conv_b, ga_w, ga_b, gx_w, gx_b, lam, w_out):
    B, S, _ = x.shape
    h = x @ w_in
    xb, gb = h[..., :LRU_WIDTH], h[..., LRU_WIDTH:]
    gate = jax.nn.gelu(gb, approximate=True)
    xb = causal_dwconv(xb, conv_w, conv_b)
    xr = xb.reshape(B, S, LRU_BLOCKS, LRU_BLOCK_WIDTH)
    r = jax.nn.sigmoid(jnp.einsum('bsnc,ncd->bsnd', xr, ga_w) + ga_b).reshape(B, S, LRU_WIDTH)
    i = jax.nn.sigmoid(jnp.einsum('bsnc,ncd->bsnd', xr, gx_w) + gx_b).reshape(B, S, LRU_WIDTH)
    log_a = LRU_C * r.astype(jnp.float32) * jax.nn.log_sigmoid(lam.astype(jnp.float32))
    a = jnp.exp(log_a)
    mult = jnp.sqrt(jnp.maximum(-jnp.expm1(2.0 * log_a), 0.0))
    b = mult * i.astype(jnp.float32) * xb.astype(jnp.float32)
    _, hs = lax.associative_scan(_lru_combine, (a, b), axis=1)
    return (hs.astype(x.dtype) * gate) @ w_out

def conv_ffn(x, w_up, conv_w, conv_b, w_down):
    u = causal_dwconv(x @ w_up, conv_w, conv_b)
    g, v = u[..., :D_FF], u[..., D_FF:]
    return (jax.nn.gelu(g, approximate=True) * v) @ w_down

def first_inputs(seed: int = 0) -> dict:
    key = jax.random.key(seed)
    ks = jax.random.split(key, 32)
    f32 = jnp.float32
    nrm = lambda k, shape, s: jax.random.normal(k, shape, f32) * s
    gain = lambda k: 1.0 + 0.05 * jax.random.normal(k, (DEPTH, D_MODEL), f32)
    a_target = jax.random.uniform(ks[20], (N_LRU_LAYERS, LRU_WIDTH), f32, 0.9, 0.999)
    p = a_target ** (1.0 / LRU_C)
    lam = jnp.log(p) - jnp.log1p(-p)
    return {
        "x": nrm(ks[0], (BATCH, SEQ, D_MODEL), 1.0),
        "norm_mix_pre": gain(ks[1]),
        "norm_mix_post": gain(ks[2]),
        "norm_ffn_pre": gain(ks[3]),
        "norm_ffn_post": gain(ks[4]),
        "rel_bias": nrm(ks[5], (NUM_BUCKETS, N_ATTN_HEADS), 0.5),
        "attn_w_qkv": nrm(ks[6], (N_ATTN_LAYERS, D_MODEL, QKV_WIDTH), D_MODEL ** -0.5),
        "attn_w_o": nrm(ks[7], (N_ATTN_LAYERS, ATTN_OUT_WIDTH, D_MODEL), ATTN_OUT_WIDTH ** -0.5),
        "lru_w_in": nrm(ks[8], (N_LRU_LAYERS, D_MODEL, 2 * LRU_WIDTH), D_MODEL ** -0.5),
        "lru_conv_w": nrm(ks[9], (N_LRU_LAYERS, LRU_CONV_WIDTH, LRU_WIDTH), LRU_CONV_WIDTH ** -0.5),
        "lru_conv_b": nrm(ks[10], (N_LRU_LAYERS, LRU_WIDTH), 0.02),
        "lru_ga_w": nrm(ks[11], (N_LRU_LAYERS, LRU_BLOCKS, LRU_BLOCK_WIDTH, LRU_BLOCK_WIDTH), LRU_BLOCK_WIDTH ** -0.5),
        "lru_ga_b": nrm(ks[12], (N_LRU_LAYERS, LRU_BLOCKS, LRU_BLOCK_WIDTH), 0.02),
        "lru_gx_w": nrm(ks[13], (N_LRU_LAYERS, LRU_BLOCKS, LRU_BLOCK_WIDTH, LRU_BLOCK_WIDTH), LRU_BLOCK_WIDTH ** -0.5),
        "lru_gx_b": nrm(ks[14], (N_LRU_LAYERS, LRU_BLOCKS, LRU_BLOCK_WIDTH), 0.02),
        "lru_lambda": lam,
        "lru_w_out": nrm(ks[15], (N_LRU_LAYERS, LRU_WIDTH, D_MODEL), LRU_WIDTH ** -0.5),
        "ffn_w_up": nrm(ks[16], (DEPTH, D_MODEL, 2 * D_FF), D_MODEL ** -0.5),
        "ffn_conv_w": nrm(ks[17], (DEPTH, FFN_CONV_WIDTH, 2 * D_FF), FFN_CONV_WIDTH ** -0.5),
        "ffn_conv_b": nrm(ks[18], (DEPTH, 2 * D_FF), 0.02),
        "ffn_w_down": nrm(ks[19], (DEPTH, D_FF, D_MODEL), D_FF ** -0.5),
    }

def first_block(x, norm_mix_pre, norm_mix_post, norm_ffn_pre, norm_ffn_post, rel_bias,
              attn_w_qkv, attn_w_o, lru_w_in, lru_conv_w, lru_conv_b, lru_ga_w, lru_ga_b,
              lru_gx_w, lru_gx_b, lru_lambda, lru_w_out, ffn_w_up, ffn_conv_w, ffn_conv_b,
              ffn_w_down):
    for layer in range(DEPTH):
        j = layer // 2
        h = rms_norm(x, norm_mix_pre[layer])
        if layer % 2 == 0:
            h = dilated_attention_mixer(h, attn_w_qkv[j], attn_w_o[j], rel_bias)
        else:
            h = rglru_mixer(h, lru_w_in[j], lru_conv_w[j], lru_conv_b[j], lru_ga_w[j], lru_ga_b[j],
                            lru_gx_w[j], lru_gx_b[j], lru_lambda[j], lru_w_out[j])
        x = x + rms_norm(h, norm_mix_post[layer])
        h = rms_norm(x, norm_ffn_pre[layer])
        h = conv_ffn(h, ffn_w_up[layer], ffn_conv_w[layer], ffn_conv_b[layer], ffn_w_down[layer])
        x = x + rms_norm(h, norm_ffn_post[layer])
    return x


HEAD_DIM_2 = 64
Q_BLOCK = 128
ROPE_THETA = 10000.0
EPS = 1e-6
NSA_HEADS = 8
NSA_KV_GROUPS = 2
NSA_CMP_LEN = 32
NSA_CMP_STRIDE = 16
NSA_CMP_HIDDEN = 128
NSA_SEL_LEN = 64
NSA_SEL_TOPK = 16
NSA_WINDOW = 512
FORCE_SCORE = 1e9
NSA_WIDTH = NSA_HEADS * HEAD_DIM_2
NSA_KV_WIDTH = NSA_KV_GROUPS * HEAD_DIM_2
FOX_HEADS = 8
FOX_WIDTH = FOX_HEADS * HEAD_DIM_2
MEM_LEN = 256
MEM_HEADS = 4
MEM_HEAD_DIM = 128
MEM_WIDTH = MEM_HEADS * MEM_HEAD_DIM
N_BRANCH = 3
IN_SPLITS = (NSA_WIDTH, 6 * NSA_KV_WIDTH, 3 * NSA_HEADS, NSA_WIDTH,
             3 * FOX_WIDTH, FOX_HEADS, FOX_WIDTH,
             MEM_WIDTH, MEM_WIDTH,
             N_BRANCH * D_MODEL)
IN_WIDTH = sum(IN_SPLITS)


def _rmsnorm(x, g):
    xf = x.astype(jnp.float32)
    y = xf * lax.rsqrt(jnp.mean(xf * xf, axis=-1, keepdims=True) + EPS)
    return (y * g.astype(jnp.float32)).astype(x.dtype)

def _rope(x, pos):
    half = x.shape[-1] // 2
    inv_freq = ROPE_THETA ** (-jnp.arange(half, dtype=jnp.float32) / half)
    ang = pos.astype(jnp.float32)[:, None] * inv_freq[None, :]
    cos = jnp.cos(ang)[None, :, None, :]
    sin = jnp.sin(ang)[None, :, None, :]
    xf = x.astype(jnp.float32)
    x1, x2 = xf[..., :half], xf[..., half:]
    return jnp.concatenate([x1 * cos - x2 * sin, x2 * cos + x1 * sin], axis=-1).astype(x.dtype)

def _masked_softmax(s, mask):
    s = jnp.where(mask, s.astype(jnp.float32), -jnp.inf)
    m = jnp.max(s, axis=-1, keepdims=True)
    m = jnp.where(jnp.isfinite(m), m, 0.0)
    e = jnp.exp(s - m)
    d = jnp.sum(e, axis=-1, keepdims=True)
    return e / jnp.where(d > 0.0, d, 1.0)

def _split(z, sizes):
    return jnp.split(z, np.cumsum(sizes)[:-1].tolist(), axis=-1)

def _compress(x, pe, w1, w2):
    B, T, G, dk = x.shape
    r = NSA_CMP_LEN // NSA_CMP_STRIDE
    n_chunk = T // NSA_CMP_STRIDE
    n_cmp = n_chunk - r + 1
    ch = x.reshape(B, n_chunk, NSA_CMP_STRIDE, G, dk)
    blk = jnp.concatenate([ch[:, i:i + n_cmp] for i in range(r)], axis=2)
    blk = blk + pe[None, None, :, None, :].astype(x.dtype)
    flat = blk.transpose(0, 1, 3, 2, 4).reshape(B, n_cmp, G, NSA_CMP_LEN * dk)
    return jax.nn.silu(flat @ w1) @ w2

def _overlap(n_cmp, n_slc):
    cs = np.arange(n_cmp)[:, None] * NSA_CMP_STRIDE
    ss = np.arange(n_slc)[None, :] * NSA_SEL_LEN
    ov = np.clip(np.minimum(cs + NSA_CMP_LEN, ss + NSA_SEL_LEN) - np.maximum(cs, ss), 0, None)
    return jnp.asarray(ov / NSA_CMP_LEN, dtype=jnp.float32)

def _nsa(q, kv, gate, pe_k, w1_k, w2_k, pe_v, w1_v, w2_v, q_g, k_g):
    B, T, _ = q.shape
    G, R, dk = NSA_KV_GROUPS, NSA_HEADS // NSA_KV_GROUPS, HEAD_DIM_2
    pos = jnp.arange(T)
    nqb = T // Q_BLOCK
    n_slc = T // NSA_SEL_LEN
    n_top = min(NSA_SEL_TOPK, n_slc)
    scale = dk ** -0.5
    qh = _rope(_rmsnorm(q.reshape(B, T, NSA_HEADS, dk), q_g), pos)
    k_c, v_c, k_s, v_s, k_w, v_w = [a.reshape(B, T, G, dk) for a in jnp.split(kv, 6, axis=-1)]
    k_c = _rmsnorm(_compress(_rope(k_c, pos), pe_k, w1_k, w2_k), k_g[0])
    v_c = _compress(v_c, pe_v, w1_v, w2_v)
    n_cmp = k_c.shape[1]
    k_s = _rope(_rmsnorm(k_s, k_g[1]), pos)
    k_w = _rope(_rmsnorm(k_w, k_g[2]), pos)
    ov = _overlap(n_cmp, n_slc)
    ks_blk = k_s.reshape(B, n_slc, NSA_SEL_LEN, G, dk).transpose(0, 3, 1, 2, 4)
    vs_blk = v_s.reshape(B, n_slc, NSA_SEL_LEN, G, dk).transpose(0, 3, 1, 2, 4)
    kw_pad = jnp.pad(k_w, ((0, 0), (NSA_WINDOW, 0), (0, 0), (0, 0)))
    vw_pad = jnp.pad(v_w, ((0, 0), (NSA_WINDOW, 0), (0, 0), (0, 0)))
    gather = jax.vmap(jax.vmap(lambda blocks, ix: blocks[ix]))
    cmp_end = jnp.arange(n_cmp) * NSA_CMP_STRIDE + NSA_CMP_LEN - 1
    jblk = jnp.arange(n_slc)
    qblocks = qh.reshape(B, nqb, Q_BLOCK, G, R, dk).transpose(1, 0, 2, 3, 4, 5)

    def block(args):
        qb, i = args
        t = i * Q_BLOCK + jnp.arange(Q_BLOCK)
        s = jnp.einsum('bqgrd,bngd->bgrqn', qb, k_c) * scale
        p_c = _masked_softmax(s, cmp_end[None, :] <= t[:, None])
        o_c = jnp.einsum('bgrqn,bngd->bqgrd', p_c.astype(v_c.dtype), v_c)
        imp = jnp.einsum('bgrqn,nj->bgqj', p_c, ov)
        cur = t // NSA_SEL_LEN
        forced = (jblk[None] == 0) | (jblk[None] == cur[:, None]) | (jblk[None] == cur[:, None] - 1)
        score = jnp.where(forced, FORCE_SCORE, imp)
        score = jnp.where(jblk[None] <= cur[:, None], score, -jnp.inf)
        _, idx = lax.top_k(score, n_top)
        sel_ok = idx <= cur[None, None, :, None]
        kg = gather(ks_blk, idx)
        vg = gather(vs_blk, idx)
        s = jnp.einsum('bqgrd,bgqnkd->bgrqnk', qb, kg) * scale
        kpos = idx[..., None] * NSA_SEL_LEN + jnp.arange(NSA_SEL_LEN)
        smask = sel_ok[..., None] & (kpos <= t[None, None, :, None, None])
        m_sel = n_top * NSA_SEL_LEN
        p_s = _masked_softmax(s.reshape(B, G, R, Q_BLOCK, m_sel),
                              smask[:, :, None].reshape(B, G, 1, Q_BLOCK, m_sel))
        o_s = jnp.einsum('bgrqm,bgqmd->bqgrd', p_s.astype(vg.dtype), vg.reshape(B, G, Q_BLOCK, m_sel, dk))
        kw = lax.dynamic_slice_in_dim(kw_pad, i * Q_BLOCK, Q_BLOCK + NSA_WINDOW, axis=1)
        vw = lax.dynamic_slice_in_dim(vw_pad, i * Q_BLOCK, Q_BLOCK + NSA_WINDOW, axis=1)
        spos = i * Q_BLOCK - NSA_WINDOW + jnp.arange(Q_BLOCK + NSA_WINDOW)
        diff = t[:, None] - spos[None, :]
        wmask = (diff >= 0) & (diff < NSA_WINDOW) & (spos[None, :] >= 0)
        s = jnp.einsum('bqgrd,bkgd->bgrqk', qb, kw) * scale
        p_w = _masked_softmax(s, wmask)
        o_w = jnp.einsum('bgrqk,bkgd->bqgrd', p_w.astype(vw.dtype), vw)
        return o_c, o_s, o_w

    o_c, o_s, o_w = lax.map(block, (qblocks, jnp.arange(nqb)))
    to_bthd = lambda o: o.transpose(1, 0, 2, 3, 4, 5).reshape(B, T, NSA_HEADS, dk)
    g = jax.nn.sigmoid(gate.astype(jnp.float32)).reshape(B, T, NSA_HEADS, 3, 1).astype(q.dtype)
    o = g[..., 0, :] * to_bthd(o_c) + g[..., 1, :] * to_bthd(o_s) + g[..., 2, :] * to_bthd(o_w)
    return o.reshape(B, T, NSA_WIDTH)

def _fox(qkv, f_logit, q_g, k_g, f_bias):
    B, T, _ = qkv.shape
    H, dk = FOX_HEADS, HEAD_DIM_2
    nqb = T // Q_BLOCK
    scale = dk ** -0.5
    q, k, v = [a.reshape(B, T, H, dk) for a in jnp.split(qkv, 3, axis=-1)]
    q = _rmsnorm(q, q_g)
    k = _rmsnorm(k, k_g)
    log_f = jax.nn.log_sigmoid(f_logit.astype(jnp.float32) + f_bias.astype(jnp.float32))
    c = jnp.cumsum(log_f, axis=1).transpose(0, 2, 1)
    qblocks = q.reshape(B, nqb, Q_BLOCK, H, dk).transpose(1, 0, 2, 3, 4)
    cblocks = c.reshape(B, H, nqb, Q_BLOCK).transpose(2, 0, 1, 3)
    kpos = jnp.arange(T)

    def block(args):
        qb, cq, i = args
        t = i * Q_BLOCK + jnp.arange(Q_BLOCK)
        s = jnp.einsum('bqhd,bkhd->bhqk', qb, k).astype(jnp.float32) * scale
        s = s + cq[..., None] - c[:, :, None, :]
        p = _masked_softmax(s, kpos[None, :] <= t[:, None])
        return jnp.einsum('bhqk,bkhd->bqhd', p.astype(v.dtype), v)

    o = lax.map(block, (qblocks, cblocks, jnp.arange(nqb)))
    return o.transpose(1, 0, 2, 3, 4).reshape(B, T, FOX_WIDTH)

def _memory_xattn(q, mem_kv, q_g, k_g):
    B, T, _ = q.shape
    M = mem_kv.shape[1]
    q = _rmsnorm(q.reshape(B, T, MEM_HEADS, MEM_HEAD_DIM), q_g)
    k, v = [a.reshape(B, M, MEM_HEADS, MEM_HEAD_DIM) for a in jnp.split(mem_kv, 2, axis=-1)]
    k = _rmsnorm(k, k_g)
    s = jnp.einsum('bthd,bmhd->bhtm', q, k).astype(jnp.float32) * (MEM_HEAD_DIM ** -0.5)
    p = jax.nn.softmax(s, axis=-1)
    return jnp.einsum('bhtm,bmhd->bthd', p.astype(v.dtype), v).reshape(B, T, MEM_WIDTH)

def second_inputs(seed: int = 0) -> dict:
    key = jax.random.key(seed)
    ks = jax.random.split(key, 24)
    f32 = jnp.float32
    L = DEPTH

    def nrm(k, shape, scale):
        return jax.random.normal(k, shape, f32) * scale

    def gain(k, shape):
        return 1.0 + 0.05 * jax.random.normal(k, shape, f32)

    cmp_in = NSA_CMP_LEN * HEAD_DIM_2
    return {
        'x': nrm(ks[0], (BATCH, SEQ, D_MODEL), 1.0),
        'mem': nrm(ks[1], (BATCH, MEM_LEN, D_MODEL), 1.0),
        'norm_g': gain(ks[2], (L, D_MODEL)),
        'mem_norm_g': gain(ks[3], (L, D_MODEL)),
        'w_in': nrm(ks[4], (L, D_MODEL, IN_WIDTH), D_MODEL ** -0.5),
        'nsa_q_norm': gain(ks[5], (L, HEAD_DIM_2)),
        'nsa_k_norm': gain(ks[6], (L, 3, HEAD_DIM_2)),
        'cmp_pe_k': nrm(ks[7], (L, NSA_CMP_LEN, HEAD_DIM_2), 0.1),
        'cmp_w1_k': nrm(ks[8], (L, cmp_in, NSA_CMP_HIDDEN), cmp_in ** -0.5),
        'cmp_w2_k': nrm(ks[9], (L, NSA_CMP_HIDDEN, HEAD_DIM_2), NSA_CMP_HIDDEN ** -0.5),
        'cmp_pe_v': nrm(ks[10], (L, NSA_CMP_LEN, HEAD_DIM_2), 0.1),
        'cmp_w1_v': nrm(ks[11], (L, cmp_in, NSA_CMP_HIDDEN), cmp_in ** -0.5),
        'cmp_w2_v': nrm(ks[12], (L, NSA_CMP_HIDDEN, HEAD_DIM_2), NSA_CMP_HIDDEN ** -0.5),
        'fox_q_norm': gain(ks[13], (L, HEAD_DIM_2)),
        'fox_k_norm': gain(ks[14], (L, HEAD_DIM_2)),
        'fox_f_bias': jax.random.uniform(ks[15], (L, FOX_HEADS), f32, 1.0, 4.0),
        'mem_q_norm': gain(ks[16], (L, MEM_HEAD_DIM)),
        'mem_k_norm': gain(ks[17], (L, MEM_HEAD_DIM)),
        'w_mem_kv': nrm(ks[18], (L, D_MODEL, 2 * MEM_WIDTH), D_MODEL ** -0.5),
        'w_branch_a': nrm(ks[19], (L, NSA_WIDTH, D_MODEL), NSA_WIDTH ** -0.5),
        'w_branch_b': nrm(ks[20], (L, FOX_WIDTH, D_MODEL), FOX_WIDTH ** -0.5),
        'w_branch_m': nrm(ks[21], (L, MEM_WIDTH, D_MODEL), MEM_WIDTH ** -0.5),
        'w_out': nrm(ks[22], (L, D_MODEL, D_MODEL), D_MODEL ** -0.5),
    }

def second_block(x, mem, norm_g, mem_norm_g, w_in, nsa_q_norm, nsa_k_norm,
              cmp_pe_k, cmp_w1_k, cmp_w2_k, cmp_pe_v, cmp_w1_v, cmp_w2_v,
              fox_q_norm, fox_k_norm, fox_f_bias, mem_q_norm, mem_k_norm, w_mem_kv,
              w_branch_a, w_branch_b, w_branch_m, w_out):
    B, T, D = x.shape
    for l in range(DEPTH):
        h = _rmsnorm(x, norm_g[l])
        z = h @ w_in[l]
        (nsa_q, nsa_kv, nsa_gate, nsa_silu, fox_qkv, fox_f, fox_silu,
         mem_q, mem_silu, merge_g) = _split(z, IN_SPLITS)
        o_a = _nsa(nsa_q, nsa_kv, nsa_gate, cmp_pe_k[l], cmp_w1_k[l], cmp_w2_k[l],
                   cmp_pe_v[l], cmp_w1_v[l], cmp_w2_v[l], nsa_q_norm[l], nsa_k_norm[l])
        o_a = o_a * jax.nn.silu(nsa_silu)
        o_b = _fox(fox_qkv, fox_f, fox_q_norm[l], fox_k_norm[l], fox_f_bias[l]) * jax.nn.silu(fox_silu)
        mem_kv = _rmsnorm(mem, mem_norm_g[l]) @ w_mem_kv[l]
        o_m = _memory_xattn(mem_q, mem_kv, mem_q_norm[l], mem_k_norm[l]) * jax.nn.silu(mem_silu)
        g = jax.nn.sigmoid(merge_g.astype(jnp.float32)).reshape(B, T, N_BRANCH, D).astype(x.dtype)
        u = (g[:, :, 0] * (o_a @ w_branch_a[l])
             + g[:, :, 1] * (o_b @ w_branch_b[l])
             + g[:, :, 2] * (o_m @ w_branch_m[l]))
        x = x + u @ w_out[l]
    return x


def setup_inputs(seed=0):
    out = dict(first_inputs(seed))
    for name, value in second_inputs(seed + 1).items():
        if name != "x":
            out[name + "_2"] = value
    return out


def reference(
    x, norm_mix_pre, norm_mix_post, norm_ffn_pre, norm_ffn_post, rel_bias, attn_w_qkv, attn_w_o,
    lru_w_in, lru_conv_w, lru_conv_b, lru_ga_w, lru_ga_b, lru_gx_w, lru_gx_b, lru_lambda,
    lru_w_out, ffn_w_up, ffn_conv_w, ffn_conv_b, ffn_w_down, mem_2, norm_g_2, mem_norm_g_2,
    w_in_2, nsa_q_norm_2, nsa_k_norm_2, cmp_pe_k_2, cmp_w1_k_2, cmp_w2_k_2, cmp_pe_v_2,
    cmp_w1_v_2, cmp_w2_v_2, fox_q_norm_2, fox_k_norm_2, fox_f_bias_2, mem_q_norm_2,
    mem_k_norm_2, w_mem_kv_2, w_branch_a_2, w_branch_b_2, w_branch_m_2, w_out_2,
):
    x = first_block(
        x, norm_mix_pre, norm_mix_post, norm_ffn_pre, norm_ffn_post, rel_bias, attn_w_qkv,
        attn_w_o, lru_w_in, lru_conv_w, lru_conv_b, lru_ga_w, lru_ga_b, lru_gx_w, lru_gx_b,
        lru_lambda, lru_w_out, ffn_w_up, ffn_conv_w, ffn_conv_b, ffn_w_down,
    )
    return second_block(
        x, mem_2, norm_g_2, mem_norm_g_2, w_in_2, nsa_q_norm_2, nsa_k_norm_2, cmp_pe_k_2,
        cmp_w1_k_2, cmp_w2_k_2, cmp_pe_v_2, cmp_w1_v_2, cmp_w2_v_2, fox_q_norm_2, fox_k_norm_2,
        fox_f_bias_2, mem_q_norm_2, mem_k_norm_2, w_mem_kv_2, w_branch_a_2, w_branch_b_2,
        w_branch_m_2, w_out_2,
    )


_drawn_inputs = setup_inputs


def setup_inputs(seed=0):
    import zlib

    import numpy as np

    out = dict(_drawn_inputs(seed))
    spreads = {}
    factors = {'lru_ga_b': 8.0,
     'lru_gx_b': 8.0,
     'mem_2': 2.729,
     'norm_g_2': 6.051,
     'mem_norm_g_2': 8.0,
     'nsa_q_norm_2': 8.0,
     'nsa_k_norm_2': 8.0,
     'cmp_pe_k_2': 8.0,
     'cmp_w1_k_2': 3.739,
     'cmp_w2_k_2': 3.663,
     'cmp_pe_v_2': 8.0,
     'fox_q_norm_2': 8.0,
     'fox_k_norm_2': 8.0,
     'mem_q_norm_2': 8.0,
     'mem_k_norm_2': 8.0}
    for name, (base, spread) in spreads.items():
        noise = np.random.default_rng([zlib.crc32(name.encode()), seed]).standard_normal(out[name].shape)
        drawn = base * np.exp(spread * noise) if base else spread * noise
        out[name] = __import__('jax').numpy.asarray(drawn.astype(out[name].dtype))
    for name, factor in factors.items():
        out[name] = (out[name] * factor).astype(out[name].dtype)
    return out
```

```python
from contextlib import ExitStack, contextmanager

import numpy as np
import concourse.bass as bass
from concourse import mybir

F32 = mybir.dt.float32
F32R = mybir.dt.float32r
BF16 = mybir.dt.bfloat16
I32 = mybir.dt.int32
ACT = mybir.ActivationFunctionType
ALU = mybir.AluOpType
AX_X = mybir.AxisListType.X

P = 128
T = 512
D = 1024
DC = D // P
TT = T // P
FC = 3 * D // P
NEG = -1.0e30
SLOTS = 3
EPS = 1e-6
CREDIT = 512

HEADS = 8
GROUPS = 3
DIL = 4
BIAS_W = T + 2 * P


class Tally:

    def __init__(self, sem, name, eng):
        self.sem, self.name, self.eng, self.n = sem, name, eng, 0


class Frame:

    def __init__(self, count):
        self.count, self.var, self.per, self.tags, self.closed = count, 0, {}, {}, False


class Mark:
    def __init__(self, tally, n, frames):
        self.tally, self.n, self.frames = tally, n, frames

    def fixed(self):
        return self.n + sum((f.count - 1) * f.per.get(self.tally, 0) for f in self.frames if f.closed)

    def moving(self):
        return [f for f in self.frames if not f.closed and f.per.get(self.tally, 0)]

    def value(self):
        v = self.fixed()
        for f in self.moving():
            v = v + f.var * f.per[self.tally]
        return v


class Program:

    def __init__(self, nc):
        self.nc, self.frames, self.tallies, self.counting = nc, [], [], False
        self.engines = (nc.tensor, nc.scalar, nc.vector)
        self.settled = {}
        self.waits = {}

    def tally(self, sem, name, eng):
        t = Tally(sem, name, eng)
        self.tallies.append(t)
        return t

    def op(self, tally, fn, *args, tag=None, **kw):
        if not self.counting:
            self.issue_waits(tally.eng)
            fn(*args, **kw).then_inc(tally.sem, 1)
        return self.step(tally, 1, tag)

    def step(self, tally, by, tag=None):
        tally.n += by
        m = Mark(tally, tally.n, list(self.frames))
        if tag is not None:
            self.frames[-1].tags[tag] = m
        return m

    def raw(self, eng, fn, *args, **kw):
        if not self.counting:
            self.issue_waits(eng)
            fn(*args, **kw)

    def wait(self, eng, *marks):
        if not self.counting:
            self.waits.setdefault(eng.engine, []).extend(m for m in marks if m is not None)

    def issue_waits(self, eng):
        latest = []
        for m in self.waits.pop(eng.engine, []):
            same = [k for k in latest if k.tally is m.tally and k.moving() == m.moving()]
            if not same:
                latest.append(m)
            elif m.fixed() > same[0].fixed():
                latest[latest.index(same[0])] = m
        for m in latest:
            eng.wait_ge(m.tally.sem, m.value())
        return bool(latest)

    def settle(self, eng):
        if not self.counting and self.issue_waits(eng):
            eng.sem_inc(self.settled[eng.engine], 1)

    def now(self, tally):
        return Mark(tally, tally.n, list(self.frames))

    def prev(self, tag):
        if self.counting:
            return None
        f = self.frames[-1]
        m = f.tags[tag]
        n = m.n - f.per[m.tally]
        assert n >= 1, f"{tag}: a wait below 1 in the first iteration"
        return Mark(m.tally, n, m.frames)

    def loop(self, count, body):
        if count == 1:
            body(0)
            return
        start = {t: t.n for t in self.tallies}
        outer, f = self.counting, Frame(count)
        self.counting = True
        self.frames.append(f)
        body(0)
        f.per = {t: t.n - start[t] for t in self.tallies}
        for t in self.tallies:
            t.n = start[t]
        self.counting = outer
        if not outer:
            for eng in self.engines:
                self.settle(eng)
            with self.nc.Fori(0, count) as i:
                f.var = i
                body(i)
                for eng in self.engines:
                    self.settle(eng)
            assert all(t.n - start[t] == f.per[t] for t in self.tallies)
        self.frames.pop()
        f.closed = True
        for t in self.tallies:
            t.n = start[t] + count * f.per[t]


def at(ap, i):
    return ap[:, bass.ds(i, 1), :].rearrange("p a n -> p (a n)")


class Chip:

    def __init__(self, nc, ctx, units_dram, n_units):
        self.nc, self.ctx = nc, ctx
        self.pe, self.act, self.dve, self.pool, self.sp = nc.tensor, nc.scalar, nc.vector, nc.gpsimd, nc.sync
        self.prog = Program(nc)
        self.names = {}
        self.units_dram, self.n_units = units_dram, n_units

        def tally(name, eng):
            return self.prog.tally(ctx.enter_context(nc.semaphore(name)), name, eng)

        self.t_unit = tally("unit_multiplied", self.pe)
        self.t_split = tally("unit_split", self.pool)
        self.t_pe = tally("pe_done", self.pe)
        self.t_act = tally("act_done", self.act)
        self.t_dve = tally("dve_done", self.dve)
        for name, eng in (("pe", self.pe), ("act", self.act), ("dve", self.dve), ("pool", self.pool)):
            self.prog.settled[eng.engine] = ctx.enter_context(nc.semaphore(f"settled_{name}"))
        for t in (self.t_pe, self.t_act, self.t_dve):
            t.eng.sem_inc(t.sem, CREDIT)
            t.n = CREDIT
        self.t_dma = tally("act_dma_done", self.act)
        self.s_loaded = [ctx.enter_context(nc.semaphore(f"unit_loaded_{s}")) for s in range(SLOTS)]
        self.s_hi = ctx.enter_context(nc.semaphore("unit_hi_done"))
        self.w_raw = [self.sb(ctx, f"w_raw{s}", [P, D], F32) for s in range(SLOTS)]
        self.w_hi = [self.sb(ctx, f"w_hi{s}", [P, D], F32R) for s in range(SLOTS)]
        self.w_lo = [self.sb(ctx, f"w_lo{s}", [P, D], F32R) for s in range(SLOTS)]
        self.bank = [ctx.enter_context(nc.psum_tensor(f"bank{b}", [P, T], F32)) for b in range(8)]
        self.x = self.sb(ctx, "x_res", [P, DC, T], F32)
        self.ident = self.sb(ctx, "ident", [P, P], F32)
        self.ones = self.sb(ctx, "ones", [P, P], F32)

    def sb(self, ctx, name, shape, dt):
        n = self.names[name] = self.names.get(name, 0) + 1
        name = name if n == 1 else f"{name}_{n}"
        return ctx.enter_context(self.nc.sbuf_tensor(name, shape, dt))

    def A(self, out, in_, func, tag=None, **kw):
        return self.prog.op(self.t_act, self.act.activation, out, in_, func, tag=tag, **kw)

    def V(self, name, *args, tag=None, **kw):
        return self.prog.op(self.t_dve, name, *args, tag=tag, **kw)

    def tt(self, out, a, b, op, tag=None):
        return self.V(self.dve.tensor_tensor, out, a, b, op, tag=tag)

    def stt(self, out, a, s, b, op0, op1, tag=None):
        return self.V(self.dve.scalar_tensor_tensor, out, a, s, b, op0, op1, tag=tag)

    def ts(self, out, a, s1, op0, s2=None, op1=None, tag=None):
        if op1 is None:
            return self.V(self.dve.tensor_scalar, out, a, s1, None, op0, tag=tag)
        return self.V(self.dve.tensor_scalar, out, a, s1, s2, op0, op1, tag=tag)

    def copy(self, out, a, tag=None):
        return self.V(self.dve.tensor_copy, out, a, tag=tag)

    def mm(self, out, lhsT, rhs, start=True, stop=True, done=True, tag=None, **kw):
        if done:
            return self.prog.op(self.t_pe, self.pe.matmul, out, lhsT, rhs, start=start, stop=stop, tag=tag, **kw)
        self.prog.raw(self.pe, self.pe.matmul, out, lhsT, rhs, start=start, stop=stop, **kw)

    def load(self, out, in_):
        if self.t_dma.n:
            self.wait(self.act, self.prog.now(self.t_dma))
        if not self.prog.counting:
            self.prog.issue_waits(self.act)
            self.act.dma_start(out, in_).then_inc(self.t_dma.sem, 16)
        return self.prog.step(self.t_dma, 16)

    def wait(self, eng, *marks):
        self.prog.wait(eng, *marks)

    def pe_now(self):
        return [self.prog.now(self.t_pe), self.prog.now(self.t_unit)]

    def fence(self):
        marks = [m for m in [self.prog.now(t) for t in (self.t_pe, self.t_unit, self.t_act, self.t_dve, self.t_dma)] if m.n > 0]
        for eng in (self.pe, self.act, self.dve):
            self.wait(eng, *marks)

    def weight_stream(self):
        full, rest = divmod(self.n_units, SLOTS)

        def fetch(u, s, first):
            if not first:
                self.sp.wait_ge(self.t_split.sem, u - SLOTS + 1)
            self.sp.dma_start(self.w_raw[s][:, :], self.units_dram[bass.ds(u, 1)].rearrange("a p n -> (a p) n"))\
                .then_inc(self.s_loaded[s], 16)

        def split(u, s, turn, first):
            self.pool.wait_ge(self.s_loaded[s], 16 * turn + 16)
            if not first:
                self.pool.wait_ge(self.t_unit.sem, u - SLOTS + 1)
            self.pool.sem_inc(self.prog.settled[self.pool.engine], 1)
            self.pool.tensor_scalar(self.w_hi[s][:, :], self.w_raw[s][:, :], 1.0, 0.0, ALU.mult, ALU.add)\
                .then_inc(self.s_hi, 1)
            self.pool.wait_ge(self.s_hi, u + 1)
            self.pool.tensor_tensor(self.w_lo[s][:, :], self.w_raw[s][:, :], self.w_hi[s][:, :].bitcast(F32),
                                    ALU.subtract).then_inc(self.t_split.sem, 1)

        for s in range(SLOTS):
            fetch(s, s, True)
        with self.sp.Fori(1, full) as j:
            for s in range(SLOTS):
                fetch(SLOTS * j + s, s, False)
        for s in range(rest):
            fetch(SLOTS * full + s, s, False)
        for s in range(SLOTS):
            split(s, s, 0, True)
        with self.pool.Fori(1, full) as j:
            for s in range(SLOTS):
                split(SLOTS * j + s, s, j, False)
        for s in range(rest):
            split(SLOTS * full + s, s, full, False)

    def unit(self, jobs, tag=None):
        slot = self.t_unit.n % SLOTS
        if not self.prog.counting:
            self.prog.issue_waits(self.pe)
            self.pe.wait_ge(self.t_split.sem, Mark(self.t_unit, self.t_unit.n + 1, list(self.prog.frames)).value())
        hi, lo = self.w_hi[slot], self.w_lo[slot]
        todo = []
        for out, tiles, start, stop in jobs:
            for n, (tile, rh, rl) in enumerate(tiles):
                w = slice(tile * P, tile * P + P)
                for k, (a, b) in enumerate(((hi, rh), (hi, rl), (lo, rh))):
                    todo.append((out, a[:, w], b, start and n == 0 and k == 0, stop and n == len(tiles) - 1 and k == 2))
        for out, a, b, start, stop in todo[:-1]:
            self.prog.raw(self.pe, self.pe.matmul, out, a, b, start=start, stop=stop)
        out, a, b, start, stop = todo[-1]
        return self.prog.op(self.t_unit, self.pe.matmul, out, a, b, start=start, stop=stop, tag=tag)

    def project(self, out, hi, lo, k0=0, start=True, stop=True, tag=None):
        return self.unit([(out, [(k, hi[:, k0 + k, :], lo[:, k0 + k, :]) for k in range(DC)], start, stop)], tag=tag)

    def rsqrt(self, r, ss, tmp, scale, ready):
        m, a = tmp
        self.wait(self.dve, *ready)
        d = self.ts(m, ss, scale, ALU.mult, EPS, ALU.add)
        self.wait(self.dve, d)
        d = self.V(self.dve.tensor_scalar, a.bitcast(I32), m.bitcast(I32), 1, None, ALU.logical_shift_right)
        self.wait(self.dve, d)
        d = self.ts(r.bitcast(I32), a.bitcast(I32), -1.0, ALU.mult, float(0x5F3759DF), ALU.add)
        for _ in range(3):
            self.wait(self.dve, d)
            d = self.tt(a, r, r, ALU.mult)
            self.wait(self.dve, d)
            d = self.stt(a, a, -0.5, m, ALU.mult, ALU.mult)
            self.wait(self.dve, d)
            d = self.stt(r, a, 1.5, r, ALU.add, ALU.mult)
        return d

    def token_scale(self, bank, r, n_tiles, ready):
        self.wait(self.pe, *ready)
        for t in range(n_tiles):
            m = self.mm(bank[:, t * P:t * P + P], r[:, t:t + 1].to_broadcast([P, P]), self.ident[:, :],
                        is_transpose=True, done=t == n_tiles - 1)
        return m

    def sum_tokens(self, bank, sq, n_tiles, first, last, ready, order):
        self.wait(self.pe, *ready)
        for t in range(n_tiles):
            m = self.mm(bank[:, t:t + 1], sq[:, t * P:t * P + P], self.ones[:, 0:1], start=first and t == 0,
                        stop=last, done=t == n_tiles - 1, skip_group_check=True)
        return m


def pre_norm(c, src, gain, hi, lo, n_tiles, sq, tmp, narrow, ready):
    n = n_tiles * P
    bank_ss, bank_r = c.bank[7], c.bank[6]
    sq_done, ss_done = [], []
    for k in range(DC):
        c.wait(c.act, *ready[k])
        if k >= 2:
            c.wait(c.act, ss_done[k - 2])
        sq_done.append(c.A(sq[k % 2][:, 0:n], src[:, k, :], ACT.Square))
        ss_done.append(c.sum_tokens(bank_ss, sq[k % 2], n_tiles, k == 0, k == DC - 1, [sq_done[k]], k))
    r, m, a = narrow
    d = c.rsqrt(r[:, 0:n_tiles], bank_ss[:, 0:n_tiles], (m[:, 0:n_tiles], a[:, 0:n_tiles]), 1.0 / D, [ss_done[-1]])
    bc = c.token_scale(bank_r, r, n_tiles, [d])
    c.wait(c.dve, bc)
    out, hi_done = [], []
    for k in range(DC):
        if k >= 2:
            c.wait(c.dve, hi_done[k - 2], out[k - 2])
        h = c.stt(tmp[k % 2][:, 0:n], src[:, k, :], gain[:, k:k + 1], bank_r[:, 0:n], ALU.mult, ALU.mult)
        c.wait(c.act, h)
        hi_done.append(c.A(hi[:, k, :], tmp[k % 2][:, 0:n], ACT.Copy))
        if k >= 1:
            c.wait(c.dve, hi_done[k - 1])
            out.append(c.tt(lo[:, k - 1, :], tmp[(k - 1) % 2][:, 0:n], hi[:, k - 1, :].bitcast(F32), ALU.subtract))
    c.wait(c.dve, hi_done[-1])
    out.append(c.tt(lo[:, DC - 1, :], tmp[(DC - 1) % 2][:, 0:n], hi[:, DC - 1, :].bitcast(F32), ALU.subtract))
    return out


def post_norm_add(c, y, gain, acc, t2, narrow, ready):
    bank_ss, bank_r = c.bank[7], c.bank[6]
    ss = c.sum_tokens(bank_ss, acc, TT, True, True, ready, 0)
    r, m, a = narrow
    d = c.rsqrt(r[:, 0:TT], bank_ss[:, 0:TT], (m[:, 0:TT], a[:, 0:TT]), 1.0 / D, [ss])
    bc = c.token_scale(bank_r, r, TT, [d])
    c.wait(c.dve, bc)
    out, scaled = [], []
    for k in range(DC + 1):
        if k < DC:
            if k >= 2:
                c.wait(c.dve, out[k - 2])
            scaled.append(c.stt(t2[k % 2][:, :], y[:, k, :], gain[:, k:k + 1], bank_r[:, :], ALU.mult, ALU.mult))
        if k >= 1:
            c.wait(c.dve, scaled[k - 1])
            out.append(c.tt(c.x[:, k - 1, :], c.x[:, k - 1, :], t2[(k - 1) % 2][:, :], ALU.add))
    return [[m] for m in out]


def collect(c, n, bank, y, acc, sq, ready, tag, first):
    c.wait(c.act, ready)
    e = c.A(at(y, n), bank, ACT.Copy, tag=tag + "_y")
    if not first:
        c.wait(c.act, c.prog.prev(tag + "_acc") if c.prog.frames else None)
    s = c.A(sq, bank, ACT.Square, tag=tag + "_sq")
    c.wait(c.dve, s)
    c.wait(c.dve, c.prog.now(c.t_dve))
    a = c.tt(acc, acc, sq, ALU.add, tag=tag + "_acc")
    return s, a


class Recent:

    def __init__(self, prog):
        self.prog, self.marks, self.looped = prog, {}, False

    def keep(self, key, mark):
        self.marks[key] = mark
        if self.looped:
            self.prog.frames[-1].tags[key] = mark
        return mark

    def get(self, key):
        if key in self.marks:
            return self.marks[key]
        if self.looped and (self.prog.counting or key in self.prog.frames[-1].tags):
            return self.prog.prev(key) if not self.prog.counting else None
        return None

    def over(self, total, group, body):
        full = total // group

        def turn(i):
            self.marks = {}
            self.looped = full > 1
            for j in range(group):
                body(i * group + j, j)
            self.looped = False

        self.prog.loop(full, turn)
        for j in range(total - full * group):
            body(full * group + j, j)


def out_projection(c, y, acc, sq, hi, lo, units_per_out, group, ready):
    c.wait(c.dve, *ready)
    zero = c.V(c.dve.memset, acc[:, :], 0.0)
    c.fence()
    c.wait(c.dve, zero)
    rec = Recent(c.prog)

    def chunk(n, j):
        c.wait(c.pe, rec.get(f"square{j}"))
        for q in range(units_per_out):
            full = c.project(c.bank[j][:, :], hi, lo, q * DC, q == 0, q == units_per_out - 1)
        c.wait(c.act, full)
        c.A(at(y, n), c.bank[j][:, :], ACT.Copy)
        c.wait(c.act, rec.get(f"sum{j}"))
        s = rec.keep(f"square{j}", c.A(sq[j][:, :], c.bank[j][:, :], ACT.Square))
        c.wait(c.dve, s, c.prog.now(c.t_dve))
        rec.keep(f"sum{j}", c.tt(acc[:, :], acc[:, :], sq[j][:, :], ALU.add))

    rec.over(DC, group, chunk)
    return c.prog.now(c.t_dve)


def dilated_attention(c, ctx, hn_hi, hn_lo, hn_ready, oh, ol, bias_dram):
    nc = c.nc
    rec = Recent(c.prog)
    scale = float(P) ** -0.5
    q = [[c.sb(ctx, f"q{s}{g}", [P, DIL, P], F32) for g in range(GROUPS)] for s in range(2)]
    k = [[c.sb(ctx, f"k{s}{g}", [P, DIL, P], F32) for g in range(GROUPS)] for s in range(2)]
    v = [[c.sb(ctx, f"v{s}{g}", [P, TT, P], F32) for g in range(GROUPS)] for s in range(2)]
    vt = [c.sb(ctx, f"vt{g}", [P, DIL, P], F32) for g in range(GROUPS)]
    bias = [c.sb(ctx, f"bias{s}", [P, DIL * T + 2 * P], F32) for s in range(2)]
    logit = [c.sb(ctx, f"logit{s}", [P, BIAS_W], F32) for s in range(2)]
    pt = [c.sb(ctx, f"pt{s}", [P, BIAS_W], F32) for s in range(2)]
    stat = [c.sb(ctx, f"stat{s}", [P, 4], F32) for s in range(2)]
    b_s0, b_s1, b_t0, b_t1, b_o = c.bank[3], c.bank[4], c.bank[5], c.bank[6], c.bank[7]

    def by_residue(ap):
        return ap.rearrange("p (u r) -> p r u", r=DIL)

    def logits(s, r):
        c.wait(c.pe, rec.get("biased"), *[rec.get(f"qk{s}{g}") for g in range(GROUPS)])
        c.mm(b_s0[:, :], q[s][0][:, r, :], k[s][0][:, :, :].rearrange("p a b -> p (a b)"), done=False)
        c.mm(b_s1[:, 0:P], q[s][1][:, r, :], k[s][1][:, r, :], done=False)
        m = c.mm(b_s1[:, P:2 * P], q[s][2][:, r, :], k[s][2][:, r, :])
        w, st = logit[r % 2], stat[r % 2]
        c.wait(c.dve, m, rec.get(f"bias{s}"), rec.get(f"pt{r % 2}"), rec.get(f"normed{r % 2}"))
        c.tt(w[:, 0:T], b_s0[:, :], bias[s][:, r * T:(r + 1) * T], ALU.add)
        d = rec.keep("biased", c.tt(w[:, T:BIAS_W], b_s1[:, 0:2 * P], bias[s][:, DIL * T:], ALU.add))
        c.wait(c.dve, d)
        d = c.V(c.dve.reduce_max, st[:, 0:1], w[:, :], AX_X)
        c.wait(c.dve, d)
        d = c.ts(st[:, 1:2], st[:, 0:1], -1.0, ALU.mult)
        c.wait(c.act, d)
        e = c.A(w[:, :], w[:, :], ACT.Exp, bias=st[:, 1:2], accum_out=st[:, 2:3])
        c.wait(c.dve, e)
        d = c.V(c.dve.reciprocal, st[:, 3:4], st[:, 2:3])
        c.wait(c.dve, d)
        rec.keep(f"normed{r % 2}", c.ts(w[:, :], w[:, :], st[:, 3:4], ALU.mult))

    def transposes(s, r):
        w = logit[r % 2]
        c.wait(c.pe, rec.get(f"normed{r % 2}"), rec.get("t0_free"), rec.get("t1_free"))
        for j in range(6):
            b = b_t0[:, j * P:j * P + P] if j < 4 else b_t1[:, (j - 4) * P:(j - 3) * P]
            m = c.mm(b, w[:, j * P:j * P + P], c.ident[:, :], is_transpose=True, done=j == 5)
        rec.keep(f"pt{r % 2}", m)
        c.wait(c.act, m, rec.get(f"pv{r % 2}"))
        rec.keep("t0_free", c.A(pt[r % 2][:, 0:T], b_t0[:, :], ACT.Copy))
        c.wait(c.dve, m, rec.get(f"pv{r % 2}"))
        rec.keep("t1_free", c.copy(pt[r % 2][:, T:BIAS_W], b_t1[:, 0:2 * P]))

    def values(s, r):
        c.wait(c.pe, rec.get("t0_free"), rec.get("t1_free"), *[rec.get(f"v{s}{g}") for g in range(GROUPS)])
        if r == 0:
            c.wait(c.pe, rec.get("o_free"))
        keys = [v[s][0][:, j, :] for j in range(TT)] + [v[s][1][:, r, :], v[s][2][:, r, :]]
        for j, vj in enumerate(keys):
            m = c.mm(b_o[:, r * P:r * P + P], vj, pt[r % 2][:, j * P:j * P + P], start=j == 0, stop=j == 5, done=j == 5)
        return rec.keep(f"pv{r % 2}", m)

    def finish(h, m):
        o_nat = b_o[:, :].rearrange("p (r u) -> p u r", r=DIL)
        c.wait(c.act, m)
        e = c.A(at(oh, h).rearrange("p (u r) -> p u r", r=DIL), o_nat, ACT.Copy)
        c.wait(c.dve, e)
        rec.keep("o_free", c.tt(at(ol, h).rearrange("p (u r) -> p u r", r=DIL), o_nat,
                                at(oh, h).bitcast(F32).rearrange("p (u r) -> p u r", r=DIL), ALU.subtract))

    def v_rows(s, g):
        c.wait(c.pe, rec.get(f"vt{g}"), rec.get("t0_free"))
        for j in range(TT):
            m = c.mm(b_t0[:, j * P:j * P + P], vt[g][:, j, :], c.ident[:, :], is_transpose=True, done=j == TT - 1)
        rec.keep(f"vt_read{g}", m)
        c.wait(c.act, m)
        rec.keep("t0_free", rec.keep(f"v{s}{g}", c.A(v[s][g][:, :, :].rearrange("p a b -> p (a b)"), b_t0[:, :], ACT.Copy)))

    kinds = [("v", 0), ("v", 1), ("v", 2), ("q", 0), ("k", 0), ("q", 1), ("k", 1), ("q", 2), ("k", 2)]

    def head(h, s, attend):
        c.wait(c.act, rec.get("biased"))
        rec.keep(f"bias{s}", c.load(bias[s][:, :], bias_dram[bass.ds(h, 1)].rearrange("a p n -> (a p) n")))
        for j, (kind, g) in enumerate(kinds):
            b = c.bank[j % 3]
            c.wait(c.pe, rec.get(f"bank{j % 3}"))
            if attend is None:
                c.wait(c.pe, *hn_ready)
            m = c.project(b[:, :], hn_hi, hn_lo)
            natural = g == 0 and kind != "q"
            src = b[:, :].rearrange("p (a b) -> p a b", a=TT) if natural else by_residue(b[:, :])
            if kind == "v":
                c.wait(c.dve, m, rec.get(f"vt_read{g}"))
                rec.keep(f"bank{j % 3}", rec.keep(f"vt{g}", c.copy(vt[g][:, :, :], src)))
            elif kind == "q":
                c.wait(c.act, m)
                rec.keep(f"bank{j % 3}", c.A(q[s][g][:, :, :], src, ACT.Copy, scale=scale))
            else:
                c.wait(c.act, m)
                rec.keep(f"bank{j % 3}", rec.keep(f"qk{s}{g}", c.A(k[s][g][:, :, :], src, ACT.Copy)))
            if attend is not None:
                r = j // 2
                if j % 2 == 0:
                    if r >= 1:
                        m = values(attend[1], r - 1)
                    if r < DIL:
                        logits(attend[1], r)
                else:
                    transposes(attend[1], r)
            if 1 <= j <= 3:
                v_rows(s, j - 1)
        if attend is not None:
            finish(attend[0], m)

    head(0, 0, None)
    c.fence()

    def two_heads(i):
        rec.marks = {}
        rec.looped = True
        head(i * 2 + 1, 1, (i * 2, 0))
        head(i * 2 + 2, 0, (i * 2 + 1, 1))
        rec.looped = False

    c.prog.loop(HEADS // 2 - 1, two_heads)
    head(HEADS - 1, 1, (HEADS - 2, 0))
    for r in range(DIL):
        logits(1, r)
        transposes(1, r)
        m = values(1, r)
    finish(HEADS - 1, m)
    return [c.prog.now(c.t_act), c.prog.now(c.t_dve)]


def conv_ffn(c, layer, taps, gain_pre, gain_post, x_ready, narrow):
    with ExitStack() as ctx:
        hid_hi = c.sb(ctx, f"hid_hi{layer}", [P, FC, T], F32R)
        hid_lo = c.sb(ctx, f"hid_lo{layer}", [P, FC, T], F32R)
        with ExitStack() as up:
            hi = c.sb(up, f"ffn_hi{layer}", [P, DC, T], F32R)
            lo = c.sb(up, f"ffn_lo{layer}", [P, DC, T], F32R)
            tap = c.sb(up, f"tap{layer}", [P, 24], F32)
            cg = [c.sb(up, f"cg{layer}{j}", [P, T], F32) for j in range(2)]
            cv = [c.sb(up, f"cv{layer}{j}", [P, T], F32) for j in range(2)]
            c.fence()
            ready = pre_norm(c, c.x, gain_pre, hi, lo, TT, cg, cv, narrow, x_ready)
            c.wait(c.pe, *ready)
            c.fence()
            rec = Recent(c.prog)

            def pair(n, j):
                if j == 0:
                    c.wait(c.dve, rec.get("taps_used_act"), c.prog.now(c.t_dve))
                    at_n = taps[:, bass.ds(n * 8, 24)]
                    rec.keep("taps", c.copy(tap[:, :], at_n))
                s = j % 2
                halves = []
                for half, buf in ((0, cg[s]), (1, cv[s])):
                    b, w = c.bank[2 * j + half], tap[:, 8 * j + 4 * half:8 * j + 4 * half + 4]
                    c.wait(c.pe, rec.get(f"bank{j}{half}"))
                    m = c.project(b[:, :], hi, lo)
                    c.wait(c.act, m, rec.get("taps"), rec.get(f"hid{s}"), rec.get(f"gated{s}"))
                    e = c.A(buf[:, :], b[:, :], ACT.Identity, scale=w[:, 2:3], bias=w[:, 3:4])
                    rec.keep("taps_used_act", e)
                    c.wait(c.dve, e)
                    d = c.stt(buf[:, 1:T], b[:, 0:T - 1], w[:, 1:2], buf[:, 1:T], ALU.mult, ALU.add)
                    c.wait(c.dve, d)
                    d = rec.keep(f"bank{j}{half}", c.stt(buf[:, 2:T], b[:, 0:T - 2], w[:, 0:1], buf[:, 2:T], ALU.mult, ALU.add))
                    halves.append(d)
                c.wait(c.act, halves[0])
                e = c.A(cg[s][:, :], cg[s][:, :], ACT.Gelu_apprx_tanh)
                c.wait(c.dve, e, halves[1])
                d = c.tt(cv[s][:, :], cg[s][:, :], cv[s][:, :], ALU.mult)
                c.wait(c.act, d)
                e = rec.keep(f"gated{s}", c.A(at(hid_hi, n), cv[s][:, :], ACT.Copy))
                c.wait(c.dve, e)
                rec.keep(f"hid{s}", c.tt(at(hid_lo, n), cv[s][:, :], at(hid_hi, n).bitcast(F32), ALU.subtract))

            rec.over(FC, 3, pair)
        with ExitStack() as down:
            y = c.sb(down, f"ffn_y{layer}", [P, DC, T], F32)
            acc = c.sb(down, f"ffn_acc{layer}", [P, T], F32)
            sq = [c.sb(down, f"ffn_sq{layer}{j}", [P, T], F32) for j in range(2)]
            c.fence()
            done = out_projection(c, y, acc, sq, hid_hi, hid_lo, FC // DC, 2, [])
            return post_norm_add(c, y, gain_post, acc, sq, narrow, [done])


def log_sigmoid(c, out, v, w, ready):
    e, z2, p = w
    c.wait(c.act, *ready)
    m = c.A(e, v, ACT.Abs)
    c.wait(c.act, m)
    m = c.A(e, e, ACT.Exp, scale=-1.0)
    c.wait(c.dve, m, *ready)
    m = c.ts(p, e, 2.0, ALU.add)
    c.wait(c.dve, m)
    m = c.V(c.dve.reciprocal, p, p)
    c.wait(c.dve, m)
    m = c.tt(e, e, p, ALU.mult)
    c.wait(c.dve, m)
    m = c.tt(z2, e, e, ALU.mult)
    c.wait(c.dve, m)
    m = c.ts(p, z2, 1.0 / 17, ALU.mult, 1.0 / 15, ALU.add)
    for d in (13, 11, 9, 7, 5, 3, 1):
        c.wait(c.dve, m)
        m = c.tt(p, p, z2, ALU.mult)
        c.wait(c.dve, m)
        m = c.ts(p, p, 1.0 / d, ALU.add)
    c.wait(c.dve, m)
    m = c.stt(p, p, -2.0, e, ALU.mult, ALU.mult)
    c.wait(c.dve, m)
    return c.stt(out, v, 0.0, p, ALU.min, ALU.add)


def rglru(c, lru, gain_pre, gain_post, x_ready, narrow):
    with ExitStack() as ctx:
        xb = c.sb(ctx, "xb", [P, DC, T], F32)
        sh = c.sb(ctx, "split_hi", [P, DC, T], F32R)
        sl = c.sb(ctx, "split_lo", [P, DC, T], F32R)
        ga = c.sb(ctx, "gate_a", [P, DC, T], F32)
        gx = c.sb(ctx, "gate_x", [P, DC, T], F32)
        cl = c.sb(ctx, "log_a_rate", [P, DC], F32)
        lam = c.sb(ctx, "lam", [P, DC], F32)
        lw = [c.sb(ctx, f"lam_tmp{j}", [P, DC], F32) for j in range(3)]
        tap = c.sb(ctx, "lru_tap", [P, 24], F32)
        with ExitStack() as inner:
            hi = c.sb(inner, "lru_in_hi", [P, DC, T], F32R)
            lo = c.sb(inner, "lru_in_lo", [P, DC, T], F32R)
            th = c.sb(inner, "tanh_sqrt_h", [P, DC, T], F32)
            tmp = [c.sb(inner, f"lru_t{j}", [P, T], F32) for j in range(2)]
            sq = [c.sb(inner, f"lru_u{j}", [P, T], F32) for j in range(2)]
            c.fence()
            cols = lru.rearrange("p (n k) -> p k n", k=8)
            d = c.copy(lam[:, :], cols[:, 7, 0:DC])
            d = log_sigmoid(c, cl[:, :], lam[:, :], [w[:, :] for w in lw], [d])
            c.wait(c.dve, d)
            rate = c.ts(cl[:, :], cl[:, :], 8.0, ALU.mult)
            ready = pre_norm(c, c.x, gain_pre, hi, lo, TT, sq, tmp, narrow, x_ready)
            c.wait(c.pe, *ready)
            c.fence()
            rec = Recent(c.prog)

            def conv(n, j):
                if j == 0:
                    c.wait(c.dve, rec.get("taps_used_act"), c.prog.now(c.t_dve))
                    rec.keep("taps", c.copy(tap[:, :], lru[:, bass.ds(n * 8, 24)]))
                b, w, buf = c.bank[j], tap[:, 8 * j:8 * j + 8], at(xb, n)
                c.wait(c.pe, rec.get(f"bank{j}"))
                m = c.project(b[:, :], hi, lo)
                c.wait(c.act, m, rec.get("taps"))
                e = rec.keep("taps_used_act", c.A(buf, b[:, :], ACT.Identity, scale=w[:, 3:4], bias=w[:, 4:5]))
                for lag in (1, 2, 3):
                    part = xb[:, bass.ds(n, 1), lag:T].rearrange("p a n -> p (a n)")
                    c.wait(c.dve, e)
                    e = c.stt(part, b[:, 0:T - lag], w[:, 3 - lag:4 - lag], part, ALU.mult, ALU.add)
                rec.keep(f"bank{j}", e)
                c.wait(c.act, e)
                e = c.A(at(sh, n), buf, ACT.Copy)
                c.wait(c.dve, e)
                c.tt(at(sl, n), buf, at(sh, n).bitcast(F32), ALU.subtract)

            rec.over(DC, 3, conv)
            c.fence()
            gated = {}
            for b in range(4):
                banks = [c.bank[4 * (b % 2) + q] for q in range(4)]
                if b >= 2:
                    c.wait(c.pe, gated[b - 2])
                m = c.unit([(banks[q][:, :], [(2 * q + k, sh[:, 2 * b + k, :], sl[:, 2 * b + k, :]) for k in range(2)], True, True)
                            for q in range(4)])
                c.wait(c.act, m)
                for n in range(2):
                    ch = 2 * b + n
                    c.A(ga[:, ch, :], banks[n][:, :], ACT.Sigmoid, bias=cols[:, 5, ch:ch + 1])
                    e = c.A(gx[:, ch, :], banks[2 + n][:, :], ACT.Sigmoid, bias=cols[:, 6, ch:ch + 1])
                    c.wait(c.dve, e)
                    c.tt(gx[:, ch, :], gx[:, ch, :], xb[:, ch, :], ALU.mult)
                gated[b] = e
            c.wait(c.pe, e)
            gb = [c.project(c.bank[n][:, :], hi, lo) for n in range(DC)]
            c.wait(c.act, rate, e)
            roots = []
            for ch in range(DC):
                e = c.A(th[:, ch, :], ga[:, ch, :], ACT.Tanh, scale=cl[:, ch:ch + 1])
                c.wait(c.act, e)
                e = c.A(ga[:, ch, :], ga[:, ch, :], ACT.Exp, scale=cl[:, ch:ch + 1])
                c.wait(c.dve, e)
                if ch >= 2:
                    c.wait(c.dve, roots[ch - 2])
                d = c.tt(tmp[ch % 2][:, :], ga[:, ch, :], ga[:, ch, :], ALU.mult)
                c.wait(c.dve, d)
                d = c.stt(th[:, ch, :], tmp[ch % 2][:, :], 1.0, th[:, ch, :], ALU.add, ALU.mult)
                c.wait(c.dve, d)
                roots.append(c.ts(th[:, ch, :], th[:, ch, :], -1.0, ALU.mult, 0.0, ALU.max))
            hs = []
            for ch in range(DC):
                c.wait(c.act, roots[ch])
                e = c.A(th[:, ch, :], th[:, ch, :], ACT.Sqrt)
                c.wait(c.dve, e)
                d = c.tt(gx[:, ch, :], gx[:, ch, :], th[:, ch, :], ALU.mult)
                c.wait(c.dve, d)
                hs.append(c.V(c.dve.tensor_tensor_scan, th[:, ch, :], ga[:, ch, :], gx[:, ch, :], 0.0, ALU.mult, ALU.add))
            split = []
            for ch in range(DC):
                c.wait(c.act, gb[ch])
                if ch >= 2:
                    c.wait(c.act, split[ch - 2])
                e = c.A(tmp[ch % 2][:, :], c.bank[ch][:, :], ACT.Gelu_apprx_tanh)
                c.wait(c.dve, e, hs[ch])
                d = c.tt(tmp[ch % 2][:, :], tmp[ch % 2][:, :], th[:, ch, :], ALU.mult)
                c.wait(c.act, d)
                e = c.A(sh[:, ch, :], tmp[ch % 2][:, :], ACT.Copy)
                c.wait(c.dve, e)
                split.append(c.tt(sl[:, ch, :], tmp[ch % 2][:, :], sh[:, ch, :].bitcast(F32), ALU.subtract))
            c.fence()
        y = c.sb(ctx, "lru_y", [P, DC, T], F32)
        acc = c.sb(ctx, "lru_acc", [P, T], F32)
        sq = [c.sb(ctx, f"lru_sq{j}", [P, T], F32) for j in range(3)]
        done = out_projection(c, y, acc, sq, sh, sl, 1, 3, [])
        return post_norm_add(c, y, gain_post, acc, sq, narrow, [done])


N_COLS = 8 * 8
UNITS_1 = 72 + 8 + 72 + 20 + 8 + 72


def block_one(c, gains, lru, taps, bias_dram, x_ready, narrow):
    def gain(kind, layer):
        k = (kind * 2 + layer) * DC
        return gains[:, k:k + DC]

    with ExitStack() as ctx:
        oh = c.sb(ctx, "attn_o_hi", [P, DC, T], F32R)
        ol = c.sb(ctx, "attn_o_lo", [P, DC, T], F32R)
        with ExitStack() as inner:
            hi = c.sb(inner, "attn_hi", [P, DC, T], F32R)
            lo = c.sb(inner, "attn_lo", [P, DC, T], F32R)
            tmp = [c.sb(inner, f"an_t{j}", [P, T], F32) for j in range(4)]
            ready = pre_norm(c, c.x, gain(0, 0), hi, lo, TT, tmp[0:2], tmp[2:4], narrow, x_ready)
            dilated_attention(c, inner, hi, lo, ready, oh, ol, bias_dram)
            c.fence()
        y = c.sb(ctx, "attn_y", [P, DC, T], F32)
        acc = c.sb(ctx, "attn_acc", [P, T], F32)
        sq = [c.sb(ctx, f"attn_sq{j}", [P, T], F32) for j in range(3)]
        done = out_projection(c, y, acc, sq, oh, ol, 1, 3, [])
        x_ready = post_norm_add(c, y, gain(1, 0), acc, sq, narrow, [done])
    x_ready = conv_ffn(c, 0, taps[:, 0:8 * FC], gain(2, 0), gain(3, 0), x_ready, narrow)
    x_ready = rglru(c, lru, gain(0, 1), gain(1, 1), x_ready, narrow)
    return conv_ffn(c, 1, taps[:, 8 * FC:16 * FC], gain(2, 1), gain(3, 1), x_ready, narrow)


def build(nc, t, out, stop_after_one=False):
    with ExitStack() as ctx:
        n_units = UNITS_1 if stop_after_one else UNITS_1 + UNITS_2
        c = Chip(nc, ctx, t["units"], n_units)
        gains = c.sb(ctx, "gains", [P, N_COLS], F32)
        lru = c.sb(ctx, "lru_cols", [P, 72], F32)
        taps = c.sb(ctx, "taps", [P, 16 * FC], F32)
        narrow = [c.sb(ctx, f"narrow{j}", [P, 8], F32) for j in range(3)]
        c.load(c.x[:, :, :].rearrange("p a b -> p (a b)"), t["x"])
        x_in = c.prog.now(c.t_dma)
        for dst, src in ((gains, "gains"), (lru, "lru"), (taps, "taps"), (c.ident, "ident")):
            c.wait(c.act, c.prog.now(c.t_dma))
            c.load(dst[:, :], t[src])
        d = c.V(c.dve.memset, c.ones[:, :], 1.0)
        c.wait(c.pe, d)
        loaded = c.prog.now(c.t_dma)
        c.weight_stream()
        for eng in (c.pe, c.dve):
            c.wait(eng, loaded)
        x_ready = block_one(c, gains, lru, taps, t["bias"], [[loaded]] * DC, narrow)
        if not stop_after_one:
            x_ready = block_two(c, t, x_ready, narrow)
        for m in x_ready:
            c.wait(c.act, *m)
        c.wait(c.act, c.prog.now(c.t_dma))
        m = c.load(out, c.x[:, :, :].rearrange("p a b -> p (a b)"))
        c.wait(c.act, m)
        c.prog.issue_waits(c.act)


HD = 64
M = 256
MT = M // P
CMP_L, CMP_S = 32, 16
NC = T // CMP_S - 1
LAYER_COLS = 2 * DC + 9 + 2 * CMP_L + P + HD
C_NORM, C_MEMNORM, C_GAINS, C_PE, C_W2 = 0, DC, 2 * DC, 2 * DC + 9, 2 * DC + 9 + 2 * CMP_L
G_NSA_Q, G_CMP_K, G_SEL_K, G_WIN_K, G_FOX_Q, G_FOX_K, G_MEM_Q, G_MEM_K, G_FOX_BIAS = range(9)
K_COS, K_SIN, K_ROT, K_MASK, K_CMASK, K_HALF, K_SEL, K_PART = 0, T, 2 * T, 2 * T + P, 2 * T + 2 * P, 2 * T + 3 * P, 2 * T + 3 * P + 2, 2 * T + 3 * P + 10
CONST_COLS = K_PART + 3
F_ROW = 64
UNITS_LAYER = 8 + 27 + 12 + 36 + 8 + 2
UNITS_2 = 2 * UNITS_LAYER


class Later:

    def __init__(self):
        self.todo = []

    def add(self, delay, fn):
        self.todo.append([delay, fn])

    def tick(self):
        for item in self.todo:
            item[0] -= 1
        due = [item for item in self.todo if item[0] <= 0]
        self.todo = [item for item in self.todo if item[0] > 0]
        for _, fn in due:
            fn()

    def flush(self):
        while self.todo:
            self.tick()


class Epilogues:

    def __init__(self, c, ctx, k, pl):
        self.c, self.k, self.pl, self.rec, self.later = c, k, pl, Recent(c.prog), Later()
        self.sq = [c.sb(ctx, f"ep_sq{j}", [P, T], F32) for j in range(2)]
        self.vt = [c.sb(ctx, f"ep_vt{j}", [P, T], F32) for j in range(2)]
        self.rc = [c.sb(ctx, f"ep_rope{j}", [P, T], F32) for j in range(2)]
        self.nar = [[c.sb(ctx, f"ep_nar{s}{j}", [P, 2 * TT], F32) for j in range(3)] for s in range(2)]
        self.wide = c.sb(ctx, "ep_wide", [P, T], F32)
        self.n_norm = self.n_vt = 0

    def norm(self, raw, dst, n, heads, gain, width, ready, rope):
        c, rec, s = self.c, self.rec, self.n_norm % 2
        self.n_norm += 1
        tiles, sq = n // P, self.sq[s]
        nar = [a[:, 0:tiles * heads] for a in self.nar[s]]
        c.wait(c.act, *ready)
        copied = c.A(dst, raw, ACT.Copy)
        c.wait(c.act, rec.get(f"sq{s}"))
        squared = c.A(sq[:, 0:n], raw, ACT.Square)
        state = {}

        def sums():
            c.wait(c.pe, squared, rec.get("ss_free"))
            ss = c.bank[7]
            rhs = self.k[:, K_HALF:K_HALF + 2] if heads == 2 else c.ones[:, 0:1]
            for t in range(tiles):
                m = c.mm(ss[:, t * heads:(t + 1) * heads], sq[:, t * P:t * P + P], rhs, start=t == 0, stop=True,
                         done=t == tiles - 1, skip_group_check=True)
            rec.keep(f"sq{s}", m)
            c.wait(c.dve, rec.get(f"nar{s}"))
            state["r"] = c.rsqrt(nar[0], ss[:, 0:tiles * heads], (nar[1], nar[2]), 1.0 / width, [m])
            rec.keep("ss_free", state["r"])
            if heads == 2:
                state["r"] = self.widen(nar[0], P, tiles)

        def spread():
            b = c.bank[6]
            c.wait(c.pe, state["r"], rec.get("r_free"))
            for t in range(tiles):
                r = self.wide[:, t * P:t * P + P] if heads == 2 else nar[0][:, t:t + 1].to_broadcast([P, P])
                m = c.mm(b[:, t * P:t * P + P], r, c.ident[:, :], is_transpose=True, done=t == tiles - 1)
            rec.keep(f"nar{s}", m)
            rec.keep("wide_free", m)
            c.wait(c.dve, m, copied)
            state["f"] = rec.keep("r_free", c.stt(dst, dst, gain, b[:, 0:n], ALU.mult, ALU.mult))

        self.later.add(1, sums)
        self.later.add(2, spread)
        if rope:
            self.later.add(3, lambda: self.rope(dst, state["f"]))
        return squared

    def widen(self, r, tokens, tiles):
        c = self.c
        c.wait(c.dve, c.prog.now(c.t_dve), self.rec.get("wide_free"))
        out = self.wide[0:tokens, 0:tiles * P].rearrange("p (h d) -> p h d", d=HD)
        return c.copy(out, r.unsqueeze(2).to_broadcast([tokens, 2 * tiles, HD]))

    def rope(self, dst, ready):
        c, rec = self.c, self.rec
        b = c.bank[5]
        c.wait(c.pe, ready, rec.get("rot_free"))
        m = c.mm(b[:, :], self.k[:, K_ROT:K_ROT + P], dst)
        c.wait(c.dve, m, ready, rec.get("roped"))
        u = c.tt(self.rc[0][:, :], dst, self.k[:, K_COS:K_COS + T], ALU.mult)
        w = rec.keep("rot_free", c.tt(self.rc[1][:, :], b[:, :], self.k[:, K_SIN:K_SIN + T], ALU.mult))
        c.wait(c.dve, w)
        return rec.keep("roped", c.tt(dst, self.rc[0][:, :], self.rc[1][:, :], ALU.add))

    def rows(self, raw, dst, n, ready):
        c, rec, s = self.c, self.rec, self.n_vt % 2
        self.n_vt += 1
        vt, tiles = self.vt[s], n // P
        c.wait(c.dve, *ready, rec.get(f"vt{s}"))
        copied = c.copy(vt[:, 0:n], raw)

        def turn():
            b = c.bank[4]
            c.wait(c.pe, copied, rec.get("rows_free"))
            for t in range(tiles):
                m = c.mm(b[:, t * P:t * P + P], vt[:, t * P:t * P + P], c.ident[:, :], is_transpose=True, done=t == tiles - 1)
            rec.keep(f"vt{s}", m)
            c.wait(c.act, m)
            rec.keep("rows_free", c.A(dst, b[:, 0:n].rearrange("p (t n) -> p t n", n=P), ACT.Copy))

        self.later.add(1, turn)
        return copied


def forget_rows(c, raw_f, base, rhs, k, w, parts, ready):
    lo, hi = slice(F_ROW, P), slice(F_ROW + 32, P)
    top = slice(F_ROW, F_ROW + 32)
    m = log_sigmoid(c, raw_f[lo, :], raw_f[lo, :], [a[lo, :] for a in w], ready)
    c.wait(c.dve, m)
    m = c.V(c.dve.memset, w[0][lo, :], 1.0)
    c.wait(c.dve, m)
    m = c.V(c.dve.tensor_tensor_scan, w[1][lo, :], w[0][lo, :], raw_f[lo, :], 0.0, ALU.mult, ALU.add)
    c.wait(c.dve, m)
    rest = w[1]
    m = c.ts(rest[lo, :], rest[lo, :], 8.0, ALU.mult)
    for j in range(3):
        c.wait(c.dve, m)
        m = c.copy(parts[j][lo, :], rest[lo, :])
        c.wait(c.dve, m)
        if j < 2:
            m = c.tt(rest[lo, :], rest[lo, :], parts[j][lo, :], ALU.subtract)
    acc = w[2]
    m = c.ts(acc[lo, :], parts[0][lo, :], k[lo, K_PART:K_PART + 1], ALU.mult)
    for j in (1, 2):
        c.wait(c.dve, m)
        m = c.stt(acc[lo, :], parts[j][lo, :], k[lo, K_PART + j:K_PART + j + 1], acc[lo, :], ALU.mult, ALU.add)
    c.wait(c.dve, m)
    c.ts(rhs[top, :], acc[top, :], -1.0, ALU.mult)
    return c.copy(base[hi, :], acc[hi, :])


def compress(c, src, pe, w1, xw, hid, rec, tag, ready, loaded):
    c.wait(c.dve, *ready, rec.get("xw_free"))
    for g in range(2):
        rows = slice(g * HD, (g + 1) * HD)
        for half in range(2):
            x = src[rows, half * CMP_S:half * CMP_S + NC * CMP_S].rearrange("p (n l) -> p l n", l=CMP_S)
            e = pe[rows, half * CMP_S:(half + 1) * CMP_S].unsqueeze(2).to_broadcast([HD, CMP_S, NC])
            m = c.tt(xw[rows, half * CMP_S:(half + 1) * CMP_S, g * NC:(g + 1) * NC], x, e, ALU.add)
    b = c.bank[3]
    c.wait(c.pe, m, loaded, rec.get("cmp_bank"))
    for l in range(CMP_L):
        m = c.mm(b[:, 0:2 * NC], w1[:, l * P:l * P + P], xw[:, l, :], start=l == 0, stop=l == CMP_L - 1, done=l == CMP_L - 1)
    rec.keep("xw_free", m)
    c.wait(c.act, m, rec.get("hid_free"))
    return rec.keep("cmp_bank", c.A(hid[:, :], b[:, 0:2 * NC], ACT.Silu))


class Attention:
    S, ST, PT = 3, 6, 3

    def __init__(self, c, ctx):
        self.c, self.rec = c, Recent(c.prog)
        self.p = [c.sb(ctx, f"at_p{j}", [P, T], F32) for j in range(self.S)]
        self.pt = [c.sb(ctx, f"at_pt{j}", [P, T], F32) for j in range(self.PT)]
        self.st = [c.sb(ctx, f"at_st{j}", [P, 6], F32) for j in range(self.ST)]
        self.tasks = []

    def task(self, add_logits, n, scale, values, width, finish, ready, gate=None, may_be_empty=False):
        self.tasks.append((n, values, width, finish, gate, may_be_empty))
        self.step(len(self.tasks) - 1, add_logits, scale, ready)

    def step(self, now, add_logits=None, scale=None, ready=()):
        def has(task):
            return 0 <= task < len(self.tasks)
        if has(now):
            maximum = self.logits(now, add_logits, ready)
        if has(now - 1):
            m = self.divisor(now - 1)
        if has(now - 2):
            self.transposed(now - 2)
        if has(now):
            self.exponentials(now, scale, maximum)
        if has(now - 1):
            self.factor(now - 1, m)
        if has(now - 5):
            self.store(now - 5)
        if has(now - 4):
            self.output(now - 4)

    def drain(self):
        n = len(self.tasks)
        for now in range(n, n + 5):
            self.step(now)
        assert n % self.ST == 0
        self.tasks = []

    def logits(self, task, add_logits, ready):
        c, rec, s, t, n = self.c, self.rec, task % self.S, task % self.ST, self.tasks[task][0]
        b = c.bank[s]
        c.wait(c.pe, rec.get(f"exp{s}"), *ready)
        m = add_logits(b)
        c.wait(c.dve, m, rec.get(f"stored{t}"))
        return c.V(c.dve.reduce_max, self.st[t][:, 0:1], b[:, 0:n], AX_X)

    def exponentials(self, task, scale, maximum):
        c, rec, s, t, n = self.c, self.rec, task % self.S, task % self.ST, self.tasks[task][0]
        st = self.st[t]
        c.wait(c.dve, maximum)
        m = c.ts(st[:, 1:2], st[:, 0:1], -1.0e29, ALU.max, -scale, ALU.mult)
        c.wait(c.act, m, rec.get(f"p{s}"))
        e = c.A(self.p[s][:, 0:n], c.bank[s][:, 0:n], ACT.Exp, scale=scale, bias=st[:, 1:2], accum_out=st[:, 2:3])
        rec.keep(f"exp{s}", rec.keep(f"sum{t}", e))

    def divisor(self, task):
        c, t = self.c, task % self.ST
        st = self.st[t]
        c.wait(c.dve, self.rec.get(f"sum{t}"))
        if self.tasks[task][5]:
            return c.ts(st[:, 3:4], st[:, 2:3], 0.5, ALU.max)
        return c.V(c.dve.reciprocal, st[:, 4:5], st[:, 2:3])

    def factor(self, task, m):
        c, t, gate = self.c, task % self.ST, self.tasks[task][4]
        st = self.st[t]
        if self.tasks[task][5]:
            c.wait(c.dve, m)
            m = c.V(c.dve.reciprocal, st[:, 4:5], st[:, 3:4])
        if gate is not None:
            c.wait(c.dve, m)
            m = c.ts(st[:, 5:6], st[:, 4:5], gate, ALU.mult)
        self.rec.keep(f"factor{t}", m)

    def transposed(self, task):
        c, rec, s, u, v, n = self.c, self.rec, task % self.S, task % 2, task % self.PT, self.tasks[task][0]
        b, rows, tiles = c.bank[3 + u], min(n, P), (n + P - 1) // P
        c.wait(c.pe, rec.get(f"exp{s}"), rec.get(f"turned{u}"))
        for j in range(tiles):
            m = c.mm(b[0:rows, j * P:j * P + P], self.p[s][:, j * P:j * P + rows], c.ident[:, :], is_transpose=True, done=j == tiles - 1)
        rec.keep(f"p{s}", m)
        c.wait(c.act, m, rec.get(f"pv{v}"))
        e = c.A(self.pt[v][0:rows, 0:tiles * P], b[0:rows, 0:tiles * P], ACT.Copy)
        rec.keep(f"turned{u}", rec.keep(f"pt{v}", e))

    def output(self, task):
        c, rec, u, v, n = self.c, self.rec, task % 2, task % self.PT, self.tasks[task][0]
        values, width = self.tasks[task][1:3]
        o, rows, last = c.bank[5 + u][:, 0:width], min(n, P), len(values) - 1
        c.wait(c.pe, rec.get(f"pt{v}"), rec.get(f"o{u}"))
        for j, keys in enumerate(values):
            m = c.mm(o, self.pt[v][0:rows, j * P:j * P + P], keys, start=j == 0, stop=j == last, done=j == last)
        rec.keep(f"out{u}", rec.keep(f"pv{v}", m))

    def store(self, task):
        c, rec, u, t = self.c, self.rec, task % 2, task % self.ST
        width, finish, gate = self.tasks[task][2:5]
        c.wait(c.dve, rec.get(f"out{u}"), rec.get(f"factor{t}"))
        factor = self.st[t][:, 4:5] if gate is None else self.st[t][:, 5:6]
        rec.keep(f"o{u}", rec.keep(f"stored{t}", finish(c.bank[5 + u][:, 0:width], factor)))


def block_two(c, t, x_ready, narrow):
    prog = c.prog
    with ExitStack() as ctx:
        k = c.sb(ctx, "consts", [P, CONST_COLS], F32)
        identb = c.sb(ctx, "ident_bf", [P, P], BF16)
        maskb = c.sb(ctx, "mask_bf", [P, 2 * P], BF16)
        c.fence()
        m = c.load(k[:, :], t["consts"])
        c.wait(c.dve, m)
        c.copy(identb[:, :], c.ident[:, :])
        c.copy(maskb[:, :], k[:, K_MASK:K_MASK + 2 * P])
        c.wait(c.act, *[m for r in x_ready for m in r])
        c.fence()
        prog.loop(2, lambda layer: layer_two(c, t, layer, k, identb, maskb, narrow))
        return [[prog.now(c.t_dve)]]


def layer_two(c, t, layer, k, identb, maskb, narrow):
    prog = c.prog
    with ExitStack() as ctx:
        pl = c.sb(ctx, "layer_cols", [P, LAYER_COLS], F32)
        hi = c.sb(ctx, "z_hi", [P, DC, T], F32R)
        lo = c.sb(ctx, "z_lo", [P, DC, T], F32R)
        o_all = c.sb(ctx, "o_all", [P, 12, T], F32)
        c.fence()
        loaded = c.load(pl[:, :], at_row(t["layer_cols"], layer))
        for eng in (c.act, c.dve):
            c.wait(eng, loaded)
        with ExitStack() as att:
            b = {n: c.sb(att, n, [P, w, T], F32) for n, w in (("nsa_q", 4), ("fox_q", 4), ("fox_k", 4), ("mem_q", 4))}
            b["sel_k"], b["win_k"] = (c.sb(att, n, [P, T], F32) for n in ("sel_k", "win_k"))
            b["sel_v"], b["win_v"] = (c.sb(att, n, [P, TT, P], F32) for n in ("sel_v", "win_v"))
            b["fox_v"] = c.sb(att, "fox_v", [P, TT, T], F32)
            b["mem_k"] = c.sb(att, "mem_k", [P, 4, M], F32)
            b["mem_v"] = c.sb(att, "mem_v", [P, MT, T], F32)
            b["cmp_k"] = c.sb(att, "cmp_k", [P, NC], F32)
            b["cmp_v"] = c.sb(att, "cmp_v", [NC, P], F32)
            b["gate"] = c.sb(att, "gate_rows", [P, TT, 32], F32)
            b["fox_base"] = c.sb(att, "fox_base", [P, T], BF16)
            b["fox_rhs"] = c.sb(att, "fox_rhs", [P, T], BF16)
            memory_keys(c, t, k, pl, b, hi, lo, narrow)
            projections(c, t, layer, k, pl, b, hi, lo, o_all, narrow)
            attend_all(c, k, identb, maskb, b, o_all)
            c.fence()
        oh = c.sb(ctx, "oz_hi", [P, 12, T], F32R)
        ol = c.sb(ctx, "oz_lo", [P, 12, T], F32R)
        silu_gates(c, hi, lo, o_all, oh, ol)
        merge_and_out(c, hi, lo, oh, ol, [o_all[:, j, :] for j in range(6)])
        c.fence()


def at_row(ap, n):
    return ap[bass.ds(n, 1)].rearrange("a p n -> (a p) n")


def memory_keys(c, t, k, pl, b, hi, lo, narrow):
    with ExitStack() as ctx:
        mem = c.sb(ctx, "mem_in", [P, DC, M], F32)
        mh, ml = hi[:, :, 0:M], lo[:, :, 0:M]
        ep = Epilogues(c, ctx, k, pl)
        c.fence()
        m = c.load(mem[:, :, :].rearrange("p a b -> p (a b)"), t["mem"])
        ready = pre_norm(c, mem, pl[:, C_MEMNORM:C_MEMNORM + DC], mh, ml, MT, ep.sq, ep.vt, narrow, [[m]] * DC)
        c.wait(c.dve, m)
        c.wait(c.pe, *ready)
        c.fence()
        rec = ep.rec
        for n in range(8):
            bank = c.bank[n % 3]
            c.wait(c.pe, rec.get(f"bank{n % 3}"))
            m = c.project(bank[:, 0:M], mh, ml)
            ep.later.tick()
            if n < 4:
                f = ep.norm(bank[:, 0:M], b["mem_k"][:, n, :], M, 1, pl[:, C_GAINS + G_MEM_K:C_GAINS + G_MEM_K + 1], P, [m], False)
            else:
                f = ep.rows(bank[:, 0:M], b["mem_v"][:, :, (n - 4) * P:(n - 3) * P], M, [m])
            rec.keep(f"bank{n % 3}", f)
        ep.later.flush()
        c.fence()


def projections(c, t, layer, k, pl, b, hi, lo, spare, narrow):
    def gain(g):
        return pl[:, C_GAINS + g:C_GAINS + g + 1]

    with ExitStack() as ctx:
        ep = Epilogues(c, ctx, k, pl)
        rec = ep.rec
        kc = [c.sb(ctx, n, [P, T], F32) for n in ("cmp_src_k", "cmp_src_v")]
        gs = c.sb(ctx, "gate_cols", [P, T], F32)
        fr = c.sb(ctx, "forget", [P, T], F32)
        spare = spare[:, :, :].rearrange("p a b -> p (a b)")
        w1 = spare[:, 0:CMP_L * P]
        xw = spare[:, CMP_L * P:CMP_L * (P + 2 * NC)].rearrange("p (l n) -> p l n", l=CMP_L)
        hid = c.sb(ctx, "cmp_hidden", [P, 2 * NC], F32)
        parts = [c.sb(ctx, f"fox_part{j}", [P, T], BF16) for j in range(3)]
        fw = [ep.rc[0], ep.rc[1], gs]
        c.fence()
        w1_ready = c.load(w1, at_row(t["cmp_w1"], layer * 2))
        c.V(c.dve.memset, gs[:, :], 0.0)
        c.V(c.dve.memset, xw[:, :, :], 0.0)
        c.V(c.dve.memset, b["fox_base"][:, :], 0.0)
        c.V(c.dve.memset, b["fox_rhs"][:, :], 0.0)
        zero = c.V(c.dve.memset, b["cmp_k"][:, :], 0.0)
        c.wait(c.dve, zero)
        c.V(c.dve.memset, b["fox_base"][F_ROW:F_ROW + 32, :], 1.0)
        c.V(c.dve.memset, b["fox_rhs"][F_ROW + 32:P, :], 1.0)
        ready = pre_norm(c, c.x, pl[:, C_NORM:C_NORM + DC], hi, lo, TT, ep.sq, ep.vt, narrow, [[]] * DC)
        c.wait(c.pe, *ready)
        c.fence()
        state = {}

        def unit(n, epilogue):
            bank = c.bank[n % 3]
            c.wait(c.pe, rec.get(f"bank{n % 3}"))
            m = c.project(bank[:, :], hi, lo)
            ep.later.tick()
            rec.keep(f"bank{n % 3}", epilogue(bank, m))

        def normed(dst, g, rope, heads=2):
            return lambda bank, m: ep.norm(bank[:, :], dst, T, heads, gain(g), P // heads, [m], rope)

        def rows(dst):
            return lambda bank, m: ep.rows(bank[:, :], dst, T, [m])

        def cmp_key(bank, m):
            c.wait(c.act, m)
            e = c.A(kc[0][:, :], bank[:, :], ACT.Copy)

            def roped():
                state["kc"] = ep.rope(kc[0][:, :], e)
            ep.later.add(1, roped)
            return e

        def cmp_value(bank, m):
            c.wait(c.act, m)
            state["vc"] = c.A(kc[1][:, :], bank[:, :], ACT.Copy)
            return state["vc"]

        def gates(bank, m):
            c.wait(c.act, m)
            e = c.A(gs[0:32, :], bank[0:32, :], ACT.Sigmoid)
            state["f"] = c.A(fr[F_ROW:P, :], bank[F_ROW:P, :], ACT.Identity, bias=pl[F_ROW:P, C_GAINS + G_FOX_BIAS:C_GAINS + G_FOX_BIAS + 1])

            def turn():
                rb = c.bank[3]
                c.wait(c.pe, e)
                for tt in range(TT):
                    m = c.mm(rb[:, tt * P:tt * P + P], gs[:, tt * P:tt * P + P], c.ident[:, :], is_transpose=True, done=tt == TT - 1)
                c.wait(c.dve, m)
                rec.keep("cmp_bank", c.copy(b["gate"][:, :, :], rb[:, :].rearrange("p (t n) -> p t n", n=P)[:, :, 0:32]))
            ep.later.add(1, turn)
            return state["f"]

        unit(0, cmp_key)
        unit(1, cmp_value)
        unit(2, gates)
        for n in range(4):
            unit(3 + n, normed(b["nsa_q"][:, n, :], G_NSA_Q, True))
        unit(7, normed(b["sel_k"][:, :], G_SEL_K, True))
        unit(8, normed(b["win_k"][:, :], G_WIN_K, True))
        unit(9, rows(b["sel_v"][:, :, :]))
        unit(10, rows(b["win_v"][:, :, :]))
        w2 = pl[:, C_W2:C_W2 + P + HD]
        e = compress(c, kc[0], pl[:, C_PE:C_PE + CMP_L], w1, xw, hid, rec, "k", [state["kc"]], w1_ready)
        cb = c.bank[3]
        c.wait(c.act, rec.get("xw_free"))
        w1_ready = c.load(w1, at_row(t["cmp_w1"], layer * 2 + 1))
        c.wait(c.pe, e)
        m = rec.keep("hid_free", c.mm(cb[:, 0:2 * NC], w2[:, 0:P], hid[:, :]))
        c.wait(c.act, m, rec.get("sq0"))
        for g in range(2):
            rws = slice(g * HD, (g + 1) * HD)
            c.A(b["cmp_k"][rws, :], cb[rws, g * NC:(g + 1) * NC], ACT.Copy)
            e = rec.keep("cmp_bank", c.A(ep.sq[0][rws, 0:NC], cb[rws, g * NC:(g + 1) * NC], ACT.Square))
        c.wait(c.pe, e, rec.get("ss_free"))
        m = c.mm(c.bank[7][0:NC, 0:2], ep.sq[0][:, 0:NC], k[:, K_HALF:K_HALF + 2])
        rec.keep("sq0", m)
        nar = [a[0:NC, 0:2] for a in ep.nar[0]]
        c.wait(c.dve, rec.get("nar0"))
        r = rec.keep("ss_free", c.rsqrt(nar[0], c.bank[7][0:NC, 0:2], (nar[1], nar[2]), 1.0 / HD, [m]))
        r = ep.widen(nar[0], NC, 1)
        c.wait(c.pe, r, rec.get("r_free"))
        prog_settle(c)
        m = c.mm(c.bank[6][:, 0:NC], ep.wide[0:NC, 0:P], c.ident[0:NC, 0:NC], is_transpose=True)
        rec.keep("nar0", m)
        rec.keep("wide_free", m)
        c.wait(c.dve, m, e)
        rec.keep("r_free", c.stt(b["cmp_k"][:, :], b["cmp_k"][:, :], gain(G_CMP_K), c.bank[6][:, 0:NC], ALU.mult, ALU.mult))
        e = compress(c, kc[1], pl[:, C_PE + CMP_L:C_PE + 2 * CMP_L], w1, xw, hid, rec, "v", [state["vc"]], w1_ready)
        c.wait(c.pe, e)
        for g in range(2):
            m = c.mm(cb[0:NC, g * HD:(g + 1) * HD], hid[:, g * NC:(g + 1) * NC], w2[:, P:P + HD], done=g == 1)
        c.wait(c.act, m)
        rec.keep("cmp_bank", c.A(b["cmp_v"][:, :], cb[0:NC, 0:P], ACT.Copy))
        for n in range(4):
            unit(11 + n, normed(b["mem_q"][:, n, :], G_MEM_Q, False, 1))
        for n in range(4):
            unit(15 + 3 * n, normed(b["fox_q"][:, n, :], G_FOX_Q, False))
            unit(16 + 3 * n, normed(b["fox_k"][:, n, :], G_FOX_K, False))
            unit(17 + 3 * n, rows(b["fox_v"][:, :, n * P:(n + 1) * P]))
        ep.later.flush()
        c.fence()
        forget_rows(c, fr, b["fox_base"], b["fox_rhs"], k, fw, parts, [state["f"]])
        c.fence()


def attend_all(c, k, identb, maskb, b, o_all):
    with ExitStack() as ctx:
        at_ = Attention(c, ctx)
        rec = at_.rec
        nq = [c.sb(ctx, f"nsa_q_half{j}", [P, T], F32) for j in range(2)]
        fq = [c.sb(ctx, f"fox_q_half{j}", [P, T], F32) for j in range(2)]
        mq = c.sb(ctx, "mem_q_now", [P, T], F32)
        fb = [c.sb(ctx, f"fox_base_head{j}", [P, T], BF16) for j in range(2)]
        sel = c.sb(ctx, "sel_now", [P, 2], F32)
        gt = c.sb(ctx, "gate_now", [P, TT, 2, 3], F32)
        rows = [c.sb(ctx, f"o_rows{j}", [P, TT, P], F32) for j in range(3)]
        c.fence()
        for buf in (*nq, *fq):
            c.V(c.dve.memset, buf[:, :], 0.0)
        c.fence()

        def chunk(n):
            rec.marks = {}
            rec.looped = True
            c.wait(c.dve, rec.get("staged_used"), rec.get("rows_out"), prog_now(c))
            c.wait(c.act, rec.get("staged_used"), rec.get("rows_out"))
            for j in range(2):
                h = slice(j * HD, (j + 1) * HD)
                c.copy(nq[j][h, :], b["nsa_q"][h, bass.ds(n, 1), :].rearrange("p a n -> p (a n)"))
                c.A(fq[j][h, :], b["fox_q"][h, bass.ds(n, 1), :].rearrange("p a n -> p (a n)"), ACT.Copy)
                c.copy(gt[:, :, j, :], b["gate"][:, :, bass.ds(3 * n + 12 * j, 3)])
            a = c.A(mq[:, :], at(b["mem_q"], n), ACT.Copy)
            d = c.copy(sel[:, :], k[:, bass.ds(K_SEL + 2 * n, 2)])
            c.wait(c.dve, d)
            for j in range(2):
                d = c.ts(fb[j][:, :], b["fox_base"][:, :], sel[:, j:j + 1], ALU.mult)
            staged = [a, d]
            for i in range(TT):
                q, keys, last = slice(i * P, i * P + P), (i + 1) * P, slice(i * P, (i + 1) * P)
                for j in range(2):
                    out = rows[0][:, i, j * HD:(j + 1) * HD]

                    def first(o, factor, out=out):
                        return rec.keep("nsa_row", c.ts(out, o, factor, ALU.mult))

                    def further(o, factor, out=out):
                        c.wait(c.dve, rec.get("nsa_row"))
                        return rec.keep("nsa_row", c.stt(out, o, factor, out, ALU.mult, ALU.add))

                    def cmp_logits(bank, i=i, j=j, q=q):
                        c.mm(bank[:, 0:NC], nq[j][:, q], b["cmp_k"][:, :], stop=False, done=False)
                        return c.mm(bank[:, 0:NC], identb[:, :], maskb[:, P + 32 * i:P + 32 * i + NC], start=False)

                    at_.task(cmp_logits, NC, HD ** -0.5, [b["cmp_v"][:, j * HD:(j + 1) * HD]], HD, first, staged,
                             gate=gt[:, i, j, 0:1], may_be_empty=True)
                    for which, (kk, vv) in enumerate((("sel_k", "sel_v"), ("win_k", "win_v")), 1):
                        def logits(bank, j=j, q=q, keys=keys, last=last, kk=kk):
                            c.mm(bank[:, 0:keys], nq[j][:, q], b[kk][:, 0:keys], stop=False, done=False)
                            return c.mm(bank[:, last], identb[:, :], maskb[:, 0:P], start=False)
                        at_.task(logits, keys, HD ** -0.5, [b[vv][:, s, j * HD:(j + 1) * HD] for s in range(i + 1)], HD, further, [],
                                 gate=gt[:, i, j, which:which + 1])
                for j in range(2):
                    def fox_logits(bank, j=j, q=q, keys=keys, last=last):
                        c.mm(bank[:, 0:keys], fq[j][:, q], b["fox_k"][:, bass.ds(n, 1), 0:keys].rearrange("p a n -> p (a n)"), stop=False, done=False)
                        c.mm(bank[:, 0:keys], fb[j][:, q], b["fox_rhs"][:, 0:keys], start=False, stop=False, done=False)
                        return c.mm(bank[:, last], identb[:, :], maskb[:, 0:P], start=False)

                    def fox_out(o, factor, out=rows[1][:, i, j * HD:(j + 1) * HD]):
                        return c.ts(out, o, factor, ALU.mult)
                    at_.task(fox_logits, keys, HD ** -0.5, [b["fox_v"][:, s, bass.ds(n * P + j * HD, HD)] for s in range(i + 1)], HD, fox_out, [])

                def mem_logits(bank, q=q):
                    return c.mm(bank[:, 0:M], mq[:, q], b["mem_k"][:, bass.ds(n, 1), :].rearrange("p a n -> p (a n)"))

                def mem_out(o, factor, out=rows[2][:, i, :]):
                    return c.ts(out, o, factor, ALU.mult)
                at_.task(mem_logits, M, P ** -0.5, [b["mem_v"][:, s, bass.ds(n * P, P)] for s in range(MT)], P, mem_out, [])
            at_.drain()
            rec.keep("staged_used", c.prog.now(c.t_pe))
            for j in range(3):
                bank = c.bank[(7, 3)[j % 2]]
                c.wait(c.pe, prog_now(c), rec.get(f"back{j % 2}"))
                for i in range(TT):
                    m = c.mm(bank[:, i * P:i * P + P], rows[j][:, i, :], c.ident[:, :], is_transpose=True, done=i == TT - 1)
                c.wait(c.act, m)
                rec.keep(f"back{j % 2}", c.A(at(o_all, n + 4 * j), bank[:, :], ACT.Copy))
            rec.keep("rows_out", m)
            rec.looped = False

        c.prog.loop(4, chunk)


def prog_settle(c):
    c.prog.settle(c.pe)


def prog_now(c):
    return c.prog.now(c.t_dve)


def silu_gates(c, hi, lo, o_all, oh, ol):
    with ExitStack() as ctx:
        s = [c.sb(ctx, f"silu{j}", [P, T], F32) for j in range(3)]
        c.fence()
        rec = Recent(c.prog)

        def chunk(n, j):
            c.wait(c.pe, rec.get(f"silu{j}"))
            m = c.project(c.bank[j][:, :], hi, lo)
            c.wait(c.act, m, rec.get(f"lo{j}"))
            e = rec.keep(f"silu{j}", c.A(s[j][:, :], c.bank[j][:, :], ACT.Silu))
            c.wait(c.dve, e)
            d = c.tt(s[j][:, :], s[j][:, :], at(o_all, n), ALU.mult)
            c.wait(c.act, d)
            e = c.A(at(oh, n), s[j][:, :], ACT.Copy)
            c.wait(c.dve, e)
            rec.keep(f"lo{j}", c.tt(at(ol, n), s[j][:, :], at(oh, n).bitcast(F32), ALU.subtract))

        rec.over(12, 3, chunk)
        c.fence()


def merge_and_out(c, hi, lo, oh, ol, g):
    with ExitStack() as ctx:
        uh = c.sb(ctx, "u_hi", [P, DC, T], F32R)
        ul = c.sb(ctx, "u_lo", [P, DC, T], F32R)
        c.fence()
        rec = Recent(c.prog)

        def two(i):
            rec.marks = {}
            rec.looped = True
            for j in range(6):
                c.wait(c.pe, rec.get(f"bank{j}"))
                m = c.project(c.bank[j][:, :], hi, lo)
                c.wait(c.act, m, rec.get(f"g{j}"))
                rec.keep(f"bank{j}", rec.keep(f"sig{j}", c.A(g[j], c.bank[j][:, :], ACT.Sigmoid)))
            for br in range(3):
                banks = [c.bank[(6 + 2 * br + e) % 8] for e in range(2)]
                names = [f"bank{(6 + 2 * br + e) % 8}" for e in range(2)]
                c.wait(c.pe, *[rec.get(n) for n in names])
                m = c.unit([(banks[e][:, :], [(4 * e + q, oh[:, 4 * br + q, :], ol[:, 4 * br + q, :]) for q in range(4)], True, True)
                            for e in range(2)])
                for e in range(2):
                    j = 3 * e + br
                    c.wait(c.dve, m, rec.get(f"sig{j}"))
                    d = rec.keep(names[e], c.tt(g[j], g[j], banks[e][:, :], ALU.mult))
                    if br:
                        c.wait(c.dve, d, rec.get(f"sum{e}"))
                        d = c.tt(g[3 * e], g[3 * e], g[j], ALU.add)
                        if br == 1:
                            rec.keep(f"g{j}", d)
                        else:
                            rec.keep(f"g{j}", d)
                    rec.keep(f"sum{e}", d)
            for e in range(2):
                c.wait(c.act, rec.get(f"sum{e}"))
                a = c.A(at(uh, 2 * i + e), g[3 * e], ACT.Copy)
                c.wait(c.dve, a)
                rec.keep(f"g{3 * e}", c.tt(at(ul, 2 * i + e), g[3 * e], at(uh, 2 * i + e).bitcast(F32), ALU.subtract))
            rec.looped = False

        c.prog.loop(4, two)
        c.fence()
        rec = Recent(c.prog)

        def out(n, j):
            c.wait(c.pe, rec.get(f"bank{j}"))
            m = c.project(c.bank[j][:, :], uh, ul)
            c.wait(c.dve, m)
            rec.keep(f"bank{j}", c.tt(at(c.x, n), at(c.x, n), c.bank[j][:, :], ALU.add))

        rec.over(DC, 3, out)
        for j in range(2):
            c.wait(c.pe, rec.get(f"bank{j}"))
            m = c.unit([(c.bank[j][:, 0:HD], [(0, uh[:, 0, 0:HD], ul[:, 0, 0:HD])], True, True)])
        c.fence()


def _bucket(dist):
    half = 16
    d = np.maximum(dist, 1).astype(np.float64)
    large = half + (np.log(d / half) / np.log(2048 / half) * half).astype(np.int32)
    return np.where(dist < half, dist, np.minimum(large, 31)).astype(np.int32)


def _bias_rows(rel_bias):
    u = np.arange(P)
    out = np.empty((HEADS, P, DIL * T + 2 * P), np.float32)

    def put(lo, m, valid, dil, g):
        rows = rel_bias[_bucket(np.clip(m, 0, P) * dil)]
        for h in range(HEADS):
            out[h, :, lo:lo + m.shape[1]] = np.where(valid, rows[:, :, g * HEADS + h], np.float32(NEG))

    for r in range(DIL):
        m = (DIL * u + r)[:, None] - np.arange(T)[None, :]
        put(r * T, m, (m >= 0) & (m <= P), 1, 0)
    m = u[:, None] - u[None, :]
    put(DIL * T, m, m >= 0, 4, 1)
    put(DIL * T + P, m // 4, (m >= 0) & (m % 4 == 0), 16, 2)
    return out


def _cols(v):
    return np.ascontiguousarray(v.reshape(-1, P).T)


def _units(w):
    k, n = w.shape
    w = w.reshape(k // D, DC, P, n // P, P)
    return w.transpose(3, 0, 2, 1, 4).reshape(n // P * (k // D), P, D)


def _feature_major(x):
    return np.ascontiguousarray(x.T.reshape(DC, P, x.shape[0]).transpose(1, 0, 2).reshape(P, -1))


def _layout_one(i):
    f = {k: np.asarray(v) for k, v in i.items()}
    qkv = _units(f["attn_w_qkv"][0]).reshape(GROUPS, 3, HEADS, P, D)
    order = [(2, 0), (2, 1), (2, 2), (0, 0), (1, 0), (0, 1), (1, 1), (0, 2), (1, 2)]
    parts = [qkv[g, kind, h][None] for h in range(HEADS) for kind, g in order]
    parts.append(_units(f["attn_w_o"][0]))

    def ffn(layer):
        up = _units(f["ffn_w_up"][layer])
        return [up.reshape(2, FC, P, D).transpose(1, 0, 2, 3).reshape(2 * FC, P, D), _units(f["ffn_w_down"][layer])]

    parts += ffn(0)
    w_in = _units(f["lru_w_in"][0])
    gates = np.stack([f["lru_ga_w"][0], f["lru_gx_w"][0]])
    gates = gates.reshape(2, 4, 2, P, 2, P).transpose(1, 3, 0, 4, 2, 5).reshape(4, P, D)
    parts += [w_in[:DC], gates, w_in[DC:], _units(f["lru_w_out"][0])]
    parts += ffn(1)
    norms = [f[k][layer] for k in ("norm_mix_pre", "norm_mix_post", "norm_ffn_pre", "norm_ffn_post") for layer in range(2)]
    lru = np.stack([_cols(v) for v in (*f["lru_conv_w"][0], f["lru_conv_b"][0], f["lru_ga_b"][0].reshape(-1),
                                       f["lru_gx_b"][0].reshape(-1), f["lru_lambda"][0])], axis=2).reshape(P, 64)
    taps = []
    for layer in range(2):
        four = np.stack([_cols(v) for v in (*f["ffn_conv_w"][layer], f["ffn_conv_b"][layer])], axis=2)
        taps.append(four.reshape(P, 2, FC, 4).transpose(0, 2, 1, 3).reshape(P, 8 * FC))
    return parts, {
        "x": _feature_major(f["x"][0]),
        "gains": np.concatenate([_cols(v) for v in norms], axis=1),
        "lru": np.concatenate([lru, np.zeros((P, 8), np.float32)], axis=1),
        "taps": np.concatenate(taps, axis=1),
        "bias": _bias_rows(f["rel_bias"]),
        "ident": np.eye(P, dtype=np.float32),
    }


def _layout_two(i):
    f = {k[:-2]: np.asarray(v) for k, v in i.items() if k.endswith("_2")}
    pair = np.concatenate([np.r_[n * HD:(n + 1) * HD, (n + 4) * HD:(n + 5) * HD] for n in range(4)])
    zero = np.zeros((D, 8), np.float32)
    parts, cols, w1 = [], [], []
    for layer in range(2):
        w = f["w_in"][layer]
        kv = _units(w[:, 512:1280])
        fr = np.concatenate([w[:, 3352:3360]] * 3 + [zero], axis=1)
        gate = np.concatenate([w[:, 1280:1304], zero, np.zeros((D, 32), np.float32), fr, fr], axis=1)
        fox = _units(w[:, 1816:3352]).reshape(3, 4, P, D).transpose(1, 0, 2, 3).reshape(12, P, D)
        merge = _units(w[:, 4896:7968]).reshape(3, DC, P, D)
        br = np.stack([f["w_branch_a"][layer][pair], f["w_branch_b"][layer], f["w_branch_m"][layer]])
        br = br.reshape(3, 4, P, 4, 2, P).transpose(3, 0, 2, 4, 1, 5).reshape(4, 3, P, D)
        both = [np.concatenate([merge[:, 2 * n], merge[:, 2 * n + 1], br[n]]) for n in range(4)]
        parts += [_units(f["w_mem_kv"][layer]), kv[0:2], _units(gate), _units(w[:, 0:512][:, pair]), kv[2:3], kv[4:5], kv[3:4],
                  kv[5:6], _units(w[:, 3872:4384]), fox, _units(w[:, 1304:1816][:, pair]), _units(w[:, 3360:3872]),
                  _units(w[:, 4384:4896]), *both, _units(f["w_out"][layer]), np.zeros((2, P, D), np.float32)]
        two = lambda v: np.concatenate([v, v], axis=0)
        fb = np.zeros(P, np.float32)
        for r in (64, 72, 80, 96, 104, 112):
            fb[r:r + 8] = f["fox_f_bias"][layer]
        one = [two(f["nsa_q_norm"][layer]), *[two(f["nsa_k_norm"][layer][j]) for j in range(3)], two(f["fox_q_norm"][layer]),
               two(f["fox_k_norm"][layer]), f["mem_q_norm"][layer], f["mem_k_norm"][layer], fb]
        cols.append(np.concatenate([
            _cols(f["norm_g"][layer]), _cols(f["mem_norm_g"][layer]), np.stack(one, axis=1),
            two(f["cmp_pe_k"][layer].T), two(f["cmp_pe_v"][layer].T),
            f["cmp_w2_k"][layer], f["cmp_w2_k"][layer], f["cmp_w2_v"][layer]], axis=1))
        for name in ("cmp_w1_k", "cmp_w1_v"):
            w1.append(two(f[name][layer].reshape(CMP_L, HD, P).transpose(1, 0, 2).reshape(HD, CMP_L * P)))
    half = HD // 2
    freq = (np.float32(10000.0) ** (-np.arange(half, dtype=np.float32) / half)).astype(np.float32)
    ang = (np.arange(T, dtype=np.float32)[None, :] * freq[:, None]).astype(np.float32)
    ang = np.concatenate([ang] * 4, axis=0)
    rot = np.zeros((P, P), np.float32)
    for m in range(P):
        if m % HD < half:
            rot[m + half, m] = -1.0
        else:
            rot[m - half, m] = 1.0
    a, b = np.arange(P)[:, None], np.arange(P)[None, :]
    mask = np.where(b > a, np.float32(NEG), np.float32(0))
    cmask = np.zeros((P, 4, 32), np.float32)
    for tile in range(4):
        end = np.arange(32) * CMP_S + CMP_L - 1
        cmask[:, tile] = np.where(end[None, :] <= tile * P + a, np.float32(0), np.float32(NEG))
    p = np.arange(P)
    halves = np.stack([p < HD, p >= HD], axis=1)
    inside = (p >= F_ROW) & (p % 32 < 24)
    sel = np.stack([inside & (p % 8 == h) for h in range(8)], axis=1)
    part = np.stack([inside & (p % 32 // 8 == j) for j in range(3)], axis=1)
    consts = np.concatenate([np.cos(ang), np.sin(ang), rot, mask, cmask.reshape(P, P), halves, sel, part], axis=1)
    return parts, {
        "mem": _feature_major(f["mem"][0]), "layer_cols": np.stack(cols), "cmp_w1": np.stack(w1),
        "consts": consts.astype(np.float32),
    }


def _layout(inputs):
    one, a = _layout_one(inputs)
    two, b = _layout_two(inputs)
    return {**a, **b, "units": np.concatenate(one + two)}


def kernel(**inputs):
    import concourse.bacc as bacc
    from concourse.bass_utils import run_bass_kernel_spmd

    arrays = _layout(inputs)
    nc = bacc.Bacc("TRN2", target_bir_lowering=False, num_devices=1, dynamic_dma_scratch_size=1024)
    t = {n: nc.dram_tensor("in_" + n, a.shape, mybir.dt.from_np(a.dtype), kind="ExternalInput").ap() for n, a in arrays.items()}
    out = nc.dram_tensor("out", (P, DC * T), F32, kind="ExternalOutput").ap()
    build(nc, t, out)
    r = run_bass_kernel_spmd(nc, [{"in_" + n: a for n, a in arrays.items()}], core_ids=[0])
    y = r.results[0]["out"].reshape(P, DC, T)
    return np.ascontiguousarray(y.transpose(2, 1, 0).reshape(1, T, D))
```

```python
from contextlib import ExitStack, contextmanager

import numpy as np
import concourse.bass as bass
from concourse import mybir

F32 = mybir.dt.float32
F32R = mybir.dt.float32r
BF16 = mybir.dt.bfloat16
I32 = mybir.dt.int32
ACT = mybir.ActivationFunctionType
ALU = mybir.AluOpType
AX_X = mybir.AxisListType.X

P = 128
T = 512
D = 1024
DC = D // P
TT = T // P
FC = 3 * D // P
NEG = -1.0e30
SLOTS = 3
EPS = 1e-6
CREDIT = 512

HEADS = 8
GROUPS = 3
DIL = 4
BIAS_W = T + 2 * P


class Tally:

    def __init__(self, sem, name, eng):
        self.sem, self.name, self.eng, self.n = sem, name, eng, 0


class Frame:

    def __init__(self, count):
        self.count, self.var, self.per, self.tags, self.closed = count, 0, {}, {}, False


class Mark:
    def __init__(self, tally, n, frames):
        self.tally, self.n, self.frames = tally, n, frames

    def fixed(self):
        return self.n + sum((f.count - 1) * f.per.get(self.tally, 0) for f in self.frames if f.closed)

    def moving(self):
        return [f for f in self.frames if not f.closed and f.per.get(self.tally, 0)]

    def value(self):
        v = self.fixed()
        for f in self.moving():
            v = v + f.var * f.per[self.tally]
        return v


class Program:

    def __init__(self, nc):
        self.nc, self.frames, self.tallies, self.counting = nc, [], [], False
        self.engines = (nc.tensor, nc.scalar, nc.vector)
        self.settled = {}
        self.waits = {}

    def tally(self, sem, name, eng):
        t = Tally(sem, name, eng)
        self.tallies.append(t)
        return t

    def op(self, tally, fn, *args, tag=None, **kw):
        if not self.counting:
            self.issue_waits(tally.eng)
            fn(*args, **kw).then_inc(tally.sem, 1)
        return self.step(tally, 1, tag)

    def step(self, tally, by, tag=None):
        tally.n += by
        m = Mark(tally, tally.n, list(self.frames))
        if tag is not None:
            self.frames[-1].tags[tag] = m
        return m

    def raw(self, eng, fn, *args, **kw):
        if not self.counting:
            self.issue_waits(eng)
            fn(*args, **kw)

    def wait(self, eng, *marks):
        if not self.counting:
            self.waits.setdefault(eng.engine, []).extend(m for m in marks if m is not None)

    def issue_waits(self, eng):
        latest = []
        for m in self.waits.pop(eng.engine, []):
            same = [k for k in latest if k.tally is m.tally and k.moving() == m.moving()]
            if not same:
                latest.append(m)
            elif m.fixed() > same[0].fixed():
                latest[latest.index(same[0])] = m
        for m in latest:
            eng.wait_ge(m.tally.sem, m.value())
        return bool(latest)

    def settle(self, eng):
        if not self.counting and self.issue_waits(eng):
            eng.sem_inc(self.settled[eng.engine], 1)

    def now(self, tally):
        return Mark(tally, tally.n, list(self.frames))

    def prev(self, tag):
        if self.counting:
            return None
        f = self.frames[-1]
        m = f.tags[tag]
        n = m.n - f.per[m.tally]
        assert n >= 1, f"{tag}: a wait below 1 in the first iteration"
        return Mark(m.tally, n, m.frames)

    def loop(self, count, body):
        if count == 1:
            body(0)
            return
        start = {t: t.n for t in self.tallies}
        outer, f = self.counting, Frame(count)
        self.counting = True
        self.frames.append(f)
        body(0)
        f.per = {t: t.n - start[t] for t in self.tallies}
        for t in self.tallies:
            t.n = start[t]
        self.counting = outer
        if not outer:
            for eng in self.engines:
                self.settle(eng)
            with self.nc.Fori(0, count) as i:
                f.var = i
                body(i)
                for eng in self.engines:
                    self.settle(eng)
            assert all(t.n - start[t] == f.per[t] for t in self.tallies)
        self.frames.pop()
        f.closed, self.last_loop = True, f
        for t in self.tallies:
            t.n = start[t] + count * f.per[t]


def at(ap, i):
    return ap[:, bass.ds(i, 1), :].rearrange("p a n -> p (a n)")


class Chip:

    def __init__(self, nc, ctx, units_dram, n_units):
        self.nc, self.ctx = nc, ctx
        self.pe, self.act, self.dve, self.pool, self.sp = nc.tensor, nc.scalar, nc.vector, nc.gpsimd, nc.sync
        self.prog = Program(nc)
        self.names = {}
        self.units_dram, self.n_units = units_dram, n_units

        def tally(name, eng):
            return self.prog.tally(ctx.enter_context(nc.semaphore(name)), name, eng)

        self.t_unit = tally("unit_multiplied", self.pe)
        self.t_split = tally("unit_split", self.pool)
        self.t_pe = tally("pe_done", self.pe)
        self.t_act = tally("act_done", self.act)
        self.t_dve = tally("dve_done", self.dve)
        for name, eng in (("pe", self.pe), ("act", self.act), ("dve", self.dve), ("pool", self.pool)):
            self.prog.settled[eng.engine] = ctx.enter_context(nc.semaphore(f"settled_{name}"))
        for t in (self.t_pe, self.t_act, self.t_dve):
            t.eng.sem_inc(t.sem, CREDIT)
            t.n = CREDIT
        self.t_dma = tally("act_dma_done", self.act)
        self.s_loaded = [ctx.enter_context(nc.semaphore(f"unit_loaded_{s}")) for s in range(SLOTS)]
        self.s_hi = ctx.enter_context(nc.semaphore("unit_hi_done"))
        self.w_raw = [self.sb(ctx, f"w_raw{s}", [P, D], F32) for s in range(SLOTS)]
        self.w_hi = [self.sb(ctx, f"w_hi{s}", [P, D], F32R) for s in range(SLOTS)]
        self.w_lo = [self.sb(ctx, f"w_lo{s}", [P, D], F32R) for s in range(SLOTS)]
        self.bank = [ctx.enter_context(nc.psum_tensor(f"bank{b}", [P, T], F32)) for b in range(8)]
        self.x = self.sb(ctx, "x_res", [P, DC, T], F32)
        self.narrow = [self.sb(ctx, f"narrow{j}", [P, 8], F32) for j in range(3)]
        self.ident = self.sb(ctx, "ident", [P, P], F32)
        self.ones = self.sb(ctx, "ones", [P, P], F32)

    def sb(self, ctx, name, shape, dt, side="left"):
        n = self.names[name] = self.names.get(name, 0) + 1
        name = name if n == 1 else f"{name}_{n}"
        return ctx.enter_context(self.nc.sbuf_tensor(name, shape, dt, side=side))

    def A(self, out, in_, func, tag=None, **kw):
        return self.prog.op(self.t_act, self.act.activation, out, in_, func, tag=tag, **kw)

    def V(self, name, *args, tag=None, **kw):
        return self.prog.op(self.t_dve, name, *args, tag=tag, **kw)

    def tt(self, out, a, b, op, tag=None):
        return self.V(self.dve.tensor_tensor, out, a, b, op, tag=tag)

    def stt(self, out, a, s, b, op0, op1, tag=None):
        return self.V(self.dve.scalar_tensor_tensor, out, a, s, b, op0, op1, tag=tag)

    def ts(self, out, a, s1, op0, s2=None, op1=None, tag=None):
        if op1 is None:
            return self.V(self.dve.tensor_scalar, out, a, s1, None, op0, tag=tag)
        return self.V(self.dve.tensor_scalar, out, a, s1, s2, op0, op1, tag=tag)

    def copy(self, out, a, tag=None):
        return self.V(self.dve.tensor_copy, out, a, tag=tag)

    def mm(self, out, lhsT, rhs, start=True, stop=True, done=True, tag=None, **kw):
        if done:
            return self.prog.op(self.t_pe, self.pe.matmul, out, lhsT, rhs, start=start, stop=stop, tag=tag, **kw)
        self.prog.raw(self.pe, self.pe.matmul, out, lhsT, rhs, start=start, stop=stop, **kw)

    def load(self, out, in_):
        if self.t_dma.n:
            self.wait(self.act, self.prog.now(self.t_dma))
        if not self.prog.counting:
            self.prog.issue_waits(self.act)
            self.act.dma_start(out, in_).then_inc(self.t_dma.sem, 16)
        return self.prog.step(self.t_dma, 16)

    def wait(self, eng, *marks):
        self.prog.wait(eng, *marks)

    def fence(self, *engines):
        marks = [m for m in [self.prog.now(t) for t in (self.t_pe, self.t_unit, self.t_act, self.t_dve, self.t_dma)] if m.n > 0]
        for eng in engines or (self.pe, self.act, self.dve):
            self.wait(eng, *marks)

    def weight_stream(self):
        full, rest = divmod(self.n_units, SLOTS)

        def fetch(u, s, first):
            if not first:
                self.sp.wait_ge(self.t_split.sem, u - SLOTS + 1)
            self.sp.dma_start(self.w_raw[s][:, :], self.units_dram[bass.ds(u, 1)].rearrange("a p n -> (a p) n"))\
                .then_inc(self.s_loaded[s], 16)

        def split(u, s, turn, first):
            self.pool.wait_ge(self.s_loaded[s], 16 * turn + 16)
            if not first:
                self.pool.wait_ge(self.t_unit.sem, u - SLOTS + 1)
            self.pool.sem_inc(self.prog.settled[self.pool.engine], 1)
            self.pool.tensor_scalar(self.w_hi[s][:, :], self.w_raw[s][:, :], 1.0, 0.0, ALU.mult, ALU.add)\
                .then_inc(self.s_hi, 1)
            self.pool.wait_ge(self.s_hi, u + 1)
            self.pool.tensor_tensor(self.w_lo[s][:, :], self.w_raw[s][:, :], self.w_hi[s][:, :].bitcast(F32),
                                    ALU.subtract).then_inc(self.t_split.sem, 1)

        for s in range(SLOTS):
            fetch(s, s, True)
        with self.sp.Fori(1, full) as j:
            for s in range(SLOTS):
                fetch(SLOTS * j + s, s, False)
        for s in range(rest):
            fetch(SLOTS * full + s, s, False)
        for s in range(SLOTS):
            split(s, s, 0, True)
        with self.pool.Fori(1, full) as j:
            for s in range(SLOTS):
                split(SLOTS * j + s, s, j, False)
        for s in range(rest):
            split(SLOTS * full + s, s, full, False)

    def unit(self, jobs, tag=None):
        slot = self.t_unit.n % SLOTS
        if not self.prog.counting:
            self.prog.issue_waits(self.pe)
            self.pe.wait_ge(self.t_split.sem, Mark(self.t_unit, self.t_unit.n + 1, list(self.prog.frames)).value())
        hi, lo = self.w_hi[slot], self.w_lo[slot]
        todo = []
        for out, tiles, start, stop in jobs:
            for n, (tile, rh, rl) in enumerate(tiles):
                w = slice(tile * P, tile * P + P)
                for k, (a, b) in enumerate(((hi, rh), (hi, rl), (lo, rh))):
                    todo.append((out, a[:, w], b, start and n == 0 and k == 0, stop and n == len(tiles) - 1 and k == 2))
        for out, a, b, start, stop in todo[:-1]:
            self.prog.raw(self.pe, self.pe.matmul, out, a, b, start=start, stop=stop)
        out, a, b, start, stop = todo[-1]
        return self.prog.op(self.t_unit, self.pe.matmul, out, a, b, start=start, stop=stop, tag=tag)

    def units_together(self, outs, act):
        todo, first = [], self.t_unit.n
        for k in range(DC):
            self.wait(self.pe, act.ready[k])
            w = slice(k * P, k * P + P)
            for u, out in enumerate(outs):
                if k == 0 and not self.prog.counting:
                    self.prog.issue_waits(self.pe)
                    self.pe.wait_ge(self.t_split.sem, Mark(self.t_unit, first + u + 1, list(self.prog.frames)).value())
                hi, lo = self.w_hi[(first + u) % SLOTS], self.w_lo[(first + u) % SLOTS]
                for p, (a, b) in enumerate(((hi, act.hi), (hi, act.lo), (lo, act.hi))):
                    args = (self.pe.matmul, out, a[:, w], b[:, k, :])
                    kw = dict(start=k == 0 and p == 0, stop=k == DC - 1 and p == 2)
                    if kw["stop"]:
                        todo.append(self.prog.op(self.t_unit, *args, **kw))
                    else:
                        self.prog.raw(self.pe, *args, **kw)
            yield
        yield todo

    def project(self, out, hi, lo, k0=0, start=True, stop=True, tag=None):
        return self.unit([(out, [(k, hi[:, k0 + k, :], lo[:, k0 + k, :]) for k in range(DC)], start, stop)], tag=tag)

    def rsqrt(self, r, ss, tmp, scale, ready, factor=None):
        m, a = tmp
        self.wait(self.dve, *ready)
        if factor is None:
            d = self.ts(m, ss, scale, ALU.mult, EPS, ALU.add)
        else:
            d = self.stt(m, ss, scale, factor[1], ALU.mult, ALU.mult)
            self.wait(self.dve, d)
            d = self.ts(m, m, EPS, ALU.add)
        self.wait(self.dve, d)
        d = self.V(self.dve.tensor_scalar, a.bitcast(I32), m.bitcast(I32), 1, None, ALU.logical_shift_right)
        self.wait(self.dve, d)
        d = self.ts(r.bitcast(I32), a.bitcast(I32), -1.0, ALU.mult, float(0x5F3759DF), ALU.add)
        for _ in range(3):
            self.wait(self.dve, d)
            d = self.tt(a, r, r, ALU.mult)
            self.wait(self.dve, d)
            d = self.stt(a, a, -0.5, m, ALU.mult, ALU.mult)
            self.wait(self.dve, d)
            d = self.stt(r, a, 1.5, r, ALU.add, ALU.mult)
        if factor is not None:
            self.wait(self.dve, d)
            d = self.tt(r, r, factor[0], ALU.mult)
        return d

    def token_scale(self, bank, r, n_tiles, ready):
        self.wait(self.pe, *ready)
        for t in range(n_tiles):
            m = self.mm(bank[:, t * P:t * P + P], r[:, t:t + 1].to_broadcast([P, P]), self.ident[:, :],
                        is_transpose=True, done=t == n_tiles - 1)
        return m

    def sum_tokens(self, bank, sq, n_tiles, first, last, ready):
        self.wait(self.pe, *ready)
        for t in range(n_tiles):
            m = self.mm(bank[:, t:t + 1], sq[:, t * P:t * P + P], self.ones[:, 0:1], start=first and t == 0,
                        stop=last, done=t == n_tiles - 1, skip_group_check=True)
        return m


class Normed:

    def __init__(self, c, src, gain, hi, lo, sq, r, n_tiles=TT, banks=(7, 6)):
        self.b_sum, self.b_wide = c.bank[banks[0]], c.bank[banks[1]]
        self.c, self.src, self.gain, self.hi, self.lo, self.sq, self.n_tiles = c, src, gain, hi, lo, sq, n_tiles
        self.rb, self.hi_done, self.ready, self.sq_done, self.summed = r, [], [], [], []
        self.wide = r.wide[:, 0:n_tiles * P]

    def split(self, k, ready):
        c, n = self.c, self.n_tiles * P
        c.wait(c.act, *ready)
        self.hi_done.append(c.A(self.hi[:, k, :], self.src[:, k, :], ACT.Copy, scale=self.gain[:, k:k + 1]))
        if k >= 2:
            c.wait(c.act, self.summed[k - 2])
        self.sq_done.append(c.A(self.sq[k % 2][:, 0:n], self.src[:, k, :], ACT.Square))

    def rest(self, k):
        c = self.c
        c.wait(c.dve, self.hi_done[k])
        self.ready.append(c.stt(self.lo[:, k, :], self.src[:, k, :], self.gain[:, k:k + 1],
                                self.hi[:, k, :].bitcast(F32), ALU.mult, ALU.subtract))

    def sums(self, k):
        self.summed.append(self.c.sum_tokens(self.b_sum, self.sq[k % 2], self.n_tiles, k == 0, k == DC - 1, [self.sq_done[k]]))

    def factors(self):
        c, rb, n = self.c, self.rb, self.n_tiles
        self.found = c.rsqrt(rb.by_token[:, 0:n], self.b_sum[:, 0:n], (rb.tmp[0][:, 0:n], rb.tmp[1][:, 0:n]), 1.0 / D, [self.summed[-1]])

    def spread(self):
        c, rb, n = self.c, self.rb, self.n_tiles
        m = c.token_scale(self.b_wide, rb.by_token, n, [self.found])
        c.wait(c.act, m)
        e = c.A(self.wide, self.b_wide[:, 0:n * P], ACT.Copy)
        if rb.heads:
            for out, heads in ((rb.by_token, 1), (rb.by_head, 2)):
                if heads == 2:
                    c.wait(c.dve, self.found)
                    self.found = c.copy(rb.by_head[:, 0:2 * n].rearrange("p (t h) -> p t h", h=2),
                                        rb.by_token[:, 0:n].unsqueeze(2).to_broadcast([P, n, 2]))
                c.wait(c.dve, self.found)
                w = n * heads
                self.squared = c.tt(rb.by_square[heads][:, 0:w], out[:, 0:w], out[:, 0:w], ALU.mult)
        self.done = e
        return e

    def head_factor(self, heads):
        rb, w = self.rb, self.n_tiles * heads
        return (rb.by_token if heads == 1 else rb.by_head)[:, 0:w], rb.by_square[heads][:, 0:w]

    def start(self, produce, outs):
        c = self.c
        marks = c.units_together(outs[0:2], self)
        for k in range(DC + 1):
            if k < DC:
                self.split(k, produce(k))
            if k >= 1:
                self.rest(k - 1)
                next(marks)
                self.sums(k - 1)
        self.factors()
        out = [*next(marks), c.project(outs[2], self.hi, self.lo)]
        self.spread()
        for eng in (c.act, c.dve, c.pe):
            c.wait(eng, self.done)
        return out


class FactorBuffers:

    def __init__(self, c, ctx, name, n_tiles=TT, heads=False):
        self.heads = heads
        self.by_token = c.sb(ctx, f"{name}_by_token", [P, TT], F32)
        self.wide = c.sb(ctx, f"{name}_wide", [P, n_tiles * P], F32)
        if heads:
            self.by_head = c.sb(ctx, f"{name}_by_head", [P, 2 * TT], F32)[:, :]
            self.by_square = {h: c.sb(ctx, f"{name}_square{h}", [P, h * TT], F32) for h in (1, 2)}
        self.tmp = [c.sb(ctx, f"{name}_tmp{j}", [P, TT], F32) for j in range(2)]


class PostNorm:

    def __init__(self, c, y, gain, acc, t2, done, copied):
        self.copied = copied
        self.c, self.y, self.gain, self.acc, self.t2, self.done, self.out = c, y, gain, acc, t2, done, []

    def begin(self):
        c = self.c
        r, m, a = [b[:, 0:TT] for b in c.narrow]
        ss = c.sum_tokens(c.bank[7], self.acc, TT, True, True, [self.done, self.copied])
        bc = c.token_scale(c.bank[6], r, TT, [c.rsqrt(r, c.bank[7][:, 0:TT], (m, a), 1.0 / D, [ss])])
        c.wait(c.dve, bc)
        self.scaled = [self.scale(0)]

    def scale(self, k):
        c = self.c
        return c.stt(self.t2[k % 2][:, :], self.y[:, k, :], self.gain[:, k:k + 1], c.bank[6][:, :], ALU.mult, ALU.mult)

    def chunk(self, k):
        c = self.c
        if k == 0:
            self.begin()
        if k + 1 < DC:
            if k >= 1:
                c.wait(c.dve, self.out[k - 1])
            self.scaled.append(self.scale(k + 1))
        c.wait(c.dve, self.scaled[k])
        self.out.append(c.tt(c.x[:, k, :], c.x[:, k, :], self.t2[k % 2][:, :], ALU.add))
        return [self.out[k]]


class Recent:

    def __init__(self, prog):
        self.prog, self.marks, self.looped = prog, {}, False

    def keep(self, key, mark):
        self.marks[key] = mark
        if self.looped:
            self.prog.frames[-1].tags[key] = mark
        return mark

    def get(self, key):
        if key in self.marks:
            return self.marks[key]
        if self.looped and (self.prog.counting or key in self.prog.frames[-1].tags):
            return self.prog.prev(key) if not self.prog.counting else None
        return None

    def over(self, total, group, body, peel=False):
        full = total // group

        def turn(i):
            if full > 1:
                self.marks, self.looped = {}, True
            for j in range(group):
                body(i * group + base + j, j)
            self.looped = False

        if peel:
            for j in range(group):
                body(j, j)
            full -= 1
            base = group
        else:
            base = 0
        self.prog.loop(full, turn)
        for j in range(total - full * group - base):
            body(full * group + base + j, j)


def out_projection(c, io, gain, hi, lo, ready, units_per_out=1, together=()):
    rec = Recent(c.prog)
    c.wait(c.dve, c.V(c.dve.memset, io.acc[:, :], 0.0))

    def chunk(n, j, bank, full=None):
        c.wait(c.pe, rec.get(f"square{j}"))
        for q in range(0 if full else units_per_out):
            if isinstance(n, int) and n == 0:
                c.wait(c.pe, *ready[q * DC:(q + 1) * DC])
            full = c.project(bank[:, :], hi, lo, q * DC, q == 0, q == units_per_out - 1)
        sq = io.sq[j % 2]
        c.wait(c.act, full, rec.get(f"sum{j % 2}"))
        s = c.A(sq[:, :], bank[:, :], ACT.Square)
        rec.keep(f"square{j}", c.A(at(io.y, n), bank[:, :], ACT.Copy))
        c.wait(c.dve, s, c.prog.now(c.t_dve))
        rec.keep(f"sum{j % 2}", c.tt(io.acc[:, :], io.acc[:, :], sq[:, :], ALU.add))

    if units_per_out == SLOTS:
        rec.over(DC, 2, lambda n, j: chunk(n, j, c.bank[6 + j]), peel=True)
    else:
        for n in range(DC):
            chunk(n, n % 4, c.bank[n % 4], together[n] if n < len(together) else None)
    return PostNorm(c, io.y, gain, io.acc, io.sq, c.prog.now(c.t_dve), c.prog.now(c.t_act)).chunk


class Chunks:

    def __init__(self, hi, lo, ready):
        self.hi, self.lo, self.ready = hi, lo, ready


class Shared:

    def __init__(self, c, ctx):
        self.rate = c.sb(ctx, "log_a_rate", [P, DC], F32)
        self.hi = c.sb(ctx, "in_hi", [P, DC, T], F32R)
        self.lo = c.sb(ctx, "in_lo", [P, DC, T], F32R)
        self.y = c.sb(ctx, "out_y", [P, DC, T], F32)
        self.acc = c.sb(ctx, "out_squares", [P, T], F32)
        self.sq = [c.sb(ctx, f"square{j}", [P, T], F32) for j in range(2)]
        self.r = FactorBuffers(c, ctx, "factor")


def dilated_attention(c, ctx, normed, produce, oh, ol, bias_dram, beside):
    rec = Recent(c.prog)
    hn_hi, hn_lo = normed.hi, normed.lo
    scale = float(P) ** -0.5
    q = [[c.sb(ctx, f"q{s}{g}", [P, DIL, P], F32) for g in range(GROUPS)] for s in range(2)]
    k = [[c.sb(ctx, f"k{s}{g}", [P, DIL, P], F32) for g in range(GROUPS)] for s in range(2)]
    v = [[c.sb(ctx, f"v{s}{g}", [P, TT, P], F32) for g in range(GROUPS)] for s in range(2)]
    vt = [c.sb(ctx, f"vt{g}", [P, DIL, P], F32) for g in range(GROUPS)]
    bias = [c.sb(ctx, f"bias{s}", [P, DIL * T + 2 * P], F32) for s in range(2)]
    logit = [c.sb(ctx, f"logit{s}", [P, BIAS_W], F32) for s in range(2)]
    pt = [c.sb(ctx, f"pt{s}", [P, BIAS_W], F32) for s in range(2)]
    stat = [c.sb(ctx, f"stat{s}", [P, 4], F32) for s in range(2)]
    b_s0, b_s1, b_t0, b_t1, b_o = c.bank[3], c.bank[4], c.bank[5], c.bank[6], c.bank[7]

    def by_residue(ap):
        return ap.rearrange("p (u r) -> p r u", r=DIL)

    def logits(s, r):
        c.wait(c.pe, rec.get("biased"), *[rec.get(f"qk{s}{g}") for g in range(GROUPS)])
        c.mm(b_s0[:, :], q[s][0][:, r, :], k[s][0][:, :, :].rearrange("p a b -> p (a b)"), done=False)
        c.mm(b_s1[:, 0:P], q[s][1][:, r, :], k[s][1][:, r, :], done=False)
        m = c.mm(b_s1[:, P:2 * P], q[s][2][:, r, :], k[s][2][:, r, :])
        w, st = logit[r % 2], stat[r % 2]
        c.wait(c.dve, m, rec.get(f"bias{s}"), rec.get(f"pt{r % 2}"), rec.get(f"normed{r % 2}"))
        c.tt(w[:, 0:T], b_s0[:, :], bias[s][:, r * T:(r + 1) * T], ALU.add)
        d = rec.keep("biased", c.tt(w[:, T:BIAS_W], b_s1[:, 0:2 * P], bias[s][:, DIL * T:], ALU.add))
        c.wait(c.dve, d)
        d = c.V(c.dve.reduce_max, st[:, 0:1], w[:, :], AX_X)
        c.wait(c.dve, d)
        d = c.ts(st[:, 1:2], st[:, 0:1], -1.0, ALU.mult)
        c.wait(c.act, d)
        e = c.A(w[:, :], w[:, :], ACT.Exp, bias=st[:, 1:2], accum_out=st[:, 2:3])
        c.wait(c.dve, e)
        d = c.V(c.dve.reciprocal, st[:, 3:4], st[:, 2:3])
        c.wait(c.dve, d)
        rec.keep(f"normed{r % 2}", c.ts(w[:, :], w[:, :], st[:, 3:4], ALU.mult))

    def transposes(s, r):
        w = logit[r % 2]
        c.wait(c.pe, rec.get(f"normed{r % 2}"), rec.get("t0_free"), rec.get("t1_free"))
        for j in range(6):
            b = b_t0[:, j * P:j * P + P] if j < 4 else b_t1[:, (j - 4) * P:(j - 3) * P]
            m = c.mm(b, w[:, j * P:j * P + P], c.ident[:, :], is_transpose=True, done=j == 5)
        rec.keep(f"pt{r % 2}", m)
        c.wait(c.act, m, rec.get(f"pv{r % 2}"))
        rec.keep("t0_free", c.A(pt[r % 2][:, 0:T], b_t0[:, :], ACT.Copy))
        c.wait(c.dve, m, rec.get(f"pv{r % 2}"))
        rec.keep("t1_free", c.copy(pt[r % 2][:, T:BIAS_W], b_t1[:, 0:2 * P]))

    def values(s, r):
        c.wait(c.pe, rec.get("t0_free"), rec.get("t1_free"), *[rec.get(f"v{s}{g}") for g in range(GROUPS)])
        if r == 0:
            c.wait(c.pe, rec.get("o_free"))
        keys = [v[s][0][:, j, :] for j in range(TT)] + [v[s][1][:, r, :], v[s][2][:, r, :]]
        for j, vj in enumerate(keys):
            m = c.mm(b_o[:, r * P:r * P + P], vj, pt[r % 2][:, j * P:j * P + P], start=j == 0, stop=j == 5, done=j == 5)
        return rec.keep(f"pv{r % 2}", m)

    def finish(h, m):
        o_nat = b_o[:, :].rearrange("p (r u) -> p u r", r=DIL)
        c.wait(c.act, m)
        e = c.A(at(oh, h).rearrange("p (u r) -> p u r", r=DIL), o_nat, ACT.Copy)
        c.wait(c.dve, e)
        rec.keep("o_free", c.tt(at(ol, h).rearrange("p (u r) -> p u r", r=DIL), o_nat,
                                at(oh, h).bitcast(F32).rearrange("p (u r) -> p u r", r=DIL), ALU.subtract))

    def v_rows(s, g):
        c.wait(c.pe, rec.get(f"vt{g}"), rec.get("t0_free"))
        for j in range(TT):
            m = c.mm(b_t0[:, j * P:j * P + P], vt[g][:, j, :], c.ident[:, :], is_transpose=True, done=j == TT - 1)
        rec.keep(f"vt_read{g}", m)
        c.wait(c.act, m)
        rec.keep("t0_free", rec.keep(f"v{s}{g}", c.A(v[s][g][:, :, :].rearrange("p a b -> p (a b)"), b_t0[:, :], ACT.Copy)))

    kinds = [("v", 0), ("v", 1), ("v", 2), ("q", 0), ("k", 0), ("q", 1), ("k", 1), ("q", 2), ("k", 2)]

    def head(h, s, attend):
        c.wait(c.act, rec.get("biased"))
        rec.keep(f"bias{s}", c.load(bias[s][:, :], bias_dram[bass.ds(h, 1)].rearrange("a p n -> (a p) n")))
        for j, (kind, g) in enumerate(kinds):
            b = c.bank[j % 3]
            c.wait(c.pe, rec.get(f"bank{j % 3}"))
            if attend is None and j < 3:
                if j == 0:
                    together = normed.start(produce, [c.bank[i][:, :] for i in range(3)])
                m = together[j]
            else:
                m = c.project(b[:, :], hn_hi, hn_lo)
            def ordered(ap):
                return ap.rearrange("p (a b) -> p a b", a=TT) if g == 0 and kind != "q" else by_residue(ap)
            src, r = ordered(b[:, :]), ordered(normed.wide)
            c.wait(c.dve, m, rec.get(f"vt_read{g}") if kind == "v" else None)
            if kind == "v":
                e = rec.keep(f"vt{g}", c.tt(vt[g][:, :, :], src, r, ALU.mult))
            elif kind == "q":
                e = rec.keep(f"q{s}{g}", c.stt(q[s][g][:, :, :], src, scale, r, ALU.mult, ALU.mult))
            else:
                e = rec.keep(f"qk{s}{g}", c.tt(k[s][g][:, :, :], src, r, ALU.mult))
            rec.keep(f"bank{j % 3}", e)
            if isinstance(h, int) and h == HEADS - 1:
                for _ in range(3):
                    next(beside, None)
            if attend is not None:
                r = j // 2
                if j % 2 == 0:
                    if r >= 1:
                        m = values(attend[1], r - 1)
                    if r < DIL:
                        logits(attend[1], r)
                else:
                    transposes(attend[1], r)
            if 1 <= j <= 3:
                v_rows(s, j - 1)
        if attend is not None:
            finish(attend[0], m)

    head(0, 0, None)
    c.fence()

    def two_heads(i):
        rec.marks = {}
        rec.looped = True
        head(i * 2 + 1, 1, (i * 2, 0))
        head(i * 2 + 2, 0, (i * 2 + 1, 1))
        rec.looped = False

    c.prog.loop(HEADS // 2 - 1, two_heads)
    head(HEADS - 1, 1, (HEADS - 2, 0))
    out = Chunks(oh, ol, [c.prog.now(c.t_dve)] * (DC - 1))
    marks = c.units_together([c.bank[j][:, :] for j in range(3)], out)
    logits(1, 0)
    for r in range(DIL):
        next(marks)
        transposes(1, r)
        if r < DIL - 1:
            logits(1, r + 1)
            next(marks)
        m = values(1, r)
    finish(HEADS - 1, m)
    out.ready.append(c.prog.now(c.t_dve))
    next(marks)
    return next(marks)


def conv_ffn(c, io, taps, gain_pre, gain_post, produce):
    with ExitStack() as ctx:
        hid_hi = c.sb(ctx, "ffn_hidden_hi", [P, FC, T], F32R)
        hid_lo = c.sb(ctx, "ffn_hidden_lo", [P, FC, T], F32R)
        tap = c.sb(ctx, "ffn_tap", [P, 24], F32)
        cg = [c.sb(ctx, f"ffn_g{j}", [P, T], F32) for j in range(2)]
        cv = [c.sb(ctx, f"ffn_v{j}", [P, T], F32) for j in range(2)]
        raw = [c.sb(ctx, f"ffn_raw{j}", [P, T], F32) for j in range(2)]
        c.fence()
        normed = Normed(c, c.x, gain_pre, io.hi, io.lo, cg, io.r)
        together = normed.start(produce, [c.bank[i][:, :] for i in range(3)])
        rec = Recent(c.prog)

        def pair(n, j):
            if j == 0:
                c.wait(c.dve, rec.get("taps_used_act"), c.prog.now(c.t_dve))
                rec.keep("taps", c.copy(tap[:, :], taps[:, bass.ds(n * 8, 24)]))
            s = j % 2
            halves = []
            for half, buf in ((0, cg[s]), (1, cv[s])):
                b, w = c.bank[2 * j + half], tap[:, 8 * j + 4 * half:8 * j + 4 * half + 4]
                if isinstance(n, int) and 2 * n + half < 3:
                    m = together[2 * n + half]
                else:
                    c.wait(c.pe, rec.get(f"bank{j}{half}"))
                    m = c.project(b[:, :], io.hi, io.lo)
                z = raw[half]
                c.wait(c.dve, m, rec.get(f"newest{half}"), rec.get(f"oldest{half}"))
                d = rec.keep(f"bank{j}{half}", c.tt(z[:, :], b[:, :], normed.wide, ALU.mult))
                c.wait(c.act, d, rec.get("taps"), rec.get(f"hid{s}"), rec.get(f"gated{s}"))
                e = rec.keep(f"newest{half}", c.A(buf[:, :], z[:, :], ACT.Identity, scale=w[:, 2:3], bias=w[:, 3:4]))
                rec.keep("taps_used_act", e)
                c.wait(c.dve, e)
                d = c.stt(buf[:, 1:T], z[:, 0:T - 1], w[:, 1:2], buf[:, 1:T], ALU.mult, ALU.add)
                c.wait(c.dve, d)
                d = rec.keep(f"oldest{half}", c.stt(buf[:, 2:T], z[:, 0:T - 2], w[:, 0:1], buf[:, 2:T], ALU.mult, ALU.add))
                halves.append(d)
            c.wait(c.act, halves[0])
            e = c.A(cg[s][:, :], cg[s][:, :], ACT.Gelu_apprx_tanh)
            c.wait(c.dve, e, halves[1])
            d = c.tt(cv[s][:, :], cg[s][:, :], cv[s][:, :], ALU.mult)
            c.wait(c.act, d)
            e = rec.keep(f"gated{s}", c.A(at(hid_hi, n), cv[s][:, :], ACT.Copy))
            c.wait(c.dve, e)
            rec.keep(f"hid{s}", c.tt(at(hid_lo, n), cv[s][:, :], at(hid_hi, n).bitcast(F32), ALU.subtract))

        rec.over(FC, 3, pair, peel=True)
        last = c.prog.now(c.t_dve)
        done = Mark(last.tally, last.n - 2 * c.prog.last_loop.per[c.t_dve], last.frames)
        return out_projection(c, io, gain_post, hid_hi, hid_lo, [done] * 2 * DC + [last] * DC, FC // DC)


def in_steps(first, ops, c):
    m = first
    for op in ops:
        c.wait(c.dve, m)
        m = op()
        yield
    return m


def to_the_end(steps):
    while True:
        try:
            next(steps)
        except StopIteration as end:
            return end.value


def log_sigmoid(c, out, v, w, ready):
    e, z2, p = w
    c.wait(c.act, *ready)
    m = c.A(e, v, ACT.Abs)
    c.wait(c.act, m)
    m = c.A(e, e, ACT.Exp, scale=-1.0)
    c.wait(c.dve, *ready)
    ops = [lambda: c.ts(p, e, 2.0, ALU.add), lambda: c.V(c.dve.reciprocal, p, p), lambda: c.tt(e, e, p, ALU.mult),
           lambda: c.tt(z2, e, e, ALU.mult), lambda: c.ts(p, z2, 1.0 / 17, ALU.mult, 1.0 / 15, ALU.add)]
    for d in (13, 11, 9, 7, 5, 3, 1):
        ops += [lambda: c.tt(p, p, z2, ALU.mult), lambda d=d: c.ts(p, p, 1.0 / d, ALU.add)]
    ops += [lambda: c.stt(p, p, -2.0, e, ALU.mult, ALU.mult), lambda: c.stt(out, v, 0.0, p, ALU.min, ALU.add)]
    return (yield from in_steps(m, ops, c))


def decay_rate(c, rate, lru, work, cols_in):
    lam, *w = work
    c.wait(c.dve, *cols_in)
    d = c.copy(lam[:, :], lru.rearrange("p (n k) -> p k n", k=8)[:, 7, 0:DC])
    d = yield from log_sigmoid(c, rate[:, :], lam[:, :], [a[:, :] for a in w], [d])
    c.wait(c.dve, d)
    c.ts(rate[:, :], rate[:, :], 8.0, ALU.mult)


def rglru(c, io, lru, gain_pre, gain_post, produce):
    with ExitStack() as ctx:
        xb = c.sb(ctx, "xb", [P, DC, T], F32)
        sh = c.sb(ctx, "split_hi", [P, DC, T], F32R)
        sl = c.sb(ctx, "split_lo", [P, DC, T], F32R)
        ga = c.sb(ctx, "gate_a", [P, DC, T], F32)
        gx = c.sb(ctx, "gate_x", [P, DC, T], F32)
        th = c.sb(ctx, "tanh_sqrt_h", [P, DC, T], F32)
        tmp = [c.sb(ctx, f"lru_t{j}", [P, T], F32) for j in range(2)]
        raw = [c.sb(ctx, f"lru_raw{j}", [P, T], F32) for j in range(2)]
        c.fence()
        hi, lo, r, cl = io.hi, io.lo, io.r.wide, io.rate
        cols = lru.rearrange("p (n k) -> p k n", k=8)
        normed = Normed(c, c.x, gain_pre, hi, lo, tmp, io.r)
        together = normed.start(produce, [c.bank[j][:, :] for j in range(3)])
        emptied, split, convolved = [], [], None

        def parts(n):
            c.wait(c.act, convolved)
            e = c.A(sh[:, n, :], xb[:, n, :], ACT.Copy)
            c.wait(c.dve, e)
            split.append(c.tt(sl[:, n, :], xb[:, n, :], sh[:, n, :].bitcast(F32), ALU.subtract))

        for n in range(DC):
            b, z, w = c.bank[n % 3], raw[n % 2], lru[:, 8 * n:8 * n + 8]
            if n < 3:
                m = together[n]
            else:
                c.wait(c.pe, emptied[n - 3])
                m = c.project(b[:, :], hi, lo)
            c.wait(c.dve, m)
            emptied.append(c.tt(z[:, :], b[:, :], r[:, :], ALU.mult))
            c.wait(c.act, emptied[n])
            e = c.A(xb[:, n, :], z[:, :], ACT.Identity, scale=w[:, 3:4], bias=w[:, 4:5])
            if n >= 1:
                parts(n - 1)
            for lag in (1, 2, 3):
                c.wait(c.dve, e)
                e = c.stt(xb[:, n, lag:T], z[:, 0:T - lag], w[:, 3 - lag:4 - lag], xb[:, n, lag:T], ALU.mult, ALU.add)
            convolved = e
        parts(DC - 1)
        gated = {}
        for b in range(4):
            banks = [c.bank[4 * ((b + 1) % 2) + q] for q in range(4)]
            c.wait(c.pe, split[2 * b + 1])
            if b == 1:
                c.wait(c.pe, *emptied[-3:])
            if b >= 2:
                c.wait(c.pe, gated[b - 2])
            m = c.unit([(banks[q][:, :], [(2 * q + k, sh[:, 2 * b + k, :], sl[:, 2 * b + k, :]) for k in range(2)], True, True)
                        for q in range(4)])
            c.wait(c.act, m)
            for n in range(2):
                ch = 2 * b + n
                c.A(ga[:, ch, :], banks[n][:, :], ACT.Sigmoid, bias=cols[:, 5, ch:ch + 1])
                e = c.A(gx[:, ch, :], banks[2 + n][:, :], ACT.Sigmoid, bias=cols[:, 6, ch:ch + 1])
                c.wait(c.dve, e)
                gated_x = c.tt(gx[:, ch, :], gx[:, ch, :], xb[:, ch, :], ALU.mult)
            gated[b] = e
        c.wait(c.pe, e)
        gb = [c.project(c.bank[n][:, :], hi, lo) for n in range(DC)]
        roots = []
        for ch in range(DC):
            e = c.A(th[:, ch, :], ga[:, ch, :], ACT.Tanh, scale=cl[:, ch:ch + 1])
            c.wait(c.act, e)
            e = c.A(ga[:, ch, :], ga[:, ch, :], ACT.Exp, scale=cl[:, ch:ch + 1])
            c.wait(c.dve, e)
            if ch >= 2:
                c.wait(c.dve, roots[ch - 2])
            d = c.tt(tmp[ch % 2][:, :], ga[:, ch, :], ga[:, ch, :], ALU.mult)
            c.wait(c.dve, d)
            d = c.stt(th[:, ch, :], tmp[ch % 2][:, :], 1.0, th[:, ch, :], ALU.add, ALU.mult)
            c.wait(c.dve, d)
            roots.append(c.ts(th[:, ch, :], th[:, ch, :], -1.0, ALU.mult, 0.0, ALU.max))
        hs, scaled = [], []

        def scale_gb(ch):
            c.wait(c.dve, gb[ch], gated_x)
            scaled.append(c.tt(xb[:, ch, :], c.bank[ch][:, :], r[:, :], ALU.mult))

        for ch in range(DC):
            c.wait(c.act, roots[ch])
            e = c.A(th[:, ch, :], th[:, ch, :], ACT.Sqrt)
            if ch < DC // 2:
                scale_gb(ch)
            c.wait(c.dve, e)
            d = c.tt(gx[:, ch, :], gx[:, ch, :], th[:, ch, :], ALU.mult)
            c.wait(c.dve, d)
            hs.append(c.V(c.dve.tensor_tensor_scan, th[:, ch, :], ga[:, ch, :], gx[:, ch, :], 0.0, ALU.mult, ALU.add))
        for ch in range(DC // 2, DC):
            scale_gb(ch)
        gelus = []
        for ch in range(DC):
            c.wait(c.act, scaled[ch])
            gelus.append(c.A(xb[:, ch, :], xb[:, ch, :], ACT.Gelu_apprx_tanh))
        c.wait(c.act, gb[0])
        c.wait(c.dve, gb[0])
        ready = []
        for ch in range(DC):
            c.wait(c.dve, gelus[ch], hs[ch])
            d = c.tt(xb[:, ch, :], xb[:, ch, :], th[:, ch, :], ALU.mult)
            c.wait(c.act, d)
            e = c.A(sh[:, ch, :], xb[:, ch, :], ACT.Copy)
            c.wait(c.dve, e)
            ready.append(c.tt(sl[:, ch, :], xb[:, ch, :], sh[:, ch, :].bitcast(F32), ALU.subtract))
        marks = c.units_together([c.bank[0][:, :], c.bank[1][:, :]], Chunks(sh, sl, ready))
        *_, together = marks
        return out_projection(c, io, gain_post, sh, sl, ready, together=together)


N_COLS = 8 * 8
UNITS_1 = 72 + 8 + 72 + 20 + 8 + 72


def block_one(c, ctx, gains, lru, taps, cols_in, bias_dram, produce):
    def gain(kind, layer):
        k = (kind * 2 + layer) * DC
        return gains[:, k:k + DC]

    io = Shared(c, ctx)
    with ExitStack() as att:
        oh = c.sb(att, "attn_o_hi", [P, DC, T], F32R)
        ol = c.sb(att, "attn_o_lo", [P, DC, T], F32R)
        with ExitStack() as inner:
            normed = Normed(c, c.x, gain(0, 0), io.hi, io.lo, io.sq, io.r)
            work = [c.sb(inner, f"decay_work{j}", [P, DC], F32) for j in range(4)]
            together = dilated_attention(c, inner, normed, produce, oh, ol, bias_dram, decay_rate(c, io.rate, lru, work, cols_in))
        produce = out_projection(c, io, gain(1, 0), oh, ol, [], together=together)
    produce = conv_ffn(c, io, taps[:, 0:8 * FC], gain(2, 0), gain(3, 0), produce)
    produce = rglru(c, io, lru, gain(0, 1), gain(1, 1), produce)
    return conv_ffn(c, io, taps[:, 8 * FC:16 * FC], gain(2, 1), gain(3, 1), produce)


def build(nc, t, out):
    with ExitStack() as ctx:
        c = Chip(nc, ctx, t["units"], UNITS_1 + UNITS_2)
        gains = c.sb(ctx, "gains", [P, N_COLS], F32)
        lru = c.sb(ctx, "lru_cols", [P, 72], F32)
        taps = c.sb(ctx, "taps", [P, 16 * FC], F32)

        def early(name, out, in_):
            loaded = c.prog.tally(ctx.enter_context(nc.semaphore(f"{name}_loaded")), name, c.act)
            c.act.dma_start(out, in_).then_inc(loaded.sem, 16)
            return c.prog.step(loaded, 16)

        gains_in = early("gains", gains[:, :], t["gains"])
        x_in = [early(f"x{k}", c.x[:, 2 * k:2 * k + 2, :].rearrange("p a b -> p (a b)"), t["x"][:, 2 * k * T:(2 * k + 2) * T])
                for k in range(DC // 2)]
        ident_in = early("ident", c.ident[:, :], t["ident"])
        cols_in = [early("lru_cols", lru[:, :], t["lru"]), early("taps", taps[:, :], t["taps"])]
        d = c.V(c.dve.memset, c.ones[:, :], 1.0)
        c.wait(c.pe, d, ident_in)
        c.wait(c.dve, gains_in)
        c.wait(c.act, gains_in)
        c.weight_stream()
        with ExitStack() as one:
            produce = block_one(c, one, gains, lru, taps, cols_in, t["bias"], lambda k: [x_in[k // 2]])
            consts = Constants(c, ctx, t)
            x_ready = [m for k in range(DC) for m in produce(k)]
        c.wait(c.act, block_two(c, t, x_ready, consts))
        c.wait(c.act, c.prog.now(c.t_dma))
        m = c.load(out, c.x[:, :, :].rearrange("p a b -> p (a b)"))
        c.wait(c.act, m)
        c.prog.issue_waits(c.act)


HD = 64
M = 256
MT = M // P
CMP_L, CMP_S = 32, 16
NC = T // CMP_S - 1
LAYER_COLS = 2 * DC + 9 + 2 * CMP_L + P + HD
C_NORM, C_MEMNORM, C_GAINS, C_PE, C_W2 = 0, DC, 2 * DC, 2 * DC + 9, 2 * DC + 9 + 2 * CMP_L
G_NSA_Q, G_CMP_K, G_SEL_K, G_WIN_K, G_FOX_Q, G_FOX_K, G_MEM_Q, G_MEM_K, G_FOX_BIAS = range(9)
K_COS, K_SIN, K_ROT, K_MASK, K_CMASK, K_HALF, K_SEL, K_PART = 0, T, 2 * T, 2 * T + P, 2 * T + 2 * P, 2 * T + 3 * P, 2 * T + 3 * P + 2, 2 * T + 3 * P + 10
CONST_COLS = K_PART + 3
F_ROW = 64
UNITS_LAYER = 8 + 27 + 12 + 36 + 8 + 2
UNITS_2 = 2 * UNITS_LAYER


class Later:

    def __init__(self):
        self.todo = []

    def add(self, delay, fn):
        self.todo.append([delay, fn])

    def tick(self):
        for item in self.todo:
            item[0] -= 1
        due = [item for item in self.todo if item[0] <= 0]
        self.todo = [item for item in self.todo if item[0] > 0]
        for _, fn in due:
            fn()

    def flush(self):
        while self.todo:
            self.tick()


class Epilogues:

    def __init__(self, c, ctx, k, pl):
        self.c, self.k, self.pl, self.rec, self.later = c, k, pl, Recent(c.prog), Later()
        self.sq = [c.sb(ctx, f"ep_sq{j}", [P, T], F32) for j in range(2)]
        self.vt = [c.sb(ctx, f"ep_vt{j}", [P, T], F32) for j in range(2)]
        self.rc = [c.sb(ctx, f"ep_rope{j}", [P, T], F32) for j in range(2)]
        self.nar = [[c.sb(ctx, f"ep_nar{s}{j}", [P, 2 * TT], F32) for j in range(3)] for s in range(2)]
        self.wide = [c.sb(ctx, f"ep_wide{j}", [P, T], F32) for j in range(2)]
        self.n_norm = self.n_vt = 0

    def norm(self, raw, dst, z, n, heads, gain, width, ready, rope):
        c, rec, s = self.c, self.rec, self.n_norm % 2
        self.n_norm += 1
        tiles, sq = n // P, self.sq[s]
        nar = [a[:, 0:tiles * heads] for a in self.nar[s]]
        c.wait(c.act, *ready)
        copied = c.A(dst, raw, ACT.Copy)
        c.wait(c.act, rec.get(f"sq{s}"))
        squared = c.A(sq[:, 0:n], raw, ACT.Square)
        state = {}

        def sums():
            c.wait(c.pe, squared, rec.get("ss_free"))
            ss = c.bank[7]
            rhs = self.k[:, K_HALF:K_HALF + 2] if heads == 2 else c.ones[:, 0:1]
            for t in range(tiles):
                m = c.mm(ss[:, t * heads:(t + 1) * heads], sq[:, t * P:t * P + P], rhs, start=t == 0, stop=True,
                         done=t == tiles - 1, skip_group_check=True)
            rec.keep(f"sq{s}", m)
            c.wait(c.dve, rec.get(f"nar{s}"))
            state["r"] = c.rsqrt(nar[0], ss[:, 0:tiles * heads], (nar[1], nar[2]), 1.0 / width, [m, z.squared],
                                  z.head_factor(heads))
            rec.keep("ss_free", state["r"])
            if heads == 2:
                c.wait(c.dve, rec.get(f"wide{s}"))
                state["r"] = self.widen(nar[0], P, tiles, self.wide[s])

        def spread():
            b = c.bank[6]
            c.wait(c.pe, state["r"], rec.get("r_free"))
            for t in range(tiles):
                r = self.wide[s][:, t * P:t * P + P] if heads == 2 else nar[0][:, t:t + 1].to_broadcast([P, P])
                m = c.mm(b[:, t * P:t * P + P], r, c.ident[:, :], is_transpose=True, done=t == tiles - 1)
            rec.keep(f"nar{s}", m)
            if heads == 2:
                rec.keep(f"wide{s}", m)
            c.wait(c.dve, m, copied)
            state["f"] = rec.keep("r_free", c.stt(dst, dst, gain, b[:, 0:n], ALU.mult, ALU.mult))

        self.later.add(1, sums)
        self.later.add(3, spread)
        if rope:
            self.later.add(4, lambda: self.rope(dst, state["f"]))
        return squared

    def widen(self, r, tokens, tiles, wide):
        c = self.c
        c.wait(c.dve, c.prog.now(c.t_dve))
        out = wide[0:tokens, 0:tiles * P].rearrange("p (h d) -> p h d", d=HD)
        return c.copy(out, r.unsqueeze(2).to_broadcast([tokens, 2 * tiles, HD]))

    def rope(self, dst, ready):
        c, rec = self.c, self.rec
        b = c.bank[5]
        c.wait(c.pe, ready, rec.get("rot_free"))
        m = c.mm(b[:, :], self.k[:, K_ROT:K_ROT + P], dst)
        c.wait(c.dve, m, ready, rec.get("roped"))
        c.tt(self.rc[0][:, :], dst, self.k[:, K_COS:K_COS + T], ALU.mult)
        m = rec.keep("rot_free", c.tt(self.rc[1][:, :], b[:, :], self.k[:, K_SIN:K_SIN + T], ALU.mult))
        c.wait(c.dve, m)
        return rec.keep("roped", c.tt(dst, self.rc[0][:, :], self.rc[1][:, :], ALU.add))

    def rows(self, raw, dst, z, n, ready):
        c, rec, s = self.c, self.rec, self.n_vt % 2
        self.n_vt += 1
        vt, tiles = self.vt[s], n // P
        c.wait(c.dve, *ready, rec.get(f"vt{s}"))
        copied = c.tt(vt[:, 0:n], raw, z.wide, ALU.mult)

        def turn():
            b = c.bank[4]
            c.wait(c.pe, copied, rec.get("rows_free"))
            for t in range(tiles):
                m = c.mm(b[:, t * P:t * P + P], vt[:, t * P:t * P + P], c.ident[:, :], is_transpose=True, done=t == tiles - 1)
            rec.keep(f"vt{s}", m)
            c.wait(c.act, m)
            rec.keep("rows_free", c.A(dst, b[:, 0:n].rearrange("p (t n) -> p t n", n=P), ACT.Copy))

        self.later.add(1, turn)
        return copied


def forget_rows(c, raw_f, base, rhs, k, w, parts, ready):
    lo, hi = slice(F_ROW, P), slice(F_ROW + 32, P)
    top = slice(F_ROW, F_ROW + 32)
    rest, acc = w[1], w[2]
    m = yield from log_sigmoid(c, raw_f[lo, :], raw_f[lo, :], [a[lo, :] for a in w], ready)
    ops = [lambda: c.V(c.dve.memset, w[0][lo, :], 1.0),
           lambda: c.V(c.dve.tensor_tensor_scan, rest[lo, :], w[0][lo, :], raw_f[lo, :], 0.0, ALU.mult, ALU.add),
           lambda: c.ts(rest[lo, :], rest[lo, :], 8.0, ALU.mult)]
    for j in range(3):
        ops.append(lambda j=j: c.copy(parts[j][lo, :], rest[lo, :]))
        if j < 2:
            ops.append(lambda j=j: c.tt(rest[lo, :], rest[lo, :], parts[j][lo, :], ALU.subtract))
    ops.append(lambda: c.ts(acc[lo, :], parts[0][lo, :], k[lo, K_PART:K_PART + 1], ALU.mult))
    for j in (1, 2):
        ops.append(lambda j=j: c.stt(acc[lo, :], parts[j][lo, :], k[lo, K_PART + j:K_PART + j + 1], acc[lo, :], ALU.mult, ALU.add))
    ops += [lambda: c.ts(rhs[top, :], acc[top, :], -1.0, ALU.mult), lambda: c.copy(base[hi, :], acc[hi, :])]
    return (yield from in_steps(m, ops, c))


def compress(c, src, pe, w1, xw, hid, rec, ready, loaded):
    c.wait(c.dve, *ready, rec.get("xw_free"))
    for g in range(2):
        rows = slice(g * HD, (g + 1) * HD)
        for half in range(2):
            x = src[rows, half * CMP_S:half * CMP_S + NC * CMP_S].rearrange("p (n l) -> p l n", l=CMP_S)
            e = pe[rows, half * CMP_S:(half + 1) * CMP_S].unsqueeze(2).to_broadcast([HD, CMP_S, NC])
            m = c.tt(xw[rows, half * CMP_S:(half + 1) * CMP_S, g * NC:(g + 1) * NC], x, e, ALU.add)
    yield
    b = c.bank[3]
    c.wait(c.pe, m, loaded, rec.get("cmp_bank"))
    for l in range(CMP_L):
        m = c.mm(b[:, 0:2 * NC], w1[:, l * P:l * P + P], xw[:, l, :], start=l == 0, stop=l == CMP_L - 1, done=l == CMP_L - 1)
    rec.keep("xw_free", m)
    c.wait(c.act, m, rec.get("hid_free"))
    rec.keep("cmp_bank", rec.keep("hidden", c.A(hid[:, :], b[:, 0:2 * NC], ACT.Silu)))
    yield


class Attention:
    S, ST, PT = 3, 6, 3

    def __init__(self, c, ctx):
        self.c, self.rec = c, Recent(c.prog)
        self.p = [c.sb(ctx, f"at_p{j}", [P, T], F32) for j in range(self.S)]
        self.pt = [c.sb(ctx, f"at_pt{j}", [P, T], F32) for j in range(self.PT)]
        self.st = [c.sb(ctx, f"at_st{j}", [P, 6], F32) for j in range(self.ST)]
        self.tasks = []

    def task(self, add_logits, n, scale, values, width, finish, ready, gate=None, may_be_empty=False):
        self.tasks.append((n, values, width, finish, gate, may_be_empty))
        self.step(len(self.tasks) - 1, add_logits, scale, ready)

    def step(self, now, add_logits=None, scale=None, ready=()):
        def has(task):
            return 0 <= task < len(self.tasks)
        if has(now - 5):
            self.store(now - 5)
        if has(now):
            maximum = self.logits(now, add_logits, ready)
        if has(now - 1):
            m = self.divisor(now - 1)
        if has(now - 2):
            self.transposed(now - 2)
        if has(now):
            self.exponentials(now, scale, maximum)
        if has(now - 1):
            self.factor(now - 1, m)
        if has(now - 4):
            self.output(now - 4)

    def drain(self):
        n = len(self.tasks)
        for now in range(n, n + 5):
            self.step(now)
        assert n % self.ST == 0
        self.tasks = []

    def logits(self, task, add_logits, ready):
        c, rec, s, t, n = self.c, self.rec, task % self.S, task % self.ST, self.tasks[task][0]
        b = c.bank[s]
        c.wait(c.pe, rec.get(f"exp{s}"), *ready)
        m = add_logits(b)
        c.wait(c.dve, m, rec.get(f"stored{t}"))
        return c.V(c.dve.reduce_max, self.st[t][:, 0:1], b[:, 0:n], AX_X)

    def exponentials(self, task, scale, maximum):
        c, rec, s, t, n = self.c, self.rec, task % self.S, task % self.ST, self.tasks[task][0]
        st = self.st[t]
        c.wait(c.dve, maximum)
        m = c.ts(st[:, 1:2], st[:, 0:1], -1.0e29, ALU.max, -scale, ALU.mult)
        c.wait(c.act, m, rec.get(f"p{s}"))
        e = c.A(self.p[s][:, 0:n], c.bank[s][:, 0:n], ACT.Exp, scale=scale, bias=st[:, 1:2], accum_out=st[:, 2:3])
        rec.keep(f"exp{s}", rec.keep(f"sum{t}", e))

    def divisor(self, task):
        c, t = self.c, task % self.ST
        st = self.st[t]
        c.wait(c.dve, self.rec.get(f"sum{t}"))
        if self.tasks[task][5]:
            return c.ts(st[:, 3:4], st[:, 2:3], 0.5, ALU.max)
        return c.V(c.dve.reciprocal, st[:, 4:5], st[:, 2:3])

    def factor(self, task, m):
        c, t, gate = self.c, task % self.ST, self.tasks[task][4]
        st = self.st[t]
        if self.tasks[task][5]:
            c.wait(c.dve, m)
            m = c.V(c.dve.reciprocal, st[:, 4:5], st[:, 3:4])
        if gate is not None:
            c.wait(c.dve, m)
            m = c.ts(st[:, 5:6], st[:, 4:5], gate, ALU.mult)
        self.rec.keep(f"factor{t}", m)

    def transposed(self, task):
        c, rec, s, u, v, n = self.c, self.rec, task % self.S, task % 2, task % self.PT, self.tasks[task][0]
        b, rows, tiles = c.bank[3 + u], min(n, P), (n + P - 1) // P
        c.wait(c.pe, rec.get(f"exp{s}"), rec.get(f"turned{u}"))
        for j in range(tiles):
            m = c.mm(b[0:rows, j * P:j * P + P], self.p[s][:, j * P:j * P + rows], c.ident[:, :], is_transpose=True, done=j == tiles - 1)
        rec.keep(f"p{s}", m)
        c.wait(c.act, m, rec.get(f"pv{v}"))
        e = c.A(self.pt[v][0:rows, 0:tiles * P], b[0:rows, 0:tiles * P], ACT.Copy)
        rec.keep(f"turned{u}", rec.keep(f"pt{v}", e))

    def output(self, task):
        c, rec, u, v, n = self.c, self.rec, task % 2, task % self.PT, self.tasks[task][0]
        values, width = self.tasks[task][1:3]
        o, rows, last = c.bank[5 + u][:, 0:width], min(n, P), len(values) - 1
        c.wait(c.pe, rec.get(f"pt{v}"), rec.get(f"o{u}"))
        for j, keys in enumerate(values):
            m = c.mm(o, self.pt[v][0:rows, j * P:j * P + P], keys, start=j == 0, stop=j == last, done=j == last)
        rec.keep(f"out{u}", rec.keep(f"pv{v}", m))

    def store(self, task):
        c, rec, u, t = self.c, self.rec, task % 2, task % self.ST
        width, finish, gate = self.tasks[task][2:5]
        c.wait(c.dve, rec.get(f"out{u}"), rec.get(f"factor{t}"))
        factor = self.st[t][:, 4:5] if gate is None else self.st[t][:, 5:6]
        rec.keep(f"o{u}", rec.keep(f"stored{t}", finish(c.bank[5 + u][:, 0:width], factor)))


class Constants:

    def __init__(self, c, ctx, t):
        self.k = c.sb(ctx, "consts", [P, CONST_COLS], F32, side="right")
        self.cols = c.sb(ctx, "both_layers_cols", [P, 2, LAYER_COLS], F32, side="right")
        self.identb = c.sb(ctx, "ident_bf", [P, P], BF16, side="right")
        self.maskb = c.sb(ctx, "mask_bf", [P, 2 * P], BF16, side="right")
        c.fence(c.act)
        self.loaded = [c.load(self.k[:, :], t["consts"])] + [c.load(self.cols[:, layer, :], t["layer_cols"][layer]) for layer in range(2)]


def block_two(c, t, x_ready, consts):
    c.wait(c.dve, *consts.loaded)
    c.copy(consts.identb[:, :], c.ident[:, :])
    c.copy(consts.maskb[:, :], consts.k[:, K_MASK:K_MASK + 2 * P])
    c.wait(c.act, *x_ready)
    c.prog.loop(2, lambda layer: layer_two(c, t, layer, consts.k, consts.cols, consts.identb, consts.maskb))
    return c.prog.now(c.t_dve)


def layer_two(c, t, layer, k, cols, identb, maskb):
    with ExitStack() as ctx:
        pl = c.sb(ctx, "layer_cols", [P, LAYER_COLS], F32)
        hi = c.sb(ctx, "z_hi", [P, DC, T], F32R)
        lo = c.sb(ctx, "z_lo", [P, DC, T], F32R)
        factors = FactorBuffers(c, ctx, "z_factor", heads=True)
        o_all = c.sb(ctx, "o_all", [P, 12, T], F32)
        c.fence()
        chosen = c.copy(pl[:, :], at(cols, layer))
        for eng in (c.act, c.dve):
            c.wait(eng, chosen)
        with ExitStack() as att:
            b = {n: c.sb(att, n, [P, w, T], F32) for n, w in (("nsa_q", 4), ("mem_q", 4))}
            b["sel_k"], b["win_k"] = (c.sb(att, n, [P, T], F32) for n in ("sel_k", "win_k"))
            b["sel_v"], b["win_v"] = (c.sb(att, n, [P, TT, P], F32) for n in ("sel_v", "win_v"))
            b["mem_k"] = c.sb(att, "mem_k", [P, 4, M], F32)
            b["mem_v"] = c.sb(att, "mem_v", [P, MT, T], F32)
            b["cmp_k"] = c.sb(att, "cmp_k", [P, NC], F32)
            b["cmp_v"] = c.sb(att, "cmp_v", [NC, P], F32)
            b["gate"] = c.sb(att, "gate_rows", [P, TT, 32], F32)
            b["fox_base"] = c.sb(att, "fox_base", [P, T], BF16)
            b["fox_rhs"] = c.sb(att, "fox_rhs", [P, T], BF16)
            projections(c, att, t, layer, k, pl, b, hi, lo, factors, o_all)
            attend_all(c, k, identb, maskb, b, o_all)
        oh = c.sb(ctx, "oz_hi", [P, 12, T], F32R)
        ol = c.sb(ctx, "oz_lo", [P, 12, T], F32R)
        banks_free = silu_gates(c, hi, lo, factors.wide, o_all, oh, ol)
        merge_and_out(c, banks_free, hi, lo, factors.wide, oh, ol, [o_all[:, j, :] for j in range(6)])
        c.fence()


def at_row(ap, n):
    return ap[bass.ds(n, 1)].rearrange("a p n -> (a p) n")


def memory_input(c, t, pl, mem, mh, ml, factors, sq, rec):
    loaded = c.load(mem[:, :, :].rearrange("p a b -> p (a b)"), t["mem"])
    yield
    z = Normed(c, mem, pl[:, C_MEMNORM:C_MEMNORM + DC], mh, ml, sq, factors, MT, banks=(4, 4))
    c.wait(c.dve, loaded)
    for n in range(DC):
        z.split(n, [loaded])
        if n >= 1:
            z.rest(n - 1)
            z.sums(n - 1)
        yield
    z.rest(DC - 1)
    z.sums(DC - 1)
    yield
    z.factors()
    yield
    rec.keep("rows_free", z.spread())
    return z


def projections(c, att, t, layer, k, pl, b, hi, lo, factors, spare):
    def gain(g):
        return pl[:, C_GAINS + g:C_GAINS + g + 1]

    with ExitStack() as ctx:
        ep = Epilogues(c, ctx, k, pl)
        rec = ep.rec
        kc = [c.sb(ctx, n, [P, T], F32) for n in ("cmp_src_k", "cmp_src_v")]
        gs = c.sb(ctx, "gate_cols", [P, T], F32)
        fr = c.sb(ctx, "forget", [P, T], F32)
        fw = [c.sb(ctx, f"forget_work{j}", [P, T], F32) for j in range(3)]
        mem_sq = [c.sb(ctx, f"mem_square{j}", [P, M], F32) for j in range(2)]
        mem_factors = FactorBuffers(c, ctx, "mem_factor", MT, heads=True)
        spare = spare[:, :, :].rearrange("p a b -> p (a b)")
        w1 = spare[:, 0:CMP_L * P]
        xw = spare[:, CMP_L * P:CMP_L * (P + 2 * NC)].rearrange("p (l n) -> p l n", l=CMP_L)
        hid = c.sb(ctx, "cmp_hidden", [P, 2 * NC], F32)
        parts = [c.sb(ctx, f"fox_part{j}", [P, T], BF16) for j in range(3)]
        mem_ctx = ExitStack()
        mem = c.sb(mem_ctx, "mem_in", [P, DC, M], F32, side="right")
        mh, ml = (c.sb(mem_ctx, n, [P, DC, M], F32R, side="right") for n in ("mem_hi", "mem_lo"))
        c.fence()
        w1_ready = c.load(w1, at_row(t["cmp_w1"], layer * 2))
        blank = [(gs[:, :], 0.0), (xw[:, :, :], 0.0), (b["cmp_k"][:, :], 0.0), (b["fox_base"][:, :], 0.0), (b["fox_rhs"][:, :], 0.0),
                 (b["fox_base"][F_ROW:F_ROW + 32, :], 1.0), (b["fox_rhs"][F_ROW + 32:P, :], 1.0)]

        def x_chunk(n):
            if n < len(blank):
                c.wait(c.dve, c.prog.now(c.t_dve))
                c.V(c.dve.memset, *blank[n])
            return []

        z = Normed(c, c.x, pl[:, C_NORM:C_NORM + DC], hi, lo, ep.sq, factors)
        together = z.start(x_chunk, [c.bank[j][:, :] for j in range(3)])
        state, beside = {}, []

        def tick():
            ep.later.tick()
            for steps, per_unit in beside:
                for _ in range(per_unit):
                    next(steps, None)

        def unit(n, epilogue):
            bank = c.bank[n % 3]
            c.wait(c.pe, rec.get(f"bank{n % 3}"))
            m = together[n] if n < 3 else c.project(bank[:, :], hi, lo)
            tick()
            rec.keep(f"bank{n % 3}", epilogue(bank, m))

        def normed(dst, g, rope, heads=2):
            return lambda bank, m: ep.norm(bank[:, :], dst, z, T, heads, gain(g), P // heads, [m], rope)

        def rows(dst):
            return lambda bank, m: ep.rows(bank[:, :], dst, z, T, [m])

        def cmp_key(bank, m):
            c.wait(c.dve, m)
            d = c.tt(kc[0][:, :], bank[:, :], z.wide, ALU.mult)

            def roped():
                state["kc"] = ep.rope(kc[0][:, :], d)
            ep.later.add(1, roped)
            return d

        def cmp_value(bank, m):
            c.wait(c.dve, m)
            state["vc"] = c.tt(kc[1][:, :], bank[:, :], z.wide, ALU.mult)
            return state["vc"]

        def gates(bank, m):
            c.wait(c.dve, m)
            c.tt(gs[0:32, :], bank[0:32, :], z.wide[0:32, :], ALU.mult)
            d = c.tt(fr[F_ROW:P, :], bank[F_ROW:P, :], z.wide[F_ROW:P, :], ALU.mult)
            c.wait(c.act, d)
            e = c.A(gs[0:32, :], gs[0:32, :], ACT.Sigmoid)
            f = c.A(fr[F_ROW:P, :], fr[F_ROW:P, :], ACT.Identity, bias=pl[F_ROW:P, C_GAINS + G_FOX_BIAS:C_GAINS + G_FOX_BIAS + 1])
            state["f"] = f

            def turn():
                rb = c.bank[3]
                c.wait(c.pe, e)
                for tt in range(TT):
                    m = c.mm(rb[:, tt * P:tt * P + P], gs[:, tt * P:tt * P + P], c.ident[:, :], is_transpose=True, done=tt == TT - 1)
                c.wait(c.dve, m)
                rec.keep("cmp_bank", c.copy(b["gate"][:, :, :], rb[:, :].rearrange("p (t n) -> p t n", n=P)[:, :, 0:32]))
            ep.later.add(1, turn)
            return d

        cmp_sq = c.sb(ctx, "cmp_squares", [P, NC], F32)
        cmp_nar = [c.sb(ctx, f"cmp_nar{j}", [NC, 2], F32) for j in range(3)]
        cmp_wide = c.sb(ctx, "cmp_wide", [NC, P], F32)
        cb, w2 = c.bank[3], pl[:, C_W2:C_W2 + P + HD]

        def compressed():
            yield from compress(c, kc[0], pl[:, C_PE:C_PE + CMP_L], w1, xw, hid, rec, [state["kc"]], w1_ready)
            c.wait(c.act, rec.get("xw_free"))
            w1_again = c.load(w1, at_row(t["cmp_w1"], layer * 2 + 1))
            c.wait(c.pe, rec.get("hidden"))
            m = rec.keep("hid_free", c.mm(cb[:, 0:2 * NC], w2[:, 0:P], hid[:, :]))
            c.wait(c.act, m)
            for g in range(2):
                rws = slice(g * HD, (g + 1) * HD)
                c.A(b["cmp_k"][rws, :], cb[rws, g * NC:(g + 1) * NC], ACT.Copy)
                e = rec.keep("cmp_bank", c.A(cmp_sq[rws, :], cb[rws, g * NC:(g + 1) * NC], ACT.Square))
            yield
            c.wait(c.pe, e, rec.get("ss_free"))
            m = c.mm(c.bank[7][0:NC, 0:2], cmp_sq[:, :], k[:, K_HALF:K_HALF + 2])
            nar = [a[:, :] for a in cmp_nar]
            rec.keep("ss_free", c.rsqrt(nar[0], c.bank[7][0:NC, 0:2], (nar[1], nar[2]), 1.0 / HD, [m]))
            r = ep.widen(nar[0], NC, 1, cmp_wide)
            yield
            c.wait(c.pe, r, rec.get("r_free"))
            c.prog.settle(c.pe)
            m = c.mm(c.bank[6][:, 0:NC], cmp_wide[:, :], c.ident[0:NC, 0:NC], is_transpose=True)
            c.wait(c.dve, m, e)
            rec.keep("r_free", c.stt(b["cmp_k"][:, :], b["cmp_k"][:, :], gain(G_CMP_K), c.bank[6][:, 0:NC], ALU.mult, ALU.mult))
            yield from compress(c, kc[1], pl[:, C_PE + CMP_L:C_PE + 2 * CMP_L], w1, xw, hid, rec, [state["vc"]], w1_again)
            c.wait(c.pe, rec.get("hidden"))
            for g in range(2):
                m = c.mm(cb[0:NC, g * HD:(g + 1) * HD], hid[:, g * NC:(g + 1) * NC], w2[:, P:P + HD], done=g == 1)
            c.wait(c.act, m)
            e = rec.keep("cmp_bank", c.A(b["cmp_v"][:, :], cb[0:NC, 0:P], ACT.Copy))
            c.wait(c.pe, e)

        def memory():
            state["mem"] = yield from memory_input(c, t, pl, mem, mh, ml, mem_factors, mem_sq, rec)

        unit(0, cmp_key)
        unit(1, cmp_value)
        unit(2, gates)
        beside += [(compressed(), 1), (memory(), 2)]
        for n in range(4):
            unit(3 + n, normed(b["nsa_q"][:, n, :], G_NSA_Q, True))
        unit(7, normed(b["sel_k"][:, :], G_SEL_K, True))
        unit(8, normed(b["win_k"][:, :], G_WIN_K, True))
        beside.append((forget_rows(c, fr, b["fox_base"], b["fox_rhs"], k, fw, parts, [state["f"]]), 2))
        unit(9, rows(b["sel_v"][:, :, :]))
        unit(10, rows(b["win_v"][:, :, :]))
        zm = state["mem"]
        c.wait(c.pe, *zm.ready, zm.done)
        c.wait(c.dve, zm.done)

        def memory_unit(n, slot):
            bank = c.bank[slot % 3]
            c.wait(c.pe, rec.get(f"bank{slot % 3}"))
            m = c.project(bank[:, 0:M], zm.hi, zm.lo)
            tick()
            if n < 4:
                f = ep.norm(bank[:, 0:M], b["mem_k"][:, n, :], zm, M, 1, gain(G_MEM_K), P, [m], False)
            else:
                f = ep.rows(bank[:, 0:M], b["mem_v"][:, :, (n - 4) * P:(n - 3) * P], zm, M, [m])
            rec.keep(f"bank{slot % 3}", f)
            return m

        for n in range(4):
            memory_unit(2 * n, 11 + 3 * n)
            m = memory_unit(2 * n + 1, 12 + 3 * n)
            unit(13 + 3 * n, normed(b["mem_q"][:, n, :], G_MEM_Q, False, 1))
        mem_ctx.close()
        for n in ("fox_q", "fox_k", "fox_v"):
            b[n] = c.sb(att, n, [P, 4, T], F32, side="right")
        for eng in (c.act, c.dve):
            c.wait(eng, m, *zm.ready, zm.done)
        for n in range(4):
            unit(23 + 2 * n, normed(b["fox_q"][:, n, :], G_FOX_Q, False))
            unit(24 + 2 * n, normed(b["fox_k"][:, n, :], G_FOX_K, False))
        for n in range(4):
            unit(31 + n, rows(b["fox_v"][:, :, n * P:(n + 1) * P]))
        ep.later.flush()
        for steps, _ in beside:
            to_the_end(steps)
        c.fence()


def attend_all(c, k, identb, maskb, b, o_all):
    with ExitStack() as ctx:
        at_ = Attention(c, ctx)
        rec = at_.rec
        nq = [c.sb(ctx, f"nsa_q_half{j}", [P, T], F32) for j in range(2)]
        fq = [c.sb(ctx, f"fox_q_half{j}", [P, T], F32) for j in range(2)]
        mq = c.sb(ctx, "mem_q_now", [P, T], F32)
        fb = [c.sb(ctx, f"fox_base_head{j}", [P, T], BF16) for j in range(2)]
        sel = c.sb(ctx, "sel_now", [P, 2], F32)
        gt = c.sb(ctx, "gate_now", [P, TT, 2, 3], F32)
        rows = [c.sb(ctx, f"o_rows{j}", [P, TT, P], F32) for j in range(3)]
        c.fence()
        for j in range(2):
            h = slice((1 - j) * HD, (2 - j) * HD)
            c.V(c.dve.memset, nq[j][h, :], 0.0)
            c.V(c.dve.memset, fq[j][h, :], 0.0)

        def chunk(n):
            rec.marks = {}
            rec.looped = True
            c.wait(c.dve, rec.get("staged_used"), rec.get("rows_out"), c.prog.now(c.t_dve))
            c.wait(c.act, rec.get("staged_used"), rec.get("rows_out"))
            for j in range(2):
                h = slice(j * HD, (j + 1) * HD)
                nq_staged = c.copy(nq[j][h, :], b["nsa_q"][h, bass.ds(n, 1), :].rearrange("p a n -> p (a n)"))
                c.A(fq[j][h, :], b["fox_q"][h, bass.ds(n, 1), :].rearrange("p a n -> p (a n)"), ACT.Copy)
            d = c.copy(sel[:, :], k[:, bass.ds(K_SEL + 2 * n, 2)])
            for j in range(2):
                c.copy(gt[:, :, j, :], b["gate"][:, :, bass.ds(3 * n + 12 * j, 3)])
            a = c.A(mq[:, :], at(b["mem_q"], n), ACT.Copy)
            c.wait(c.dve, d)
            for j in range(2):
                d = c.ts(fb[j][:, :], b["fox_base"][:, :], sel[:, j:j + 1], ALU.mult)
            staged = [a, d]
            todo = [[] for _ in range(TT)]
            for i in range(TT):
                def task(*args, i=i, **kw):
                    todo[i].append((args, kw))

                q, keys, last = slice(i * P, i * P + P), (i + 1) * P, slice(i * P, (i + 1) * P)
                for j in range(2):
                    out = rows[0][:, i, j * HD:(j + 1) * HD]

                    def first(o, factor, out=out):
                        return rec.keep("nsa_row", c.ts(out, o, factor, ALU.mult))

                    def further(o, factor, out=out):
                        c.wait(c.dve, rec.get("nsa_row"))
                        return rec.keep("nsa_row", c.stt(out, o, factor, out, ALU.mult, ALU.add))

                    def cmp_logits(bank, i=i, j=j, q=q):
                        c.mm(bank[:, 0:NC], nq[j][:, q], b["cmp_k"][:, :], stop=False, done=False)
                        return c.mm(bank[:, 0:NC], identb[:, :], maskb[:, P + 32 * i:P + 32 * i + NC], start=False)

                    task(cmp_logits, NC, HD ** -0.5, [b["cmp_v"][:, j * HD:(j + 1) * HD]], HD, first, [nq_staged],
                             gate=gt[:, i, j, 0:1], may_be_empty=True)
                    for which, (kk, vv) in enumerate((("sel_k", "sel_v"), ("win_k", "win_v")), 1):
                        def logits(bank, j=j, q=q, keys=keys, last=last, kk=kk):
                            c.mm(bank[:, 0:keys], nq[j][:, q], b[kk][:, 0:keys], stop=False, done=False)
                            return c.mm(bank[:, last], identb[:, :], maskb[:, 0:P], start=False)
                        task(logits, keys, HD ** -0.5, [b[vv][:, s, j * HD:(j + 1) * HD] for s in range(i + 1)], HD, further, [],
                                 gate=gt[:, i, j, which:which + 1])
                for j in range(2):
                    def fox_logits(bank, j=j, q=q, keys=keys, last=last):
                        c.mm(bank[:, 0:keys], fq[j][:, q], b["fox_k"][:, bass.ds(n, 1), 0:keys].rearrange("p a n -> p (a n)"), stop=False, done=False)
                        c.mm(bank[:, 0:keys], fb[j][:, q], b["fox_rhs"][:, 0:keys], start=False, stop=False, done=False)
                        return c.mm(bank[:, last], identb[:, :], maskb[:, 0:P], start=False)

                    def fox_out(o, factor, out=rows[1][:, i, j * HD:(j + 1) * HD]):
                        return c.ts(out, o, factor, ALU.mult)
                    task(fox_logits, keys, HD ** -0.5, [b["fox_v"][:, s, bass.ds(n * P + j * HD, HD)] for s in range(i + 1)], HD, fox_out, staged)

                def mem_logits(bank, q=q):
                    return c.mm(bank[:, 0:M], mq[:, q], b["mem_k"][:, bass.ds(n, 1), :].rearrange("p a n -> p (a n)"))

                def mem_out(o, factor, out=rows[2][:, i, :]):
                    return c.ts(out, o, factor, ALU.mult)
                task(mem_logits, M, P ** -0.5, [b["mem_v"][:, s, bass.ds(n * P, P)] for s in range(MT)], P, mem_out, staged)
            for pair in ((0, 3), (1, 2)):
                for tasks in zip(*[todo[i] for i in pair]):
                    for args, kw in tasks:
                        at_.task(*args, **kw)
            at_.drain()
            rec.keep("staged_used", c.prog.now(c.t_pe))
            for j in range(3):
                bank = c.bank[(7, 3)[j % 2]]
                c.wait(c.pe, c.prog.now(c.t_dve), rec.get(f"back{j % 2}"))
                for i in range(TT):
                    m = c.mm(bank[:, i * P:i * P + P], rows[j][:, i, :], c.ident[:, :], is_transpose=True, done=i == TT - 1)
                c.wait(c.act, m)
                rec.keep(f"back{j % 2}", c.A(at(o_all, n + 4 * j), bank[:, :], ACT.Copy))
            rec.keep("rows_out", m)
            rec.looped = False

        c.prog.loop(4, chunk)


def silu_gates(c, hi, lo, r, o_all, oh, ol):
    with ExitStack() as ctx:
        s = [c.sb(ctx, f"silu{j}", [P, T], F32) for j in range(3)]
        c.fence(c.act, c.dve)
        rec = Recent(c.prog)

        def chunk(n, j):
            c.wait(c.pe, rec.get(f"silu{j}"))
            m = c.project(c.bank[j][:, :], hi, lo)
            c.wait(c.dve, m, rec.get(f"lo{j}"))
            d = rec.keep(f"silu{j}", c.tt(s[j][:, :], c.bank[j][:, :], r[:, :], ALU.mult))
            c.wait(c.act, d)
            e = c.A(s[j][:, :], s[j][:, :], ACT.Silu)
            c.wait(c.dve, e)
            d = c.tt(s[j][:, :], s[j][:, :], at(o_all, n), ALU.mult)
            c.wait(c.act, d)
            e = c.A(at(oh, n), s[j][:, :], ACT.Copy)
            c.wait(c.dve, e)
            rec.keep(f"lo{j}", c.tt(at(ol, n), s[j][:, :], at(oh, n).bitcast(F32), ALU.subtract))

        rec.over(12, 3, chunk)
        return [rec.get(f"silu{j}") for j in range(3)]


def merge_and_out(c, banks_free, hi, lo, r, oh, ol, g):
    with ExitStack() as ctx:
        uh = c.sb(ctx, "u_hi", [P, DC, T], F32R)
        ul = c.sb(ctx, "u_lo", [P, DC, T], F32R)
        gated = c.prog.now(c.t_dve)
        c.fence(c.act, c.dve)
        c.wait(c.pe, *banks_free)
        rec = Recent(c.prog)

        def two(i):
            rec.marks = {}
            rec.looped = True
            for j in range(6):
                c.wait(c.pe, rec.get(f"bank{j}"))
                m = c.project(c.bank[j][:, :], hi, lo)
                c.wait(c.dve, m, rec.get(f"g{j}"))
                d = rec.keep(f"bank{j}", c.tt(g[j], c.bank[j][:, :], r[:, :], ALU.mult))
                c.wait(c.act, d)
                rec.keep(f"sig{j}", c.A(g[j], g[j], ACT.Sigmoid))
            for br in range(3):
                banks = [c.bank[(6 + 2 * br + e) % 8] for e in range(2)]
                names = [f"bank{(6 + 2 * br + e) % 8}" for e in range(2)]
                c.wait(c.pe, gated, *[rec.get(n) for n in names])
                m = c.unit([(banks[e][:, :], [(4 * e + q, oh[:, 4 * br + q, :], ol[:, 4 * br + q, :]) for q in range(4)], True, True)
                            for e in range(2)])
                for e in range(2):
                    j = 3 * e + br
                    c.wait(c.dve, m, rec.get(f"sig{j}"))
                    d = rec.keep(names[e], c.tt(g[j], g[j], banks[e][:, :], ALU.mult))
                    if br:
                        c.wait(c.dve, d, rec.get(f"sum{e}"))
                        d = c.tt(g[3 * e], g[3 * e], g[j], ALU.add)
                        rec.keep(f"g{j}", d)
                    rec.keep(f"sum{e}", d)
            for e in range(2):
                c.wait(c.act, rec.get(f"sum{e}"))
                a = c.A(at(uh, 2 * i + e), g[3 * e], ACT.Copy)
                c.wait(c.dve, a)
                rec.keep(f"g{3 * e}", c.tt(at(ul, 2 * i + e), g[3 * e], at(uh, 2 * i + e).bitcast(F32), ALU.subtract))
            rec.looped = False

        c.prog.loop(4, two)
        last = c.prog.now(c.t_dve)
        early = Mark(last.tally, last.n - c.prog.last_loop.per[c.t_dve], last.frames)
        c.wait(c.pe, rec.get("bank4"), rec.get("bank5"))
        marks = c.units_together([c.bank[j][:, :] for j in (4, 5)], Chunks(uh, ul, [early] * (DC - 2) + [last] * 2))
        *_, together = marks
        added = []
        for n in range(DC):
            bank = c.bank[(4, 5, 6, 7)[n % 4]]
            if n in (2, 3):
                c.wait(c.pe, last)
            elif n >= 4:
                c.wait(c.pe, added[n - 4])
            m = together[n] if n < 2 else c.project(bank[:, :], uh, ul)
            c.wait(c.dve, m)
            added.append(c.tt(c.x[:, n, :], c.x[:, n, :], bank[:, :], ALU.add))
        for j in range(2):
            m = c.unit([(c.bank[j][:, 0:HD], [(0, uh[:, 0, 0:HD], ul[:, 0, 0:HD])], True, True)])


def _bucket(dist):
    half = 16
    d = np.maximum(dist, 1).astype(np.float64)
    large = half + (np.log(d / half) / np.log(2048 / half) * half).astype(np.int32)
    return np.where(dist < half, dist, np.minimum(large, 31)).astype(np.int32)


def _bias_rows(rel_bias):
    u = np.arange(P)
    out = np.empty((HEADS, P, DIL * T + 2 * P), np.float32)

    def put(lo, m, valid, dil, g):
        rows = rel_bias[_bucket(np.clip(m, 0, P) * dil)]
        for h in range(HEADS):
            out[h, :, lo:lo + m.shape[1]] = np.where(valid, rows[:, :, g * HEADS + h], np.float32(NEG))

    for r in range(DIL):
        m = (DIL * u + r)[:, None] - np.arange(T)[None, :]
        put(r * T, m, (m >= 0) & (m <= P), 1, 0)
    m = u[:, None] - u[None, :]
    put(DIL * T, m, m >= 0, 4, 1)
    put(DIL * T + P, m // 4, (m >= 0) & (m % 4 == 0), 16, 2)
    return out


def _cols(v):
    return np.ascontiguousarray(v.reshape(-1, P).T)


def _units(w):
    k, n = w.shape
    w = w.reshape(k // D, DC, P, n // P, P)
    return w.transpose(3, 0, 2, 1, 4).reshape(n // P * (k // D), P, D)


def _feature_major(x):
    return np.ascontiguousarray(x.T.reshape(DC, P, x.shape[0]).transpose(1, 0, 2).reshape(P, -1))


def _layout_one(i):
    f = {k: np.asarray(v) for k, v in i.items()}
    qkv = _units(f["attn_w_qkv"][0]).reshape(GROUPS, 3, HEADS, P, D)
    order = [(2, 0), (2, 1), (2, 2), (0, 0), (1, 0), (0, 1), (1, 1), (0, 2), (1, 2)]
    parts = [qkv[g, kind, h][None] for h in range(HEADS) for kind, g in order]
    parts.append(_units(f["attn_w_o"][0]))

    def ffn(layer):
        up = _units(f["ffn_w_up"][layer])
        return [up.reshape(2, FC, P, D).transpose(1, 0, 2, 3).reshape(2 * FC, P, D), _units(f["ffn_w_down"][layer])]

    parts += ffn(0)
    w_in = _units(f["lru_w_in"][0])
    gates = np.stack([f["lru_ga_w"][0], f["lru_gx_w"][0]])
    gates = gates.reshape(2, 4, 2, P, 2, P).transpose(1, 3, 0, 4, 2, 5).reshape(4, P, D)
    parts += [w_in[:DC], gates, w_in[DC:], _units(f["lru_w_out"][0])]
    parts += ffn(1)
    norms = [f[k][layer] for k in ("norm_mix_pre", "norm_mix_post", "norm_ffn_pre", "norm_ffn_post") for layer in range(2)]
    lru = np.stack([_cols(v) for v in (*f["lru_conv_w"][0], f["lru_conv_b"][0], f["lru_ga_b"][0].reshape(-1),
                                       f["lru_gx_b"][0].reshape(-1), f["lru_lambda"][0])], axis=2).reshape(P, 64)
    taps = []
    for layer in range(2):
        four = np.stack([_cols(v) for v in (*f["ffn_conv_w"][layer], f["ffn_conv_b"][layer])], axis=2)
        taps.append(four.reshape(P, 2, FC, 4).transpose(0, 2, 1, 3).reshape(P, 8 * FC))
    return parts, {
        "x": _feature_major(f["x"][0]),
        "gains": np.concatenate([_cols(v) for v in norms], axis=1),
        "lru": np.concatenate([lru, np.zeros((P, 8), np.float32)], axis=1),
        "taps": np.concatenate(taps, axis=1),
        "bias": _bias_rows(f["rel_bias"]),
        "ident": np.eye(P, dtype=np.float32),
    }


def _layout_two(i):
    f = {k[:-2]: np.asarray(v) for k, v in i.items() if k.endswith("_2")}
    pair = np.concatenate([np.r_[n * HD:(n + 1) * HD, (n + 4) * HD:(n + 5) * HD] for n in range(4)])
    zero = np.zeros((D, 8), np.float32)
    parts, cols, w1 = [], [], []
    for layer in range(2):
        w = f["w_in"][layer]
        kv = _units(w[:, 512:1280])
        fr = np.concatenate([w[:, 3352:3360]] * 3 + [zero], axis=1)
        gate = np.concatenate([w[:, 1280:1304], zero, np.zeros((D, 32), np.float32), fr, fr], axis=1)
        fox = _units(w[:, 1816:3352]).reshape(3, 4, P, D)
        fox = np.concatenate([fox[0:2].transpose(1, 0, 2, 3).reshape(8, P, D), fox[2]])
        mem = np.concatenate([_units(f["w_mem_kv"][layer]).reshape(4, 2, P, D), _units(w[:, 3872:4384])[:, None]], axis=1)
        mem = mem.reshape(12, P, D)
        merge = _units(w[:, 4896:7968]).reshape(3, DC, P, D)
        br = np.stack([f["w_branch_a"][layer][pair], f["w_branch_b"][layer], f["w_branch_m"][layer]])
        br = br.reshape(3, 4, P, 4, 2, P).transpose(3, 0, 2, 4, 1, 5).reshape(4, 3, P, D)
        both = [np.concatenate([merge[:, 2 * n], merge[:, 2 * n + 1], br[n]]) for n in range(4)]
        parts += [kv[0:2], _units(gate), _units(w[:, 0:512][:, pair]), kv[2:3], kv[4:5], kv[3:4],
                  kv[5:6], mem, fox,
                  _units(w[:, 1304:1816][:, pair]), _units(w[:, 3360:3872]),
                  _units(w[:, 4384:4896]), *both, _units(f["w_out"][layer]), np.zeros((2, P, D), np.float32)]
        two = lambda v: np.concatenate([v, v], axis=0)
        fb = np.zeros(P, np.float32)
        for r in (64, 72, 80, 96, 104, 112):
            fb[r:r + 8] = f["fox_f_bias"][layer]
        one = [two(f["nsa_q_norm"][layer]), *[two(f["nsa_k_norm"][layer][j]) for j in range(3)], two(f["fox_q_norm"][layer]),
               two(f["fox_k_norm"][layer]), f["mem_q_norm"][layer], f["mem_k_norm"][layer], fb]
        cols.append(np.concatenate([
            _cols(f["norm_g"][layer]), _cols(f["mem_norm_g"][layer]), np.stack(one, axis=1),
            two(f["cmp_pe_k"][layer].T), two(f["cmp_pe_v"][layer].T),
            f["cmp_w2_k"][layer], f["cmp_w2_k"][layer], f["cmp_w2_v"][layer]], axis=1))
        for name in ("cmp_w1_k", "cmp_w1_v"):
            w1.append(two(f[name][layer].reshape(CMP_L, HD, P).transpose(1, 0, 2).reshape(HD, CMP_L * P)))
    half = HD // 2
    freq = (np.float32(10000.0) ** (-np.arange(half, dtype=np.float32) / half)).astype(np.float32)
    ang = (np.arange(T, dtype=np.float32)[None, :] * freq[:, None]).astype(np.float32)
    ang = np.concatenate([ang] * 4, axis=0)
    rot = np.zeros((P, P), np.float32)
    for m in range(P):
        if m % HD < half:
            rot[m + half, m] = -1.0
        else:
            rot[m - half, m] = 1.0
    a, b = np.arange(P)[:, None], np.arange(P)[None, :]
    mask = np.where(b > a, np.float32(NEG), np.float32(0))
    cmask = np.zeros((P, 4, 32), np.float32)
    for tile in range(4):
        end = np.arange(32) * CMP_S + CMP_L - 1
        cmask[:, tile] = np.where(end[None, :] <= tile * P + a, np.float32(0), np.float32(NEG))
    p = np.arange(P)
    halves = np.stack([p < HD, p >= HD], axis=1)
    inside = (p >= F_ROW) & (p % 32 < 24)
    sel = np.stack([inside & (p % 8 == h) for h in range(8)], axis=1)
    part = np.stack([inside & (p % 32 // 8 == j) for j in range(3)], axis=1)
    consts = np.concatenate([np.cos(ang), np.sin(ang), rot, mask, cmask.reshape(P, P), halves, sel, part], axis=1)
    return parts, {
        "mem": _feature_major(f["mem"][0]), "layer_cols": np.stack(cols), "cmp_w1": np.stack(w1),
        "consts": consts.astype(np.float32),
    }


def _layout(inputs):
    one, a = _layout_one(inputs)
    two, b = _layout_two(inputs)
    return {**a, **b, "units": np.concatenate(one + two)}


def kernel(**inputs):
    import concourse.bacc as bacc
    from concourse.bass_utils import run_bass_kernel_spmd

    arrays = _layout(inputs)
    nc = bacc.Bacc("TRN2", target_bir_lowering=False, num_devices=1, dynamic_dma_scratch_size=1024)
    t = {n: nc.dram_tensor("in_" + n, a.shape, mybir.dt.from_np(a.dtype), kind="ExternalInput").ap() for n, a in arrays.items()}
    out = nc.dram_tensor("out", (P, DC * T), F32, kind="ExternalOutput").ap()
    build(nc, t, out)
    r = run_bass_kernel_spmd(nc, [{"in_" + n: a for n, a in arrays.items()}], core_ids=[0])
    y = r.results[0]["out"].reshape(P, DC, T)
    return np.ascontiguousarray(y.transpose(2, 1, 0).reshape(1, T, D))
```
